# Optimizing a Trainium2 kernel written in Bass

```python
import jax, jax.numpy as jnp
from jax import lax
import numpy as np

D_MODEL = 1024
BATCH = 1
SEQ = 512
DEPTH = 1

CHUNK = 64
NORM_EPS = 1e-6

N_HEADS_A = 4
HEAD_DIM_A = 128
KEY_DIM_A = N_HEADS_A * HEAD_DIM_A
VAL_DIM_A = N_HEADS_A * HEAD_DIM_A
CONV_WIDTH = 4
CONV_DIM = 2 * KEY_DIM_A + VAL_DIM_A

N_Q_HEADS_B = 8
N_KV_HEADS_B = 2
GQA_GROUP = N_Q_HEADS_B // N_KV_HEADS_B
HEAD_DIM_B = 64
Q_DIM_B = N_Q_HEADS_B * HEAD_DIM_B
KV_DIM_B = N_KV_HEADS_B * HEAD_DIM_B
WINDOW = 128
WINDOW_CHUNKS = WINDOW // CHUNK

IN_PROJ_WIDTHS = (CONV_DIM, VAL_DIM_A, N_HEADS_A, N_HEADS_A, Q_DIM_B, KV_DIM_B, KV_DIM_B, D_MODEL, D_MODEL)
IN_PROJ_DIM = sum(IN_PROJ_WIDTHS)

N_EXPERT_GROUPS = 4
EXPERTS_PER_GROUP = 4
N_EXPERTS = N_EXPERT_GROUPS * EXPERTS_PER_GROUP
TOP_K_IN_GROUP = 2
D_FF_EXPERT = 256

kernel_name = "hybrid_deltanet_swa_hmoe_block"

def rms_norm(x, w):
    xf = x.astype(jnp.float32)
    y = xf * lax.rsqrt(jnp.mean(xf * xf, axis=-1, keepdims=True) + NORM_EPS)
    return (y * w.astype(jnp.float32)).astype(x.dtype)

def l2_normalize(x):
    xf = x.astype(jnp.float32)
    return (xf * lax.rsqrt(jnp.sum(xf * xf, axis=-1, keepdims=True) + NORM_EPS)).astype(x.dtype)

def causal_depthwise_conv(x, w):
    return lax.conv_general_dilated(
        x, w[:, None, :].astype(x.dtype), window_strides=(1,),
        padding=[(w.shape[0] - 1, 0)], dimension_numbers=('NWC', 'WIO', 'NWC'),
        feature_group_count=x.shape[-1])

def alibi_slopes(n_heads):
    return jnp.exp2(-8.0 * (jnp.arange(n_heads, dtype=jnp.float32) + 1.0) / n_heads)

def gated_delta_rule(q, k, v, g, beta):
    out_dtype = v.dtype
    f32 = jnp.float32
    b, s, h, dk = q.shape
    dv = v.shape[-1]
    nc = s // CHUNK

    def chunks(t):
        return t.astype(f32).reshape(b, nc, CHUNK, h, -1).transpose(0, 1, 3, 2, 4)

    q = chunks(q) * dk ** -0.5
    k = chunks(k)
    v = chunks(v)
    g = chunks(g[..., None])[..., 0]
    beta = chunks(beta[..., None])[..., 0]
    G = jnp.cumsum(g, axis=-1)
    idx = jnp.arange(CHUNK)
    causal = idx[:, None] >= idx[None, :]
    strict = idx[:, None] > idx[None, :]
    decay = jnp.exp(jnp.where(causal, G[..., :, None] - G[..., None, :], -jnp.inf))
    kk = jnp.einsum('bnhid,bnhjd->bnhij', k, k)
    a_mat = jnp.where(strict, beta[..., :, None] * kk * decay, 0.0) + jnp.eye(CHUNK, dtype=f32)
    rhs = jnp.concatenate([v * beta[..., None], k * (beta * jnp.exp(G))[..., None]], axis=-1)
    sol = lax.linalg.triangular_solve(a_mat, rhs, left_side=True, lower=True, unit_diagonal=True)
    u, w = sol[..., :dv], sol[..., dv:]
    qk = jnp.where(causal, jnp.einsum('bnhid,bnhjd->bnhij', q, k) * decay, 0.0)
    q_dec = q * jnp.exp(G)[..., None]
    k_dec = k * jnp.exp(G[..., -1:] - G)[..., None]
    chunk_decay = jnp.exp(G[..., -1])

    def step(state, inp):
        u_c, w_c, qk_c, qd_c, kd_c, cd_c = inp
        v_new = u_c - jnp.einsum('bhcd,bhde->bhce', w_c, state)
        o_c = jnp.einsum('bhcd,bhde->bhce', qd_c, state) + jnp.einsum('bhij,bhje->bhie', qk_c, v_new)
        state = state * cd_c[..., None, None] + jnp.einsum('bhcd,bhce->bhde', kd_c, v_new)
        return state, o_c

    xs = (jnp.moveaxis(u, 1, 0), jnp.moveaxis(w, 1, 0), jnp.moveaxis(qk, 1, 0),
          jnp.moveaxis(q_dec, 1, 0), jnp.moveaxis(k_dec, 1, 0), jnp.moveaxis(chunk_decay, 1, 0))
    state0 = jnp.zeros((b, h, dk, dv), f32)
    _, o = lax.scan(step, state0, xs)
    return o.transpose(1, 0, 3, 2, 4).reshape(b, s, h, dv).astype(out_dtype)

def sliding_window_attention(q, k, v, sinks):
    f32 = jnp.float32
    b, s = q.shape[:2]
    nc = s // CHUNK
    band_len = WINDOW_CHUNKS * CHUNK
    qc = q.reshape(b, nc, CHUNK, N_KV_HEADS_B, GQA_GROUP, HEAD_DIM_B)

    def band(t):
        tc = t.reshape(b, nc, CHUNK, N_KV_HEADS_B, HEAD_DIM_B)
        tp = jnp.pad(tc, ((0, 0), (WINDOW_CHUNKS - 1, 0), (0, 0), (0, 0), (0, 0)))
        return jnp.concatenate([tp[:, i:i + nc] for i in range(WINDOW_CHUNKS)], axis=2)

    kb, vb = band(k), band(v)
    scores = jnp.einsum('bnqhgd,bnkhd->bnhgqk', qc, kb).astype(f32) * HEAD_DIM_B ** -0.5
    q_pos = (WINDOW_CHUNKS - 1) * CHUNK + jnp.arange(CHUNK)
    k_pos = jnp.arange(band_len)
    dist = jnp.abs(q_pos[:, None] - k_pos[None, :]).astype(f32)
    slopes = alibi_slopes(N_Q_HEADS_B).reshape(N_KV_HEADS_B, GQA_GROUP)
    scores = scores - slopes[:, :, None, None] * dist
    key_chunk = jnp.arange(nc)[:, None] + k_pos[None, :] // CHUNK - (WINDOW_CHUNKS - 1)
    valid = key_chunk >= 0
    scores = jnp.where(valid[None, :, None, None, None, :], scores, -jnp.inf)
    sink = jnp.broadcast_to(sinks.astype(f32).reshape(N_KV_HEADS_B, GQA_GROUP, 1, 1),
                            scores.shape[:-1] + (1,))
    probs = jax.nn.softmax(jnp.concatenate([scores, sink], axis=-1), axis=-1)[..., :-1]
    out = jnp.einsum('bnhgqk,bnkhd->bnqhgd', probs.astype(v.dtype), vb)
    return out.reshape(b, s, Q_DIM_B)

def hierarchical_moe(h, w_rg, b_rg, w_re, b_re, w_gate, w_up, w_down):
    f32 = jnp.float32
    b, s, d = h.shape
    t = h.reshape(b * s, d)
    grp_prob = jax.nn.softmax((t @ w_rg).astype(f32) + b_rg.astype(f32), axis=-1)
    grp_p, grp_idx = lax.top_k(grp_prob, 1)
    exp_logits = ((t @ w_re).astype(f32) + b_re.astype(f32)).reshape(-1, N_EXPERT_GROUPS, EXPERTS_PER_GROUP)
    grp_onehot = jax.nn.one_hot(grp_idx[:, 0], N_EXPERT_GROUPS, dtype=f32)
    in_group = jnp.einsum('tg,tge->te', grp_onehot, exp_logits)
    top_logits, top_local = lax.top_k(in_group, TOP_K_IN_GROUP)
    weights = grp_p * jax.nn.softmax(top_logits, axis=-1)
    expert_id = grp_idx * EXPERTS_PER_GROUP + top_local
    combine = jnp.einsum('tk,tke->te', weights,
                         jax.nn.one_hot(expert_id, N_EXPERTS, dtype=f32)).astype(h.dtype)
    out = jnp.zeros_like(t)
    for gi in range(N_EXPERT_GROUPS):
        e = slice(gi * EXPERTS_PER_GROUP, (gi + 1) * EXPERTS_PER_GROUP)
        act = jax.nn.silu(jnp.einsum('td,edf->tef', t, w_gate[e])) * jnp.einsum('td,edf->tef', t, w_up[e])
        out = out + jnp.einsum('tef,efd->td', act * combine[:, e, None], w_down[e])
    return out.reshape(b, s, d)

def setup_inputs(seed: int = 0) -> dict:
    key = jax.random.key(seed)
    ks = jax.random.split(key, 20)
    f32 = jnp.float32
    L = DEPTH

    def dense(k, shape, fan_in):
        return jax.random.normal(k, shape, f32) * fan_in ** -0.5

    def gain(k, shape):
        return 1.0 + 0.02 * jax.random.normal(k, shape, f32)

    dt = jnp.exp(jax.random.uniform(ks[5], (L, N_HEADS_A), f32, jnp.log(1e-3), jnp.log(1e-1)))
    return {
        "x": jax.random.normal(ks[0], (BATCH, SEQ, D_MODEL), f32),
        "norm_mix_w": gain(ks[1], (L, D_MODEL)),
        "w_in": dense(ks[2], (L, D_MODEL, IN_PROJ_DIM), D_MODEL),
        "conv_w": dense(ks[3], (L, CONV_WIDTH, CONV_DIM), CONV_WIDTH),
        "a_log": jnp.log(jax.random.uniform(ks[4], (L, N_HEADS_A), f32, 1.0, 16.0)),
        "dt_bias": dt + jnp.log(-jnp.expm1(-dt)),
        "delta_norm_w": gain(ks[6], (L, HEAD_DIM_A)),
        "sinks": 0.5 * jax.random.normal(ks[7], (L, N_Q_HEADS_B), f32),
        "w_out_a": dense(ks[8], (L, VAL_DIM_A, D_MODEL), VAL_DIM_A),
        "w_out_b": dense(ks[9], (L, Q_DIM_B, D_MODEL), Q_DIM_B),
        "w_out": dense(ks[10], (L, D_MODEL, D_MODEL), D_MODEL),
        "norm_ffn_w": gain(ks[11], (L, D_MODEL)),
        "w_router_group": dense(ks[12], (L, D_MODEL, N_EXPERT_GROUPS), D_MODEL),
        "b_router_group": 0.01 * jax.random.normal(ks[13], (L, N_EXPERT_GROUPS), f32),
        "w_router_expert": dense(ks[14], (L, D_MODEL, N_EXPERTS), D_MODEL),
        "b_router_expert": 0.01 * jax.random.normal(ks[15], (L, N_EXPERTS), f32),
        "w_gate": dense(ks[16], (L, N_EXPERTS, D_MODEL, D_FF_EXPERT), D_MODEL),
        "w_up": dense(ks[17], (L, N_EXPERTS, D_MODEL, D_FF_EXPERT), D_MODEL),
        "w_down": dense(ks[18], (L, N_EXPERTS, D_FF_EXPERT, D_MODEL), D_FF_EXPERT),
        "norm_final_w": gain(ks[19], (D_MODEL,)),
    }

def reference(x, norm_mix_w, w_in, conv_w, a_log, dt_bias, delta_norm_w, sinks, w_out_a, w_out_b, w_out,
              norm_ffn_w, w_router_group, b_router_group, w_router_expert, b_router_expert,
              w_gate, w_up, w_down, norm_final_w):
    f32 = jnp.float32
    b, s, _ = x.shape
    split_points = np.cumsum(IN_PROJ_WIDTHS)[:-1].tolist()
    for layer in range(DEPTH):
        h = rms_norm(x, norm_mix_w[layer])
        proj = h @ w_in[layer]
        qkv_a, z_a, beta_a, alpha_a, q_b, k_b, v_b, gate_a, gate_b = jnp.split(proj, split_points, axis=-1)

        qkv_a = jax.nn.silu(causal_depthwise_conv(qkv_a, conv_w[layer]))
        q_a, k_a, v_a = jnp.split(qkv_a, [KEY_DIM_A, 2 * KEY_DIM_A], axis=-1)
        q_a = l2_normalize(q_a.reshape(b, s, N_HEADS_A, HEAD_DIM_A))
        k_a = l2_normalize(k_a.reshape(b, s, N_HEADS_A, HEAD_DIM_A))
        v_a = v_a.reshape(b, s, N_HEADS_A, HEAD_DIM_A)
        beta = jax.nn.sigmoid(beta_a.astype(f32))
        log_decay = -jnp.exp(a_log[layer].astype(f32)) * jax.nn.softplus(
            alpha_a.astype(f32) + dt_bias[layer].astype(f32))
        o_a = gated_delta_rule(q_a, k_a, v_a, log_decay, beta)
        o_a = rms_norm(o_a, delta_norm_w[layer]) * jax.nn.silu(z_a.reshape(b, s, N_HEADS_A, HEAD_DIM_A))
        y_a = o_a.reshape(b, s, VAL_DIM_A) @ w_out_a[layer]

        o_b = sliding_window_attention(q_b.reshape(b, s, N_Q_HEADS_B, HEAD_DIM_B),
                                       k_b.reshape(b, s, N_KV_HEADS_B, HEAD_DIM_B),
                                       v_b.reshape(b, s, N_KV_HEADS_B, HEAD_DIM_B),
                                       sinks[layer])
        y_b = o_b @ w_out_b[layer]

        merged = jax.nn.sigmoid(gate_a) * y_a + jax.nn.sigmoid(gate_b) * y_b
        x = x + merged @ w_out[layer]

        x = x + hierarchical_moe(rms_norm(x, norm_ffn_w[layer]), w_router_group[layer], b_router_group[layer],
                                 w_router_expert[layer], b_router_expert[layer],
                                 w_gate[layer], w_up[layer], w_down[layer])
    return rms_norm(x, norm_final_w)


_drawn_inputs = setup_inputs


def setup_inputs(seed=0):
    import zlib

    import numpy as np

    out = dict(_drawn_inputs(seed))
    spreads = {}
    factors = {'norm_mix_w': 2.678,
     'delta_norm_w': 12.297,
     'sinks': 64.0,
     'b_router_group': 54.081,
     'b_router_expert': 38.696,
     'norm_final_w': 8.067,
     'norm_ffn_w': 8.0}
    for name, (base, spread) in spreads.items():
        noise = np.random.default_rng([zlib.crc32(name.encode()), seed]).standard_normal(out[name].shape)
        drawn = base * np.exp(spread * noise) if base else spread * noise
        out[name] = __import__('jax').numpy.asarray(drawn.astype(out[name].dtype))
    for name, factor in factors.items():
        out[name] = (out[name] * factor).astype(out[name].dtype)
    return out
```

```python
from contextlib import ExitStack

import numpy as np

import concourse.bass as bass
from concourse import mybir

F32 = mybir.dt.float32
F32R = mybir.dt.float32r
ALU = mybir.AluOpType
ACT = mybir.ActivationFunctionType
AX = mybir.AxisListType

P = 128
D = 1024
S = 512
KT = D // P
TT = S // P
CHUNK = 64
HA, DA = 4, 128
KEYS_A = HA * DA
CONV = 3 * KEYS_A
TAPS = 4
HB, DB = 8, 64
KVB = 2
GRP = HB // KVB
WIN = 3 * CHUNK
NG, EG = 4, 4
NE = NG * EG
FF = 256
EPS = 1e-6
NEG = -1.0e30

C_Z = CONV
C_BA = C_Z + KEYS_A
C_QB = C_BA + 2 * HA
C_KV = C_QB + HB * DB
C_GA = C_KV + 2 * KVB * DB
C_GB = C_GA + D

U = 2048
RING = 3
UNITS_PROJ = 11
UNITS_MERGE = 12
UNITS_OUT = 4
UNITS_PRE = UNITS_PROJ + UNITS_MERGE + UNITS_OUT
ITEMS = 2 * UNITS_PROJ
CONV_ITEMS = CONV // P
NORM_ITEMS = 2 * HA
KIND_G, KIND_U, KIND_D = 0, 1, 2


def build(nc, a, out):
    ctx = ExitStack()
    cursor = [16512]

    def at(name, shape, dt, offset):
        return nc.alloc_sbuf_tensor_at(name, shape, dt, offset=offset)

    def region(nbytes):
        o = cursor[0]
        cursor[0] += (nbytes + 31) // 32 * 32
        return o

    def new(name, shape, dt=F32):
        return at(name, shape, dt, region(int(np.prod(shape[1:])) * 4))

    with ctx:
        def sem(name):
            return ctx.enter_context(nc.semaphore(name))

        raw = [new(f"w_raw{i}", [P, U]) for i in range(RING)]
        whi = [new(f"w_hi{i}", [P, U], F32R) for i in range(RING)]
        wlo = [new(f"w_lo{i}", [P, U], F32R) for i in range(RING)]
        h_hi = new("h_hi", [P, KT, S], F32R)
        h_lo = new("h_lo", [P, KT, S], F32R)
        r_main = region(4 * 2 * KT * S)
        fm = at("conv_z_F", [P, 16, S], F32, r_main)
        m_hi = at("merged_hi", [P, KT, S], F32R, r_main)
        m_lo = at("merged_lo", [P, KT, S], F32R, r_main + 4 * KT * S)
        tx = at("ffn_in_T", [P, TT, D], F32, r_main)
        r_b = region(4 * (6 * S))
        qb = at("attn_q_F", [P, 4, S], F32, r_b)
        kb = at("attn_k_F", [P, S], F32, r_b + 4 * 4 * S)
        vb = at("attn_v_T", [P, TT, P], F32, r_b + 4 * 5 * S)
        r_tmp = region(4 * 3584)
        r_x = region(4 * TT * D)
        x = at("x_T", [P, TT, D], F32, r_x)
        oa_hi = at("oA_hi", [P, 4, S], F32R, r_x)
        oa_lo = at("oA_lo", [P, 4, S], F32R, r_x + 4 * 4 * S)
        r_o = region(4 * TT * D + 64)
        ob_hi = at("oB_hi", [P, 4, S], F32R, r_o)
        ob_lo = at("oB_lo", [P, 4, S], F32R, r_o + 4 * 4 * S)
        y = at("y_T", [P, TT, D], F32, r_x)
        xpad = [at(f"conv_in{i}", [P, S + 8], F32, r_o + i * 4 * (S + 8)) for i in range(2)]
        cacc = [at(f"conv_acc{i}", [P, S], F32, r_o + 4160 + i * 4 * S) for i in range(2)]
        sqb = [at(f"square{i}", [P, S], F32, r_o + 8256 + i * 4 * S) for i in range(2)]
        rsb = [at(f"norm_factor{i}", [P, S], F32, r_o + 12352 + i * 2048) for i in range(2)]
        junk = at("square_junk", [P, D], F32, r_tmp)
        junk_f = at("square_junk_final", [P, D], F32, r_tmp + 8192)
        rows = at("small_rows", [57, P], F32, r_tmp + 4096)
        ba_raw = at("ba_raw", [P, KT, 8], F32, r_tmp + 4608)
        ba_hi = at("ba_hi", [P, KT, 8], F32R, r_tmp + 4864)
        ba_lo = at("ba_lo", [P, KT, 8], F32R, r_tmp + 5120)
        ba_t = at("ba_T", [P, TT, 8], F32, r_tmp + 5376)
        ga1 = at("decay_in", [P, TT, HA], F32, r_tmp + 5504)
        ga2 = at("decay_abs", [P, TT, HA], F32, r_tmp + 5568)
        ga3 = at("decay_exp", [P, TT, HA], F32, r_tmp + 5632)
        dist_i = at("key_distance_i", [P, WIN], mybir.dt.int32, r_tmp + 8192)
        dist = at("key_distance", [P, WIN], F32, r_tmp + 8960)
        dist_m = at("key_distance_abs", [P, WIN], F32, r_tmp + 9728)
        wmask = at("window_mask", [P, WIN], F32, r_tmp + 10496)
        ob_t = at("attn_out_T", [P, HB, DB], F32, r_tmp + 11264)
        mxs = at("score_max", [P, GRP], F32, r_tmp + 13312)
        nmx = at("score_max_neg", [P, GRP], F32, r_tmp + 13344)
        esk = at("sink_term", [P, GRP], F32, r_tmp + 13376)
        sms = at("prob_sum", [P, GRP], F32, r_tmp + 13408)
        den = at("prob_norm", [P, GRP], F32, r_tmp + 13440)
        bias = at("alibi_bias", [P, HB, WIN], F32, r_x)
        pb = at("probs", [P, GRP, 2 * P], F32, r_x + 6144)
        pt = at("probs_F", [P, 2, GRP, P], F32, r_x + 10240)
        dn = [at(f"dn{i}", [P, HA, P], F32, r_b + 2048 * i) for i in range(12)]
        (d_dec, d_lt, d_qd, d_kq, d_k, d_v, d_kd, d_inv, d_invT, d_x, d_c, d_s) = dn
        sg = at("gates_F", [P, 4, S], F32, r_b)
        prod = at("gated_A", [P, 2, S], F32, r_b + 4 * 4 * S)
        mrg = at("merged", [P, 2, S], F32, r_tmp)
        nfin = at("norm_final_b", [P, D], F32, r_tmp + 4096)
        eg = at("gate_silu", [P, 2, S], F32, r_main + 4 * KT * S)
        ea = at("hidden", [P, 2, S], F32, r_main + 4 * KT * S + 4096)
        ea_hi = at("hidden_hi", [P, 2, S], F32R, r_main + 4 * KT * S + 8192)
        ea_lo = at("hidden_lo", [P, 2, S], F32R, r_main + 4 * KT * S + 12288)
        rt_at = [r_o]

        def rt(name, shape):
            o = rt_at[0]
            rt_at[0] += (int(np.prod(shape[1:])) * 4 + 31) // 32 * 32
            return at(name, shape, F32, o)

        lg = rt("router_logits", [P, TT, NG + NE])
        gmx, gsm, gp = rt("group_max", [P, TT]), rt("group_sum", [P, TT]), rt("group_prob", [P, TT])
        gex, gkey, goh = rt("group_exp", [P, TT, NG]), rt("group_key", [P, TT, NG]), rt("group_onehot", [P, TT, NG])
        kmx = rt("key_max", [P, TT])
        eprod = rt("group_logits", [P, TT * NG, EG])
        ig, ekey = rt("in_group", [P, TT, EG]), rt("expert_key", [P, TT, EG])
        e1, e2 = rt("first_onehot", [P, TT, EG]), rt("second_onehot", [P, TT, EG])
        m1, m2, dif, w1, w2 = (rt(n_, [P, TT]) for n_ in ("first_logit", "second_logit", "logit_gap", "first_weight", "second_weight"))
        ce, ce2 = rt("in_group_weights", [P, TT, EG]), rt("in_group_weights2", [P, TT, EG])
        ident = new("ident", [P, P])
        ones = new("ones", [P, P])
        tri = new("tri", [P, P])
        negm = new("neg_mask", [P, P])
        blk = new("same_chunk", [P, P])
        lvl = new("level_masks", [P, 6, P])
        cols = new("small_cols", [P, 57])
        nffn = new("norm_ffn_cols", [P, KT])
        ssq = new("sum_squares", [P, TT])
        rst = new("rms_factor", [P, TT])
        rsq_i = new("rsqrt_seed", [P, TT], mybir.dt.int32)
        rsq_t = new("rsqrt_tmp", [P, TT])
        epsb = new("eps", [P, 1])
        bta = new("beta_T", [P, TT, HA])
        gdt = new("log_decay_T", [P, TT, HA])
        alog = new("a_log_b", [P, HA])
        dtb = new("dt_bias_b", [P, HA])
        ealog = new("exp_a_log", [P, HA])
        gsum = new("decay_sums_T", [P, 4, TT * HA])
        gexp = new("exp_G", [P, TT, HA])
        kds = new("exp_Gend_minus_G", [P, TT, HA])
        cdec = new("chunk_decay", [P, 2, TT, HA])
        bexp = new("beta_exp_G", [P, TT, HA])
        osq = new("out_square_sum", [P, HA])
        ors = new("out_rms_factor", [P, HA])
        sinkb = new("sinks_b", [P, HB])
        rw_raw = new("router_raw", [P, KT, NG + NE])
        rw_hi = new("router_hi", [P, KT, NG + NE], F32R)
        rw_lo = new("router_lo", [P, KT, NG + NE], F32R)
        prio = new("index_priority", [P, EG])
        comb = new("combine", [P, TT, NE])
        cwe = new("combine_of_expert", [P, TT])
        brg = new("router_bias", [P, NG + NE])

        ps = [ctx.enter_context(nc.psum_tensor(f"bank{i}", [P, S], F32)) for i in range(8)]

        x_in = [sem(f"x_in{t}") for t in range(TT)]
        small_in = sem("small_in")
        raw_in = [sem(f"raw_in{i}") for i in range(RING)]
        dve_step, act_step, pool_step = sem("dve_step"), sem("act_step"), sem("pool_step")
        consts = sem("consts_ready")
        eps_set = sem("eps_set")
        hi_done, lo_done = sem("w_hi_done"), sem("w_lo_done")
        ssq_done, x_scaled = sem("ssq_done"), sem("x_scaled")
        rows_ps, cols_done = sem("rows_ps"), sem("cols_done")
        ht_ps, ht_hi, ht_lo = sem("ht_ps"), sem("ht_hi"), sem("ht_lo")
        pad_zero = sem("pad_zero")
        ba_hi_done, ba_lo_done, ba_ps, ba_copied = sem("ba_hi_done"), sem("ba_lo_done"), sem("ba_ps"), sem("ba_copied")
        proj_ps, proj_evac = sem("proj_ps"), sem("proj_evac")
        conv_done, silu_done, sq_done = sem("conv_done"), sem("silu_done"), sem("sq_done")
        norm_ps, root_done, norm_done = sem("norm_ps"), sem("root_done"), sem("norm_done")
        gd_abs, gd_exp, gd_ln, gates_done = sem("gd_abs"), sem("gd_exp"), sem("gd_ln"), sem("gates_done")
        dist_set, bias_done, attn_zero = sem("dist_set"), sem("bias_done"), sem("probs_zeroed")
        sc_ps, max_done, exp_done = sem("scores_ps"), sem("max_done"), sem("probs_exp")
        pt_ps, pt_prev, pt_cur = sem("probsF_ps"), sem("probsF_prev"), sem("probsF_cur")
        pv_ps, ob_ready, obt_ps = sem("pv_ps"), sem("attn_out_T_ready"), sem("attn_out_F_ps")
        ob_hi_done, ob_lo_done = sem("oB_hi_done"), sem("oB_lo_done")
        gsum_ps, gsum_sub, gexp_done, dscal_done = sem("gsum_ps"), sem("gsum_sub"), sem("gexp_done"), sem("dscal_done")
        rb_ready, rb_ps, dec_in = sem("row_source"), sem("row_bcast_ps"), sem("decay_arg")
        egb_done, dec_done = sem("exp_G_rows"), sem("decay_done")
        kk_ps, kv_ps, qd_done, kbv_done = sem("kk_ps"), sem("kv_T_ps"), sem("q_decayed"), sem("kv_scaled")
        inv0, inv0_ps, inv0_copied = sem("inv_T_first"), sem("inv_first_ps"), sem("inv_first")
        ct_done, x_ps, xs_done, de_ps, de_done = (sem("level_block"), sem("block_inv_ps"), sem("block_inv"),
                                                  sem("inv_update_ps"), sem("inv_updated"))
        wu_ps, wu_done = sem("wu_ps"), sem("wu_done")
        s_zero, ws_ps, vn_done, o_ps, ds_ps, s_done = (sem("state_zero"), sem("w_state_ps"), sem("v_new"),
                                                       sem("o_ps"), sem("state_add_ps"), sem("state_done"))
        on_done, oat_ps, oaf_done = sem("o_normed"), sem("oA_F_ps"), sem("oA_F_gated")
        oa_hi_done, oa_lo_done = sem("oA_hi_done"), sem("oA_lo_done")
        mg_ps, sg_done, mul_done = sem("merge_ps"), sem("gate_sigmoid"), sem("gate_product")
        mg_hi, mg_lo = sem("merged_hi_done"), sem("merged_lo_done")
        x2_in, out_used, y_done = sem("x_again"), sem("out_proj_ps"), sem("residual_done")
        ssq2, t_scaled, tt_ps, tt_hi, tt_lo = sem("ssq2"), sem("ffn_scaled"), sem("ffn_F_ps"), sem("ffn_hi"), sem("ffn_lo")
        rw_hi_done, rw_lo_done, lg_ps = sem("router_w_hi"), sem("router_w_lo"), sem("router_ps")
        gd_in, gd_out, ed_in, ed_out, comb_done = (sem("group_arg"), sem("group_exp_done"), sem("pair_arg"),
                                                   sem("pair_exp_done"), sem("combine_done"))
        gate_ps, up_ps, dn_ps = sem("gate_ps"), sem("up_ps"), sem("down_ps")
        gsilu, hid_done, hid_hi, hid_lo = sem("gate_silu_done"), sem("hidden_done"), sem("hidden_hi_done"), sem("hidden_lo_done")
        cwe_done, yacc = sem("combine_col"), sem("y_added")
        nfin_in, ssq3, fin_done, stored = sem("norm_final_in"), sem("ssq3"), sem("final_done"), sem("stored")

        w_in = a["w_in"][0].rearrange("(k p) n -> p k n", p=P)

        def unit_sources(u):
            r = raw[u % RING][:, :].rearrange("p (k n) -> p k n", k=KT)
            if u < 8:
                return [(r, w_in[:, :, 256 * u:256 * (u + 1)])]
            if u < 10:
                q = w_in[:, :, C_QB:C_QB + HB * DB].rearrange("p k (g j c) -> p k j g c", g=KVB, j=GRP)
                return [(r[:, :, 128 * i + 64 * g:128 * i + 64 * g + 64], q[:, :, 2 * (u - 8) + i, g, :])
                        for i in range(2) for g in range(KVB)]
            if u == 10:
                return [(r, w_in[:, :, C_KV:C_KV + 256])]
            if u < UNITS_PROJ + UNITS_MERGE:
                j, c = divmod(u - UNITS_PROJ, 3)
                cs = slice(256 * j, 256 * (j + 1))
                if c < 2:
                    o = (C_GA, C_GB)[c] + 256 * j
                    return [(r, w_in[:, :, o:o + 256])]
                return [(r[:, 0:4, :], a["w_out_a"][0].rearrange("(k p) n -> p k n", p=P)[:, :, cs]),
                        (r[:, 4:8, :], a["w_out_b"][0].rearrange("(k p) n -> p k n", p=P)[:, :, cs])]
            n_, kh = divmod(u - UNITS_PROJ - UNITS_MERGE, 2)
            return [(raw[u % RING][:, :].rearrange("p (k n) -> p k n", k=4),
                     a["w_out"][0].rearrange("(k p) n -> p k n", p=P)[:, 4 * kh:4 * kh + 4, 512 * n_:512 * (n_ + 1)])]

        def unit_dmas(u):
            return len(unit_sources(u))

        def raw_value(u):
            return 16 * sum(unit_dmas(v) for v in range(u % RING, u + 1, RING))

        def bc_mid(ap, n):
            return ap.unsqueeze(1).broadcast_to([ap.shape[0], n, ap.shape[1]])

        def bc_last(ap, n):
            return ap.unsqueeze(2).broadcast_to([ap.shape[0], ap.shape[1], n])

        def bank4(i):
            return ps[i][:, :].rearrange("p (h c) -> p h c", h=4)

        block = ctx.enter_context(nc.Block())

        RAW_PRE = [16 * sum(unit_dmas(v) for v in range(s_, UNITS_PRE, RING)) for s_ in range(RING)]

        def wait_used(eng, v):
            if v < UNITS_PROJ:
                eng.wait_ge(proj_ps, 2 * (v + 1))
            elif v < UNITS_PROJ + UNITS_MERGE:
                j, c = divmod(v - UNITS_PROJ, 3)
                eng.wait_ge(mg_ps, 8 * j + (2, 4, 8)[c])
            else:
                eng.wait_ge(out_used, v - UNITS_PROJ - UNITS_MERGE + 1)

        def up_at(e):
            return UNITS_PRE + 2 + 3 * e

        def gate_at(e):
            return UNITS_PRE + 3 * e

        def down_at(e):
            last = isinstance(e, int) and e == NE - 1
            return UNITS_PRE + 4 + 3 * e - last

        def is_first(e):
            return isinstance(e, int) and e == 0

        w_gate_v = a["w_gate"][0].rearrange("e (p k) f -> e p (k f)", p=P)
        w_up_v = a["w_up"][0].rearrange("e (p k) f -> e p (k f)", p=P)
        w_down_v = a["w_down"][0].rearrange("e (f p) d -> e p f d", p=P)
        kv_ = lambda r: r[:, :].rearrange("p (k n) -> p k n", k=KT)
        fd_ = lambda r: r[:, :].rearrange("p (f d) -> p f d", f=2)
        full, rest = NE - 2, (NE - 2, NE - 1)

        def norms_at(i):
            return range(2 * (i - 17), 2 * (i - 17) + 2) if 17 <= i < 17 + NORM_ITEMS // 2 else ()

        @block.sync
        def _(sp):
            for t in range(TT):
                sp.dma_start(x[:, t, :], a["x"][0, t * P:(t + 1) * P, :]).then_inc(x_in[t], 16)
            sp.dma_start(rows[0:8, :], a["norm_mix_w"][0].rearrange("(k p) -> k p", p=P)).then_inc(small_in, 16)
            sp.dma_start(rows[8:56, :], a["conv_w"][0].rearrange("j (i p) -> (j i) p", p=P)).then_inc(small_in, 16)
            sp.dma_start(rows[56:57, :], a["delta_norm_w"]).then_inc(small_in, 16)
            sp.dma_start(ba_raw[:, :, :], w_in[:, :, C_BA:C_BA + 8]).then_inc(small_in, 16)
            sp.dma_start(dtb[:, :], a["dt_bias"].to_broadcast([P, HA])).then_inc(small_in, 16)
            sp.dma_start(alog[:, :], a["a_log"].to_broadcast([P, HA])).then_inc(small_in, 16)
            sp.dma_start(sinkb[:, :], a["sinks"].to_broadcast([P, HB])).then_inc(small_in, 16)
            sp.dma_start(brg[:, 0:NG], a["b_router_group"].to_broadcast([P, NG])).then_inc(small_in, 16)
            sp.dma_start(brg[:, NG:], a["b_router_expert"].to_broadcast([P, NE])).then_inc(small_in, 16)
            sp.dma_start(nffn[:, :], a["norm_ffn_w"][0].rearrange("(p k) -> p k", k=KT)).then_inc(small_in, 16)
            sp.dma_start(rw_raw[:, :, 0:NG], a["w_router_group"][0].rearrange("(p k) n -> p k n", k=KT)).then_inc(small_in, 16)
            sp.dma_start(rw_raw[:, :, NG:], a["w_router_expert"][0].rearrange("(p k) n -> p k n", k=KT)).then_inc(small_in, 16)
            for u in range(UNITS_PRE):
                if u >= RING:
                    sp.wait_ge(hi_done, u - RING + 1)
                    sp.wait_ge(lo_done, u - RING + 1)
                for dst, src in unit_sources(u):
                    sp.dma_start(dst, src).then_inc(raw_in[u % RING], 16)
            sp.wait_ge(mg_ps, 8 * 4)
            sp.dma_start(y[:, :, :], a["x"][0].rearrange("(t p) d -> p t d", p=P)).then_inc(x2_in, 16)
            sp.dma_start(nfin[:, :], a["norm_final_w"].rearrange("(o d) -> o d", o=1).to_broadcast([P, D])).then_inc(nfin_in, 16)

            def load(slot, src, split):
                sp.wait_ge(hi_done, split)
                sp.wait_ge(lo_done, split)
                dst = fd_(raw[slot]) if slot == KIND_D else raw[slot][:, :]
                sp.dma_start(dst, src).then_inc(raw_in[slot], 16)

            load(KIND_G, w_gate_v[0], UNITS_PRE - 2)
            load(KIND_U, w_up_v[0], UNITS_PRE - 1)
            load(KIND_G, w_gate_v[1], UNITS_PRE + 1)
            load(KIND_D, w_down_v[0], UNITS_PRE)

            def expert_loads(e, gates=True):
                load(KIND_U, w_up_v[e + 1], up_at(e))
                if gates:
                    load(KIND_G, w_gate_v[e + 2], gate_at(e + 1))
                load(KIND_D, w_down_v[e + 1], down_at(e))

            expert_loads(0)
            with sp.Fori(1, full) as e:
                expert_loads(e)
            expert_loads(full, gates=False)
            for t in range(TT):
                sp.wait_ge(fin_done, t + 1)
                sp.dma_start(out[0, t * P:(t + 1) * P, :], tx[:, t, :]).then_inc(stored, 16)
            sp.wait_ge(stored, 16 * TT)

        @block.gpsimd
        def _(pool):
            n = [0]

            def link(ins):
                n[0] += 1
                ins.then_inc(pool_step, 1)
                pool.wait_ge(pool_step, n[0])

            nc.gpsimd.memset(ones[:, :], 1.0)
            nc.gpsimd.memset(blk[:, :], 0.0)
            nc.gpsimd.memset(tri[:, :], 1.0)
            nc.gpsimd.memset(lvl[:, :, :], 1.0)
            link(nc.gpsimd.memset(ident[:, :], 0.0))
            link(nc.gpsimd.affine_select(out=ident[:, :], in_=ident[:, :], compare_op=ALU.not_equal, fill=1.0,
                                         base=0, pattern=[[-1, P]], channel_multiplier=1))
            link(nc.gpsimd.memset(blk[0:64, 0:64], 1.0))
            link(nc.gpsimd.memset(blk[64:128, 64:128], 1.0))
            link(nc.gpsimd.affine_select(out=tri[:, :], in_=tri[:, :], compare_op=ALU.is_ge, fill=0.0,
                                         base=0, pattern=[[1, P]], channel_multiplier=-1))
            link(nc.gpsimd.affine_select(out=tri[:, 64:128], in_=tri[:, 64:128], compare_op=ALU.is_ge, fill=0.0,
                                         base=-64, pattern=[[0, 64]], channel_multiplier=1))
            for l in range(6):
                b = 1 << l
                m = lvl[:, l, :].rearrange("p (n r) -> p n r", r=2 * b)
                nc.gpsimd.memset(m[:, :, 0:b], 0.0).then_inc(pool_step, 1)
                n[0] += 1
                pool.wait_ge(pool_step, n[0])
                link(nc.gpsimd.affine_select(out=m, in_=m, compare_op=ALU.is_ge, fill=0.0, base=0,
                                             pattern=[[-2 * b, P // (2 * b)], [0, 2 * b]], channel_multiplier=1))
                link(nc.gpsimd.affine_select(out=m, in_=m, compare_op=ALU.is_ge, fill=0.0, base=b - 1,
                                             pattern=[[2 * b, P // (2 * b)], [0, 2 * b]], channel_multiplier=-1))
            nc.gpsimd.tensor_scalar(negm[:, :], tri[:, :], -1.0, -NEG, ALU.add, ALU.mult).then_inc(consts, 1)
            link(nc.gpsimd.iota(dist_i[:, :], pattern=[[-1, WIN]], base=CHUNK, channel_multiplier=1))
            link(nc.gpsimd.memset(wmask[:, :], 0.0))
            nc.gpsimd.memset(wmask[0:64, 128:192], NEG)
            nc.gpsimd.memset(wmask[64:128, 0:64], NEG).then_inc(dist_set, 1)

        @block.scalar
        def _(act):
            n = [0]

            def link(ins):
                n[0] += 1
                ins.then_inc(act_step, 1)
                act.wait_ge(act_step, n[0])

            def split_hi(u):
                act.wait_ge(raw_in[u % RING], raw_value(u))
                if u >= RING:
                    wait_used(act, u - RING)
                act.activation(whi[u % RING][:, :], raw[u % RING][:, :], ACT.Copy).then_inc(hi_done, 1)

            act.wait_ge(eps_set, 1)
            for t in range(TT):
                act.wait_ge(x_in[t], 16)
                link(act.activation(junk[:, :], x[:, t, :], ACT.Square, accum_out=ssq[:, t:t + 1]))
                act.activation(rst[:, t:t + 1], ssq[:, t:t + 1], ACT.Sqrt, scale=1.0 / D, bias=epsb[:, :]).then_inc(ssq_done, 1)
            act.wait_ge(small_in, 192)
            act.activation(ba_hi[:, :, :], ba_raw[:, :, :], ACT.Copy).then_inc(ba_hi_done, 1)
            act.activation(rw_hi[:, :, :], rw_raw[:, :, :], ACT.Copy).then_inc(rw_hi_done, 1)
            act.activation(ealog[:, :], alog[:, :], ACT.Exp).then_inc(gd_exp, 1)
            split_hi(0)
            split_hi(1)
            act.wait_ge(cols_done, 1)
            for k in range(KT):
                act.wait_ge(ht_ps, k + 1)
                act.activation(h_hi[:, k, :], ps[k % 2][:, :], ACT.Copy, scale=cols[:, k:k + 1]).then_inc(ht_hi, 1)

            def conv_silu(i):
                act.wait_ge(conv_done, i + 1)
                act.activation(fm[:, i, :], cacc[i % 2][:, :], ACT.Silu).then_inc(silu_done, 1)

            def square(i):
                act.wait_ge(silu_done, i + 1)
                if i >= 2:
                    act.wait_ge(norm_ps, i - 1)
                act.activation(sqb[i % 2][:, :], fm[:, i, :], ACT.Square).then_inc(sq_done, 1)

            def norm_root(i):
                act.wait_ge(norm_ps, i + 1)
                if i >= 2:
                    act.wait_ge(norm_done, i - 1)
                act.activation(rsb[i % 2][:, :], ps[2 + i % 2][:, :], ACT.Sqrt, bias=epsb[:, :]).then_inc(root_done, 1)

            for i in range(ITEMS):
                if i % 2 == 0 and i // 2 + 2 < UNITS_PROJ:
                    split_hi(i // 2 + 2)
                act.wait_ge(proj_ps, i + 1)
                if i < CONV_ITEMS:
                    act.wait_ge(pad_zero, 2)
                    if i >= 2:
                        act.wait_ge(conv_done, i - 1)
                    act.activation(xpad[i % 2][:, 3:3 + S], ps[i % 2][:, :], ACT.Copy).then_inc(proj_evac, 1)
                elif i < 16:
                    act.activation(fm[:, i, :], ps[i % 2][:, :], ACT.Silu).then_inc(proj_evac, 1)
                elif i < 20:
                    act.activation(qb[:, i - 16, :], ps[i % 2][:, :], ACT.Copy).then_inc(proj_evac, 1)
                elif i == 20:
                    act.activation(kb[:, :], ps[i % 2][:, :], ACT.Copy).then_inc(proj_evac, 1)
                else:
                    act.activation(vb[:, :, :], ps[i % 2][:, :].rearrange("p (t c) -> p t c", t=TT),
                                   ACT.Copy).then_inc(proj_evac, 1)
                if 1 <= i <= CONV_ITEMS:
                    conv_silu(i - 1)
                for j in norms_at(i):
                    norm_root(j)
                for j in norms_at(i + 1):
                    square(j)
            act.wait_ge(ba_copied, 1)
            act.activation(bta[:, :, :], ba_t[:, :, 0:HA], ACT.Sigmoid).then_inc(gates_done, 1)
            act.wait_ge(gd_abs, 1)
            link(act.activation(ga3[:, :, :], ga2[:, :, :], ACT.Exp, scale=-1.0))
            act.activation(ga2[:, :, :], ga3[:, :, :], ACT.Ln, bias=1.0).then_inc(gd_ln, 1)


            for a_ in range(2 * TT):
                m, g = a_ // 2, a_ % 2
                c0 = CHUNK if m else P
                act.wait_ge(max_done, a_ + 1)
                for h in range(GRP):
                    act.activation(pb[:, h, c0:], pb[:, h, c0:], ACT.Exp, bias=nmx[:, h:h + 1], accum_out=sms[:, h:h + 1])
                act.activation(esk[:, :], esk[:, :], ACT.Exp).then_inc(exp_done, 1)
                if m:
                    act.wait_ge(pt_ps, 2 * a_ + 1)
                    if a_ > 2:
                        act.wait_ge(pv_ps, a_)
                    act.activation(pt[:, 0, :, :], bank4(2), ACT.Copy).then_inc(pt_prev, 1)
                if g == 1:
                    act.wait_ge(obt_ps, m + 1)
                    act.activation(ob_hi[:, :, m * P:(m + 1) * P], bank4(5), ACT.Copy).then_inc(ob_hi_done, 1)

            act.wait_ge(gsum_sub, 1)
            act.activation(gexp[:, :, :], gsum[:, 0, :], ACT.Exp)
            act.activation(kds[:, :, :], gsum[:, 1, :], ACT.Exp)
            act.activation(cdec[:, :, :, :], gsum[:, 2:4, :], ACT.Exp).then_inc(gexp_done, 1)
            for m in range(TT):
                act.wait_ge(dec_in, m + 1)
                if m:
                    act.wait_ge(o_ps, m)
                act.activation(d_qd[:, :, :], bank4(2), ACT.Exp).then_inc(egb_done, 1)
                act.activation(d_dec[:, :, :], d_dec[:, :, :], ACT.Exp).then_inc(dec_done, 1)
                act.wait_ge(inv0_ps, m + 1)
                act.activation(d_inv[:, :, :], bank4(2), ACT.Copy).then_inc(inv0_copied, 1)
                for l in range(1, 6):
                    act.wait_ge(x_ps, 5 * m + l)
                    act.activation(d_x[:, :, :], bank4(2), ACT.Copy).then_inc(xs_done, 1)
                act.wait_ge(wu_ps, m + 1)
                act.activation(d_k[:, :, :], bank4(5), ACT.Copy)
                act.activation(d_v[:, :, :], bank4(6), ACT.Copy).then_inc(wu_done, 1)
                act.wait_ge(oaf_done, m + 1)
                act.activation(oa_hi[:, :, m * P:(m + 1) * P], d_lt[:, :, :], ACT.Copy).then_inc(oa_hi_done, 1)

            act.wait_ge(oa_lo_done, TT)
            for u in range(UNITS_PROJ, UNITS_PROJ + 2):
                split_hi(u)
            for j in range(4):
                for r in range(4):
                    if r % 2 == 0:
                        split_hi(UNITS_PROJ + 2 + 3 * j + r // 2)
                    act.wait_ge(mg_ps, 8 * j + r + 1)
                    if j:
                        act.wait_ge(mul_done, 4 * j)
                    act.activation(sg[:, r, :], ps[r][:, :], ACT.Sigmoid).then_inc(sg_done, 1)
                for r in range(2):
                    act.wait_ge(mul_done, 4 * j + 3 + r)
                    act.activation(m_hi[:, 2 * j + r, :], mrg[:, r, :], ACT.Copy).then_inc(mg_hi, 1)
                split_hi(UNITS_PROJ + 4 + 3 * j)
            for u in range(UNITS_PRE - 2, UNITS_PRE):
                split_hi(u)
            for t in range(TT):
                act.wait_ge(y_done, 4 + t + 1)
                if t:
                    act.wait_ge(ssq2, t)
                act.activation(junk[:, :], y[:, t, :], ACT.Square, accum_out=ssq[:, t:t + 1]).then_inc(ssq2, 1)

            def split_expert(slot, arrived, free=None):
                act.wait_ge(raw_in[slot], arrived)
                if free:
                    act.wait_ge(*free)
                act.activation(whi[slot][:, :], raw[slot][:, :], ACT.Copy).then_inc(hi_done, 1)

            split_expert(KIND_G, RAW_PRE[KIND_G] + 16, (out_used, 2))
            split_expert(KIND_U, RAW_PRE[KIND_U] + 16, (out_used, 3))
            for k in range(KT):
                act.wait_ge(tt_ps, k + 1)
                act.activation(h_hi[:, k, :], ps[k % 2][:, :], ACT.Copy, scale=nffn[:, k:k + 1]).then_inc(tt_hi, 1)
            act.wait_ge(gd_in, 1)
            act.activation(gex[:, :, :], gex[:, :, :], ACT.Exp).then_inc(gd_out, 1)
            act.wait_ge(ed_in, 1)
            act.activation(dif[:, :], dif[:, :], ACT.Exp).then_inc(ed_out, 1)

            def gate_silu(e):
                for f in range(2):
                    act.wait_ge(gate_ps, 2 * e + f + 1)
                    act.activation(eg[:, f, :], ps[f][:, :], ACT.Silu).then_inc(gsilu, 1)

            gate_silu(0)
            split_expert(KIND_G, RAW_PRE[KIND_G] + 32, (gate_ps, 2))
            split_expert(KIND_D, RAW_PRE[KIND_D] + 16, (out_used, 4))

            def expert_act(e, gates=True, last=False):
                if not last:
                    split_expert(KIND_U, RAW_PRE[KIND_U] + 16 * (e + 2), (up_ps, 2 * e + 2))
                if not is_first(e):
                    act.wait_ge(dn_ps, 8 * e)
                for f in range(2):
                    act.wait_ge(hid_done, 2 * e + f + 1)
                    act.activation(ea_hi[:, f, :], ea[:, f, :], ACT.Copy).then_inc(hid_hi, 1)
                if not last:
                    gate_silu(e + 1)
                    if gates:
                        split_expert(KIND_G, RAW_PRE[KIND_G] + 16 * (e + 3), (gate_ps, 2 * e + 4))
                    split_expert(KIND_D, RAW_PRE[KIND_D] + 16 * (e + 2), (dn_ps, 8 * e + 8))

            expert_act(0)
            with act.Fori(1, full) as e:
                expert_act(e)
            expert_act(rest[0], gates=False)
            expert_act(rest[1], last=True)
            act.wait_ge(yacc, 8 * NE)
            for t in range(TT):
                if t:
                    act.wait_ge(ssq3, t)
                act.activation(junk_f[:, :], y[:, t, :], ACT.Square, accum_out=ssq[:, t:t + 1]).then_inc(ssq3, 1)

        @block.vector
        def _(dve):
            n = [0]

            def link(ins):
                n[0] += 1
                ins.then_inc(dve_step, 1)
                dve.wait_ge(dve_step, n[0])

            def split_lo(u):
                s = u % RING
                dve.wait_ge(hi_done, u + 1)
                dve.tensor_tensor(wlo[s][:, :], raw[s][:, :], whi[s][:, :].bitcast(F32), ALU.subtract).then_inc(lo_done, 1)

            dve.memset(epsb[:, :], EPS).then_inc(eps_set, 1)
            for t in range(TT):
                dve.wait_ge(ssq_done, t + 1)
                link(dve.reciprocal(rst[:, t:t + 1], rst[:, t:t + 1]))
                dve.tensor_scalar(x[:, t, :], x[:, t, :], rst[:, t:t + 1], None, ALU.mult).then_inc(x_scaled, 1)
            dve.wait_ge(rows_ps, 1)
            dve.tensor_copy(cols[:, :], ps[7][:, 0:57]).then_inc(cols_done, 1)
            dve.wait_ge(rw_hi_done, 1)
            dve.tensor_tensor(rw_lo[:, :, :], rw_raw[:, :, :], rw_hi[:, :, :].bitcast(F32), ALU.subtract).then_inc(rw_lo_done, 1)
            for i in range(EG):
                dve.memset(prio[:, i:i + 1], float(EG - i))
            dve.wait_ge(ba_hi_done, 1)
            dve.tensor_tensor(ba_lo[:, :, :], ba_raw[:, :, :], ba_hi[:, :, :].bitcast(F32), ALU.subtract).then_inc(ba_lo_done, 1)
            split_lo(0)
            split_lo(1)
            dve.wait_ge(cols_done, 1)
            for k in range(KT):
                dve.wait_ge(ht_hi, k + 1)
                dve.scalar_tensor_tensor(h_lo[:, k, :], ps[k % 2][:, :], cols[:, k:k + 1],
                                         h_hi[:, k, :].bitcast(F32), ALU.mult, ALU.subtract).then_inc(ht_lo, 1)
            for i in range(2):
                dve.memset(xpad[i][:, 0:3], 0.0).then_inc(pad_zero, 1)

            def tap(j, i):
                c = KT + j * CONV_ITEMS + i
                return cols[:, c:c + 1]

            def conv(i):
                b = i % 2
                dve.wait_ge(proj_evac, i + 1)
                if i >= 2:
                    dve.wait_ge(silu_done, i - 1)
                link(dve.tensor_scalar(cacc[b][:, :], xpad[b][:, 0:S], tap(0, i), None, ALU.mult))
                for j in range(1, TAPS):
                    ins = dve.scalar_tensor_tensor(cacc[b][:, :], xpad[b][:, j:j + S], tap(j, i), cacc[b][:, :],
                                                   ALU.mult, ALU.add)
                    if j < TAPS - 1:
                        link(ins)
                    else:
                        ins.then_inc(conv_done, 1)

            def l2_norm(i):
                dve.wait_ge(root_done, i + 1)
                r = rsb[i % 2][:, :]
                link(dve.reciprocal(r, r))
                dve.scalar_tensor_tensor(fm[:, i, :], fm[:, i, :], float(DA) ** -0.5 if i < HA else 1.0, r,
                                         ALU.mult, ALU.mult).then_inc(norm_done, 1)

            for i in range(ITEMS):
                if i % 2 == 0 and i // 2 + 2 < UNITS_PROJ:
                    split_lo(i // 2 + 2)
                if i < CONV_ITEMS:
                    conv(i)
                for j in norms_at(i):
                    l2_norm(j)
                if i == 0:
                    dve.wait_ge(ba_ps, 1)
                    dve.tensor_copy(ba_t[:, :, :], ps[4][:, 0:32].rearrange("p (t c) -> p t c", t=TT)).then_inc(ba_copied, 1)
            dve.wait_ge(ba_copied, 1)
            for t in range(TT):
                ins = dve.tensor_tensor(ga1[:, t, :], ba_t[:, t, HA:], dtb[:, :], ALU.add)
            link(ins)
            dve.scalar_tensor_tensor(ga2[:, :, :], ga1[:, :, :], -1.0, ga1[:, :, :], ALU.mult, ALU.max).then_inc(gd_abs, 1)
            dve.wait_ge(gd_ln, 1)
            link(dve.scalar_tensor_tensor(ga3[:, :, :], ga1[:, :, :], 0.0, ga2[:, :, :], ALU.max, ALU.add))
            dve.wait_ge(gd_exp, 1)
            for t in range(TT):
                ins = dve.scalar_tensor_tensor(gdt[:, t, :], ga3[:, t, :], -1.0, ealog[:, :], ALU.mult, ALU.mult)
            ins.then_inc(gates_done, 1)


            dve.wait_ge(dist_set, 1)
            link(dve.tensor_copy(dist[:, :], dist_i[:, :]))
            link(dve.scalar_tensor_tensor(dist_m[:, :], dist[:, :], -1.0, dist[:, :], ALU.mult, ALU.max))
            for h in range(HB):
                slope = 2.0 ** (-8.0 * (h + 1) / HB)
                dve.scalar_tensor_tensor(bias[:, h, :], dist_m[:, :], -slope, wmask[:, :], ALU.mult, ALU.add)
            link(dve.memset(pb[:, :, 0:CHUNK], 0.0))
            for a_ in range(2 * TT):
                m, g = a_ // 2, a_ % 2
                c0 = CHUNK if m else P
                heads = slice(GRP * g, GRP * (g + 1))
                dve.wait_ge(sc_ps, a_ + 1)
                if a_:
                    dve.wait_ge(pt_ps, 2 * a_)
                for b in range(2):
                    bank = ps[b][:, :].rearrange("p (h c) -> p h c", h=2)
                    hs = GRP * g + 2 * b
                    ins = dve.scalar_tensor_tensor(pb[:, 2 * b:2 * b + 2, c0:], bank[:, :, c0:], DB ** -0.5,
                                                   bias[:, hs:hs + 2, c0 - CHUNK:], ALU.mult, ALU.add)
                link(ins)
                link(dve.tensor_reduce(mxs[:, :], pb[:, :, c0:], AX.X, ALU.max))
                link(dve.tensor_tensor(mxs[:, :], mxs[:, :], sinkb[:, heads], ALU.max))
                dve.tensor_scalar(nmx[:, :], mxs[:, :], -1.0, None, ALU.mult)
                dve.tensor_tensor(esk[:, :], sinkb[:, heads], mxs[:, :], ALU.subtract).then_inc(max_done, 1)
                dve.wait_ge(pt_ps, 2 * a_ + 2)
                if a_:
                    dve.wait_ge(pv_ps, a_)
                dve.tensor_copy(pt[:, 1, :, :], bank4(3)).then_inc(pt_cur, 1)
                dve.wait_ge(exp_done, a_ + 1)
                link(dve.tensor_tensor(den[:, :], sms[:, :], esk[:, :], ALU.add))
                link(dve.reciprocal(den[:, :], den[:, :]))
                dve.wait_ge(pv_ps, a_ + 1)
                if g == 0 and m:
                    dve.wait_ge(obt_ps, m)
                ins = dve.tensor_tensor(ob_t[:, heads, :], ps[4][:, 0:GRP * DB].rearrange("p (h c) -> p h c", h=GRP),
                                        bc_last(den[:, :], DB), ALU.mult)
                ins.then_inc(ob_ready, 1)
                if g == 1:
                    dve.wait_ge(ob_hi_done, m + 1)
                    ts = slice(m * P, (m + 1) * P)
                    dve.tensor_tensor(ob_lo[:, :, ts], bank4(5), ob_hi[:, :, ts].bitcast(F32), ALU.subtract).then_inc(ob_lo_done, 1)

            def rsqrt(v, y):
                w = y.shape[1]
                i, t = rsq_i[:, 0:w], rsq_t[:, 0:w]
                link(dve.tensor_scalar(i, v.bitcast(mybir.dt.int32), 1, None, ALU.arith_shift_right))
                link(dve.tensor_scalar(y.bitcast(mybir.dt.int32), i, -1.0, float(0x5F3759DF), ALU.mult, ALU.add))
                for _ in range(4):
                    link(dve.tensor_tensor(t, y, y, ALU.mult))
                    link(dve.scalar_tensor_tensor(t, t, -0.5, v, ALU.mult, ALU.mult))
                    link(dve.scalar_tensor_tensor(y, t, 1.5, y, ALU.add, ALU.mult))

            dve.wait_ge(gsum_ps, 1)
            dve.tensor_copy(gsum[:, 3, :], ps[6][:, 48:64])
            link(dve.tensor_copy(gsum[:, 0:3, :], ps[5][:, 0:48].rearrange("p (a c) -> p a c", a=3)))
            dve.tensor_tensor(gsum[:, 1, :], gsum[:, 1, :], gsum[:, 0, :], ALU.subtract).then_inc(gsum_sub, 1)
            dve.wait_ge(gexp_done, 1)
            link(dve.tensor_tensor(bexp[:, :, :], bta[:, :, :], gexp[:, :, :], ALU.mult))
            dve.memset(d_s[:, :, :], 0.0).then_inc(s_zero, 1)
            gT = gsum[:, 0, :].rearrange("p (t h) -> p t h", t=TT)
            for m in range(TT):
                ts = slice(m * P, (m + 1) * P)
                if m:
                    dve.wait_ge(oat_ps, m)
                dve.tensor_tensor(d_x[:, :, :], bc_mid(tri[:, :], HA), bc_last(gdt[:, m, :], P), ALU.mult).then_inc(rb_ready, 1)
                dve.tensor_tensor(d_c[:, :, :], bc_mid(ident[:, :], HA), bc_last(bta[:, m, :], P), ALU.mult).then_inc(rb_ready, 1)
                dve.wait_ge(rb_ps, 2 * m + 1)
                for h in range(HA):
                    ins = dve.scalar_tensor_tensor(d_dec[:, h, :], bank4(2)[:, h, :], gT[:, m, h:h + 1], negm[:, :],
                                                   ALU.subtract, ALU.add)
                ins.then_inc(dec_in, 1)
                dve.wait_ge(kk_ps, 2 * m + 1)
                dve.wait_ge(dec_done, m + 1)
                if m:
                    dve.wait_ge(oa_hi_done, m)
                    dve.wait_ge(oa_lo_done, m)
                link(dve.tensor_tensor(d_lt[:, :, :], bank4(4), d_dec[:, :, :], ALU.mult))
                dve.wait_ge(rb_ps, 2 * m + 2)
                link(dve.tensor_tensor(d_lt[:, :, :], d_lt[:, :, :], bank4(3), ALU.mult))
                link(dve.tensor_tensor(d_x[:, :, :], d_lt[:, :, :], bc_mid(lvl[:, 0, :], HA), ALU.mult))
                dve.tensor_tensor(d_invT[:, :, :], bc_mid(ident[:, :], HA), d_x[:, :, :], ALU.subtract).then_inc(inv0, 1)
                dve.wait_ge(kk_ps, 2 * m + 2)
                dve.tensor_tensor(d_kq[:, :, :], bank4(5), d_dec[:, :, :], ALU.mult)
                dve.wait_ge(egb_done, m + 1)
                dve.tensor_tensor(d_qd[:, :, :], fm[:, 0:HA, ts], d_qd[:, :, :], ALU.mult).then_inc(qd_done, 1)
                dve.wait_ge(kv_ps, 2 * m + 1)
                dve.tensor_tensor(d_k[:, :, :], bank4(6), bc_last(bexp[:, m, :], P), ALU.mult)
                dve.tensor_tensor(d_kd[:, :, :], bank4(6), bc_last(kds[:, m, :], P), ALU.mult)
                dve.wait_ge(kv_ps, 2 * m + 2)
                dve.tensor_tensor(d_v[:, :, :], bank4(7), bc_last(bta[:, m, :], P), ALU.mult).then_inc(kbv_done, 1)
                dve.wait_ge(inv0, m + 1)
                dve.wait_ge(inv0_copied, m + 1)
                for l in range(1, 6):
                    if l > 1:
                        dve.wait_ge(x_ps, 5 * m + l - 1)
                    dve.tensor_tensor(d_c[:, :, :], d_lt[:, :, :], bc_mid(lvl[:, l, :], HA), ALU.mult).then_inc(ct_done, 1)
                    dve.wait_ge(de_ps, 5 * m + l)
                    if l < 5:
                        dve.tensor_tensor(d_inv[:, :, :], d_inv[:, :, :], bank4(3), ALU.subtract)
                    dve.tensor_tensor(d_invT[:, :, :], d_invT[:, :, :], bank4(4), ALU.subtract).then_inc(de_done, 1)
                    dve.wait_ge(de_done, 5 * m + l)
                dve.wait_ge(wu_done, m + 1)
                for c in range(2):
                    r = slice(CHUNK * c, CHUNK * (c + 1))
                    j = 2 * m + c
                    dve.wait_ge(ws_ps, j + 1)
                    dve.tensor_tensor(d_x[r, :, :], d_v[r, :, :], bank4(2)[r, :, :], ALU.subtract).then_inc(vn_done, 1)
                    dve.wait_ge(ds_ps, j + 1)
                    for h in range(HA):
                        ins = dve.scalar_tensor_tensor(d_s[:, h, :], d_s[:, h, :], cdec[:, c, m, h:h + 1], bank4(3)[:, h, :],
                                                       ALU.mult, ALU.add)
                    ins.then_inc(s_done, 1)
                dve.wait_ge(o_ps, m + 1)
                link(dve.tensor_copy(d_c[:, :, :], bank4(7)))
                link(dve.tensor_tensor(d_dec[:, :, :], d_c[:, :, :], d_c[:, :, :], ALU.mult))
                link(dve.tensor_reduce(osq[:, :], d_dec[:, :, :], AX.X, ALU.add))
                link(dve.tensor_scalar(osq[:, :], osq[:, :], 1.0 / DA, EPS, ALU.mult, ALU.add))
                rsqrt(osq[:, :], ors[:, :])
                dve.tensor_tensor(d_c[:, :, :], d_c[:, :, :], bc_last(ors[:, :], P), ALU.mult).then_inc(on_done, 1)
                dve.wait_ge(oat_ps, m + 1)
                dve.scalar_tensor_tensor(d_lt[:, :, :], bank4(4), cols[:, 56:57], fm[:, 12:16, ts],
                                         ALU.mult, ALU.mult).then_inc(oaf_done, 1)
                dve.wait_ge(oa_hi_done, m + 1)
                dve.tensor_tensor(oa_lo[:, :, ts], d_lt[:, :, :], oa_hi[:, :, ts].bitcast(F32), ALU.subtract).then_inc(oa_lo_done, 1)

            for u in range(UNITS_PROJ, UNITS_PROJ + 2):
                split_lo(u)
            for j in range(4):
                split_lo(UNITS_PROJ + 2 + 3 * j)
                split_lo(UNITS_PROJ + 3 + 3 * j)
                for r in range(4):
                    h = r % 2
                    dve.wait_ge(mg_ps, 8 * j + 4 + r + 1)
                    dve.wait_ge(sg_done, 4 * j + r + 1)
                    if r < 2:
                        dve.tensor_tensor(prod[:, h, :], sg[:, r, :], ps[4 + r][:, :], ALU.mult).then_inc(mul_done, 1)
                    else:
                        if j:
                            dve.wait_ge(mg_hi, 2 * j)
                        link(dve.tensor_tensor(mrg[:, h, :], sg[:, r, :], ps[4 + r][:, :], ALU.mult))
                        dve.wait_ge(mul_done, 4 * j + h + 1)
                        dve.tensor_tensor(mrg[:, h, :], mrg[:, h, :], prod[:, h, :], ALU.add).then_inc(mul_done, 1)
                for r in range(2):
                    dve.wait_ge(mg_hi, 2 * j + r + 1)
                    dve.tensor_tensor(m_lo[:, 2 * j + r, :], mrg[:, r, :], m_hi[:, 2 * j + r, :].bitcast(F32),
                                      ALU.subtract).then_inc(mg_lo, 1)
                split_lo(UNITS_PROJ + 4 + 3 * j)
            for u in range(UNITS_PRE - 2, UNITS_PRE):
                split_lo(u)
            dve.wait_ge(x2_in, 16)
            for n_ in range(2):
                dve.wait_ge(out_used, 2 * n_ + 2)
                for t in range(TT):
                    o = y[:, t, 512 * n_:512 * (n_ + 1)]
                    dve.tensor_tensor(o, o, ps[4 * n_ + t][:, :], ALU.add).then_inc(y_done, 1)

            def token_rms(done):
                dve.wait_ge(done, TT)
                link(dve.tensor_scalar(ssq[:, :], ssq[:, :], 1.0 / D, EPS, ALU.mult, ALU.add))
                rsqrt(ssq[:, :], rst[:, :])

            def split_lo_expert(slot, split):
                dve.wait_ge(hi_done, split)
                dve.tensor_tensor(wlo[slot][:, :], raw[slot][:, :], whi[slot][:, :].bitcast(F32), ALU.subtract).then_inc(lo_done, 1)

            token_rms(ssq2)
            for t in range(TT):
                dve.tensor_scalar(tx[:, t, :], y[:, t, :], rst[:, t:t + 1], None, ALU.mult).then_inc(t_scaled, 1)
            split_lo_expert(KIND_G, UNITS_PRE + 1)
            split_lo_expert(KIND_U, UNITS_PRE + 2)
            for k in range(KT):
                dve.wait_ge(tt_hi, k + 1)
                dve.scalar_tensor_tensor(h_lo[:, k, :], ps[k % 2][:, :], nffn[:, k:k + 1],
                                         h_hi[:, k, :].bitcast(F32), ALU.mult, ALU.subtract).then_inc(tt_lo, 1)

            def one_hot(oh, v, vmax, key):
                link(dve.tensor_tensor(key, v, bc_last(vmax, EG), ALU.is_equal))
                link(dve.tensor_tensor(key, key, bc_mid(prio[:, :], TT), ALU.mult))
                link(dve.tensor_reduce(kmx[:, :], key, AX.X, ALU.max))
                link(dve.tensor_tensor(oh, key, bc_last(kmx[:, :], EG), ALU.is_equal))

            dve.wait_ge(lg_ps, 1)
            link(dve.tensor_tensor(lg[:, :, :], ps[2][:, 0:TT * (NG + NE)].rearrange("p (t c) -> p t c", t=TT),
                                   bc_mid(brg[:, :], TT), ALU.add))
            gl = lg[:, :, 0:NG]
            link(dve.tensor_reduce(gmx[:, :], gl, AX.X, ALU.max))
            dve.tensor_tensor(gex[:, :, :], gl, bc_last(gmx[:, :], NG), ALU.subtract).then_inc(gd_in, 1)
            one_hot(goh[:, :, :], gl, gmx[:, :], gkey[:, :, :])
            for t in range(TT):
                ins = dve.tensor_tensor(eprod[:, NG * t:NG * (t + 1), :], lg[:, t, NG:].rearrange("p (g e) -> p g e", g=NG),
                                        bc_last(goh[:, t, :], EG), ALU.mult)
            link(ins)
            link(dve.tensor_reduce(ig[:, :, :], eprod[:, :, :].rearrange("p (t g) e -> p t e g", t=TT), AX.X, ALU.add))
            link(dve.tensor_reduce(m1[:, :], ig[:, :, :], AX.X, ALU.max))
            one_hot(e1[:, :, :], ig[:, :, :], m1[:, :], ekey[:, :, :])
            link(dve.scalar_tensor_tensor(ig[:, :, :], e1[:, :, :], NEG, ig[:, :, :], ALU.mult, ALU.add))
            link(dve.tensor_reduce(m2[:, :], ig[:, :, :], AX.X, ALU.max))
            dve.tensor_tensor(dif[:, :], m2[:, :], m1[:, :], ALU.subtract).then_inc(ed_in, 1)
            one_hot(e2[:, :, :], ig[:, :, :], m2[:, :], ekey[:, :, :])
            dve.wait_ge(gd_out, 1)
            link(dve.tensor_reduce(gsm[:, :], gex[:, :, :], AX.X, ALU.add))
            link(dve.reciprocal(gp[:, :], gsm[:, :]))
            dve.wait_ge(ed_out, 1)
            link(dve.tensor_scalar(w1[:, :], dif[:, :], 1.0, None, ALU.add))
            link(dve.reciprocal(w1[:, :], w1[:, :]))
            link(dve.tensor_tensor(w1[:, :], w1[:, :], gp[:, :], ALU.mult))
            link(dve.tensor_tensor(w2[:, :], w1[:, :], dif[:, :], ALU.mult))
            link(dve.tensor_tensor(ce[:, :, :], e1[:, :, :], bc_last(w1[:, :], EG), ALU.mult))
            link(dve.tensor_tensor(ce2[:, :, :], e2[:, :, :], bc_last(w2[:, :], EG), ALU.mult))
            link(dve.tensor_tensor(ce[:, :, :], ce[:, :, :], ce2[:, :, :], ALU.add))
            for t in range(TT):
                ins = dve.tensor_tensor(comb[:, t, :].rearrange("p (g e) -> p g e", g=NG), bc_last(goh[:, t, :], EG),
                                        bc_mid(ce[:, t, :], NG), ALU.mult)
            ins.then_inc(comb_done, 1)
            dve.wait_ge(comb_done, 1)

            split_lo_expert(KIND_G, UNITS_PRE + 3)
            split_lo_expert(KIND_D, UNITS_PRE + 4)

            def expert_dve(e, gates=True, last=False):
                if not is_first(e):
                    dve.wait_ge(yacc, 8 * e)
                dve.tensor_copy(cwe[:, :], comb[:, :, bass.ds(e, 1)].rearrange("p t o -> p (t o)")).then_inc(cwe_done, 1)
                for f in range(2):
                    dve.wait_ge(gsilu, 2 * e + f + 1)
                    dve.wait_ge(up_ps, 2 * e + f + 1)
                    dve.tensor_tensor(ea[:, f, :], eg[:, f, :], ps[2 + f][:, :], ALU.mult).then_inc(hid_done, 1)
                for f in range(2):
                    dve.wait_ge(hid_hi, 2 * e + f + 1)
                    dve.tensor_tensor(ea_lo[:, f, :], ea[:, f, :], ea_hi[:, f, :].bitcast(F32), ALU.subtract).then_inc(hid_lo, 1)
                if not last:
                    split_lo_expert(KIND_U, up_at(e + 1))
                dve.wait_ge(cwe_done, e + 1)
                for q in range(8):
                    if q == 2 and gates and not last:
                        split_lo_expert(KIND_G, gate_at(e + 2))
                    t, n_ = divmod(q, 2)
                    dve.wait_ge(dn_ps, 8 * e + q + 1)
                    o = y[:, t, 512 * n_:512 * (n_ + 1)]
                    dve.scalar_tensor_tensor(o, ps[4 + q % 4][:, :], cwe[:, t:t + 1], o, ALU.mult, ALU.add).then_inc(yacc, 1)
                if not last:
                    split_lo_expert(KIND_D, down_at(e + 1))

            expert_dve(0)
            with dve.Fori(1, full) as e:
                expert_dve(e)
            expert_dve(rest[0], gates=False)
            expert_dve(rest[1], last=True)
            token_rms(ssq3)
            dve.wait_ge(nfin_in, 16)
            for t in range(TT):
                dve.scalar_tensor_tensor(tx[:, t, :], y[:, t, :], rst[:, t:t + 1], nfin[:, :],
                                         ALU.mult, ALU.mult).then_inc(fin_done, 1)

        @block.tensor
        def _(pe):
            def three(out_ap, lhs_hi, lhs_lo, rhs_hi, rhs_lo, first, last):
                pe.matmul(out_ap, lhs_hi, rhs_hi, start=first, stop=False)
                pe.matmul(out_ap, lhs_hi, rhs_lo, start=False, stop=False)
                return pe.matmul(out_ap, lhs_lo, rhs_hi, start=False, stop=last)

            pe.wait_ge(consts, 1)
            pe.wait_ge(small_in, 192)
            pe.transpose(ps[7][:, 0:57], rows[:, :], ident[0:57, 0:57]).then_inc(rows_ps, 1)
            for k in range(KT):
                if k >= 2:
                    pe.wait_ge(ht_lo, k - 1)
                for t in range(TT):
                    pe.wait_ge(x_scaled, t + 1)
                    ins = pe.transpose(ps[k % 2][:, t * P:(t + 1) * P], x[:, t, k * P:(k + 1) * P], ident[:, :])
                ins.then_inc(ht_ps, 1)
            pe.wait_ge(ht_lo, KT)
            pe.wait_ge(ba_lo_done, 1)
            for t in range(TT):
                ts = slice(t * P, (t + 1) * P)
                for k in range(KT):
                    ins = three(ps[4][:, 8 * t:8 * t + 8], h_hi[:, k, ts], h_lo[:, k, ts],
                                ba_hi[:, k, :], ba_lo[:, k, :], k == 0, k == KT - 1)
            ins.then_inc(ba_ps, 1)

            def sum_squares(i):
                pe.wait_ge(sq_done, i + 1)
                if i >= 2:
                    pe.wait_ge(root_done, i - 1)
                pe.matmul(ps[2 + i % 2][:, :], ones[:, :], sqb[i % 2][:, :], start=True, stop=True).then_inc(norm_ps, 1)

            for i in range(ITEMS):
                u, half = i // 2, i % 2
                hi = whi[u % RING][:, :].rearrange("p (k n) -> p k n", k=KT)
                lo = wlo[u % RING][:, :].rearrange("p (k n) -> p k n", k=KT)
                pe.wait_ge(lo_done, u + 1)
                if i >= 2:
                    pe.wait_ge(proj_evac, i - 1)
                bank = ps[i % 2]
                if i == ITEMS - 1:
                    for t in range(TT):
                        ts = slice(t * P, (t + 1) * P)
                        for k in range(KT):
                            ins = three(bank[:, ts], h_hi[:, k, ts], h_lo[:, k, ts],
                                        hi[:, k, 128:256], lo[:, k, 128:256], k == 0, k == KT - 1)
                else:
                    for k in range(KT):
                        wh, wl = (w[:, k, 128 * half:128 * half + 128] for w in (hi, lo))
                        ins = three(bank[:, :], wh, wl, h_hi[:, k, :], h_lo[:, k, :], k == 0, k == KT - 1)
                ins.then_inc(proj_ps, 1)
                for j in norms_at(i):
                    sum_squares(j)


            pe.wait_ge(proj_evac, ITEMS)
            for a_ in range(2 * TT):
                m, g = a_ // 2, a_ % 2
                d = slice(DB * g, DB * (g + 1))
                c0 = CHUNK if m else P
                if a_:
                    pe.wait_ge(max_done, a_)
                for h in range(GRP):
                    o = ps[h // 2][:, 256 * (h % 2) + c0:256 * (h % 2) + 256]
                    ins = pe.matmul(o, qb[d, h, m * P:(m + 1) * P], kb[d, m * P - P + c0:(m + 1) * P],
                                    start=True, stop=True)
                ins.then_inc(sc_ps, 1)
                pe.wait_ge(exp_done, a_ + 1)
                for half in range(2):
                    if half == 1 or m:
                        if a_ > 2 and half == 0:
                            pe.wait_ge(pt_prev, a_ - 2)
                        if a_ and half == 1:
                            pe.wait_ge(pt_cur, a_)
                        for h in range(GRP):
                            ins = pe.transpose(bank4(2 + half)[:, h, :], pb[:, h, half * P:(half + 1) * P], ident[:, :])
                        ins.then_inc(pt_ps, 1 if m else 2)
                if m:
                    pe.wait_ge(pt_prev, a_ - 1)
                pe.wait_ge(pt_cur, a_ + 1)
                if a_:
                    pe.wait_ge(ob_ready, a_)
                for h in range(GRP):
                    o = ps[4][:, DB * h:DB * (h + 1)]
                    if m:
                        pe.matmul(o, pt[:, 0, h, :], vb[:, m - 1, d], start=True, stop=False)
                    ins = pe.matmul(o, pt[:, 1, h, :], vb[:, m, d], start=not m, stop=True)
                ins.then_inc(pv_ps, 1)
                if g == 1:
                    pe.wait_ge(ob_ready, a_ + 1)
                    if m:
                        pe.wait_ge(ob_lo_done, m)
                    for k in range(4):
                        ins = pe.transpose(bank4(5)[:, k, :], ob_t[:, 2 * k:2 * k + 2, :], ident[:, :])
                    ins.then_inc(obt_ps, 1)

            pe.wait_ge(gates_done, 2)
            pe.wait_ge(norm_done, NORM_ITEMS)
            pe.wait_ge(ob_lo_done, TT)
            g_all = gdt[:, :, :].rearrange("p t h -> p (t h)")
            pe.matmul(ps[5][:, 0:16], tri[:, :], g_all, start=True, stop=True)
            pe.matmul(ps[5][:, 16:32], blk[:, :], g_all, start=True, stop=True)
            for c in range(2):
                r = slice(CHUNK * c, CHUNK * (c + 1))
                o = ps[5 + c][:, 32 + 16 * c:48 + 16 * c]
                ins = pe.matmul(o, ones[r, :],
                                gdt[r, :, :].rearrange("p t h -> p (t h)"), start=True, stop=True)
            ins.then_inc(gsum_ps, 1)
            pe.wait_ge(gsum_sub, 1)
            for m in range(TT):
                ts = slice(m * P, (m + 1) * P)
                pe.wait_ge(rb_ready, 2 * m + 1)
                pe.matmul(ps[2][:, :], ones[:, :], d_x[:, :, :], start=True, stop=True).then_inc(rb_ps, 1)
                pe.wait_ge(rb_ready, 2 * m + 2)
                if m:
                    pe.wait_ge(s_done, 2 * m)
                pe.matmul(ps[3][:, :], ones[:, :], d_c[:, :, :], start=True, stop=True).then_inc(rb_ps, 1)
                if m:
                    pe.wait_ge(oaf_done, m)
                for h in range(HA):
                    ins = pe.matmul(bank4(4)[:, h, :], fm[:, HA + h, ts], fm[:, HA + h, ts], start=True, stop=True)
                ins.then_inc(kk_ps, 1)
                for h in range(HA):
                    ins = pe.matmul(bank4(5)[:, h, :], fm[:, HA + h, ts], fm[:, h, ts], start=True, stop=True)
                ins.then_inc(kk_ps, 1)
                for w in range(2):
                    if w and m:
                        pe.wait_ge(on_done, m)
                    for h in range(HA):
                        ins = pe.transpose(bank4(6 + w)[:, h, :], fm[:, HA * (w + 1) + h, ts], ident[:, :])
                    ins.then_inc(kv_ps, 1)
                pe.wait_ge(inv0, m + 1)
                for h in range(HA):
                    ins = pe.transpose(bank4(2)[:, h, :], d_invT[:, h, :], ident[:, :])
                ins.then_inc(inv0_ps, 1)
                pe.wait_ge(inv0_copied, m + 1)
                for l in range(1, 6):
                    if l > 1:
                        pe.wait_ge(de_done, 5 * m + l - 1)
                    pe.wait_ge(ct_done, 5 * m + l)
                    for h in range(HA):
                        ins = pe.matmul(bank4(2)[:, h, :], d_c[:, h, :], d_inv[:, h, :], start=True, stop=True)
                    ins.then_inc(x_ps, 1)
                    pe.wait_ge(xs_done, 5 * m + l)
                    if l < 5:
                        for h in range(HA):
                            pe.matmul(bank4(3)[:, h, :], d_invT[:, h, :], d_x[:, h, :], start=True, stop=True)
                    for h in range(HA):
                        ins = pe.matmul(bank4(4)[:, h, :], d_x[:, h, :], d_invT[:, h, :], start=True, stop=True)
                    ins.then_inc(de_ps, 1)
                pe.wait_ge(de_done, 5 * m + 5)
                pe.wait_ge(kbv_done, m + 1)
                pe.wait_ge(qd_done, m + 1)
                for h in range(HA):
                    pe.matmul(bank4(5)[:, h, :], d_k[:, h, :], d_invT[:, h, :], start=True, stop=True)
                for h in range(HA):
                    ins = pe.matmul(bank4(6)[:, h, :], d_invT[:, h, :], d_v[:, h, :], start=True, stop=True)
                ins.then_inc(wu_ps, 1)
                pe.wait_ge(wu_done, m + 1)
                for c in range(2):
                    r = slice(CHUNK * c, CHUNK * (c + 1))
                    j = 2 * m + c
                    pe.wait_ge(s_zero, 1)
                    if j:
                        pe.wait_ge(s_done, j)
                    for h in range(HA):
                        ins = pe.matmul(bank4(2)[r, h, :], d_k[:, h, r], d_s[:, h, :], start=True, stop=True)
                    ins.then_inc(ws_ps, 1)
                    pe.wait_ge(vn_done, j + 1)
                    for h in range(HA):
                        pe.matmul(bank4(7)[r, h, :], d_qd[:, h, r], d_s[:, h, :], start=True, stop=False)
                        ins = pe.matmul(bank4(7)[r, h, :], d_kq[r, h, r], d_x[r, h, :], start=False, stop=True)
                    if c == 1:
                        ins.then_inc(o_ps, 1)
                    for h in range(HA):
                        ins = pe.matmul(bank4(3)[:, h, :], d_kd[r, h, :], d_x[r, h, :], start=True, stop=True)
                    ins.then_inc(ds_ps, 1)
                pe.wait_ge(on_done, m + 1)
                for h in range(HA):
                    ins = pe.transpose(bank4(4)[:, h, :], d_c[:, h, :], ident[:, :])
                ins.then_inc(oat_ps, 1)


            for j in range(4):
                for r in range(8):
                    c, half = min(r // 2, 2), r % 2
                    u = UNITS_PROJ + 3 * j + c
                    hi, lo = kv_(whi[u % RING]), kv_(wlo[u % RING])
                    cs = slice(128 * half, 128 * half + 128)
                    pe.wait_ge(lo_done, u + 1)
                    if j:
                        pe.wait_ge(sg_done if r < 4 else mul_done, 4 * (j - 1) + r % 4 + 1)
                    if r < 4:
                        for k in range(KT):
                            ins = three(ps[r][:, :], hi[:, k, cs], lo[:, k, cs], h_hi[:, k, :], h_lo[:, k, :],
                                        k == 0, k == KT - 1)
                    else:
                        xh, xl = (oa_hi, oa_lo) if r < 6 else (ob_hi, ob_lo)
                        if j == 0:
                            pe.wait_ge(oa_lo_done, TT)
                        for k in range(4):
                            kk = k + (0 if r < 6 else 4)
                            ins = three(ps[r][:, :], hi[:, kk, cs], lo[:, kk, cs], xh[:, k, :], xl[:, k, :], k == 0, k == 3)
                    ins.then_inc(mg_ps, 1)
            pe.wait_ge(mg_lo, KT)
            for n_ in range(2):
                for kh in range(2):
                    u = UNITS_PROJ + UNITS_MERGE + 2 * n_ + kh
                    hi, lo = (w[u % RING][:, :].rearrange("p (k n) -> p k n", k=4) for w in (whi, wlo))
                    pe.wait_ge(lo_done, u + 1)
                    if kh == 0:
                        pe.wait_ge(mul_done if n_ else sg_done, 16)
                    for t in range(TT):
                        ts = slice(t * P, (t + 1) * P)
                        for k in range(4):
                            kk = 4 * kh + k
                            ins = three(ps[4 * n_ + t][:, :], m_hi[:, kk, ts], m_lo[:, kk, ts], hi[:, k, :], lo[:, k, :],
                                        kk == 0, kk == KT - 1)
                    ins.then_inc(out_used, 1)
            pe.wait_ge(y_done, 8)
            for k in range(KT):
                if k >= 2:
                    pe.wait_ge(tt_lo, k - 1)
                for t in range(TT):
                    pe.wait_ge(t_scaled, t + 1)
                    ins = pe.transpose(ps[k % 2][:, t * P:(t + 1) * P],
                                       tx[:, t, :].rearrange("p (c k) -> p k c", k=KT)[:, k, :], ident[:, :])
                ins.then_inc(tt_ps, 1)
            pe.wait_ge(tt_lo, KT)
            pe.wait_ge(rw_lo_done, 1)
            for t in range(TT):
                ts = slice(t * P, (t + 1) * P)
                for k in range(KT):
                    ins = three(ps[2][:, (NG + NE) * t:(NG + NE) * (t + 1)], h_hi[:, k, ts], h_lo[:, k, ts],
                                rw_hi[:, k, :], rw_lo[:, k, :], k == 0, k == KT - 1)
            ins.then_inc(lg_ps, 1)

            def into_hidden(slot, bank, done):
                hi, lo = kv_(whi[slot]), kv_(wlo[slot])
                for f in range(2):
                    fs = slice(P * f, P * (f + 1))
                    for k in range(KT):
                        ins = three(ps[bank + f][:, :], hi[:, k, fs], lo[:, k, fs], h_hi[:, k, :], h_lo[:, k, :],
                                    k == 0, k == KT - 1)
                    ins.then_inc(done, 1)

            pe.wait_ge(lo_done, UNITS_PRE + 1)
            into_hidden(KIND_G, 0, gate_ps)
            pe.wait_ge(comb_done, 1)

            def expert_pe(e, last=False):
                pe.wait_ge(lo_done, up_at(e))
                if not is_first(e):
                    pe.wait_ge(hid_done, 2 * e)
                into_hidden(KIND_U, 2, up_ps)
                if not last:
                    pe.wait_ge(lo_done, gate_at(e + 1))
                    pe.wait_ge(gsilu, 2 * e + 2)
                    into_hidden(KIND_G, 0, gate_ps)
                pe.wait_ge(lo_done, down_at(e))
                pe.wait_ge(hid_lo, 2 * e + 2)
                hi, lo = fd_(whi[KIND_D]), fd_(wlo[KIND_D])
                for q in range(8):
                    t, n_ = divmod(q, 2)
                    ts, ns = slice(t * P, (t + 1) * P), slice(512 * n_, 512 * (n_ + 1))
                    if not is_first(e) or q > 3:
                        pe.wait_ge(yacc, 8 * e + max(q - 3, 0))
                    for f in range(2):
                        ins = three(ps[4 + q % 4][:, :], ea_hi[:, f, ts], ea_lo[:, f, ts], hi[:, f, ns], lo[:, f, ns],
                                    f == 0, f == 1)
                    ins.then_inc(dn_ps, 1)

            expert_pe(0)
            with pe.Fori(1, full) as e:
                expert_pe(e)
            expert_pe(rest[0])
            expert_pe(rest[1], last=True)


_INS = ["x", "norm_mix_w", "w_in", "conv_w", "a_log", "dt_bias", "delta_norm_w", "sinks", "w_out_a", "w_out_b",
        "w_out", "norm_ffn_w", "w_router_group", "b_router_group", "w_router_expert", "b_router_expert",
        "w_gate", "w_up", "w_down", "norm_final_w"]


def kernel(**inputs):
    import concourse.bacc as bacc
    from concourse.bass_utils import run_bass_kernel_spmd

    nc = bacc.Bacc("TRN2", target_bir_lowering=False, num_devices=1)
    arrays, args = {}, {}
    for name in _INS:
        arr = np.ascontiguousarray(inputs[name])
        arrays[f"in_{name}"] = arr
        args[name] = nc.dram_tensor(f"in_{name}", arr.shape, mybir.dt.from_np(arr.dtype), kind="ExternalInput").ap()
    out = nc.dram_tensor("out_y", (1, S, D), F32, kind="ExternalOutput").ap()
    build(nc, args, out)
    r = run_bass_kernel_spmd(nc, [arrays], core_ids=[0])
    return r.results[0]["out_y"]
```

```python
from contextlib import ExitStack

import numpy as np

import concourse.bass as bass
from concourse import mybir

F32 = mybir.dt.float32
F32R = mybir.dt.float32r
ALU = mybir.AluOpType
ACT = mybir.ActivationFunctionType
AX = mybir.AxisListType

P = 128
D = 1024
S = 512
KT = D // P
TT = S // P
CHUNK = 64
HA, DA = 4, 128
KEYS_A = HA * DA
CONV = 3 * KEYS_A
TAPS = 4
HB, DB = 8, 64
KVB = 2
GRP = HB // KVB
WIN = 3 * CHUNK
NG, EG = 4, 4
NE = NG * EG
FF = 256
EPS = 1e-6
NEG = -1.0e30

C_Z = CONV
C_BA = C_Z + KEYS_A
C_QB = C_BA + 2 * HA
C_KV = C_QB + HB * DB
C_GA = C_KV + 2 * KVB * DB
C_GB = C_GA + D

U = 2048
RING = 3
UNITS_PROJ = 11
UNITS_MERGE = 12
UNITS_OUT = 4
UNITS_PRE = UNITS_PROJ + UNITS_MERGE + UNITS_OUT
ITEMS = 2 * UNITS_PROJ
CONV_ITEMS = CONV // P
NORM_ITEMS = 2 * HA
KIND_G, KIND_U, KIND_D = 0, 1, 2
SLOTS = (S + NG * (P - 1)) // P
EXPERT_RING = 4
HALF = SLOTS * P // 2


def build(nc, a, out):
    ctx = ExitStack()
    cursor = [16512]

    def at(name, shape, dt, offset):
        return nc.alloc_sbuf_tensor_at(name, shape, dt, offset=offset)

    def region(nbytes):
        o = cursor[0]
        cursor[0] += (nbytes + 31) // 32 * 32
        return o

    def new(name, shape, dt=F32):
        return at(name, shape, dt, region(int(np.prod(shape[1:])) * 4))

    with ctx:
        def sem(name):
            return ctx.enter_context(nc.semaphore(name))

        raw = [new(f"w_raw{i}", [P, U]) for i in range(RING)]
        whi = [new(f"w_hi{i}", [P, U], F32R) for i in range(RING)]
        wlo = [new(f"w_lo{i}", [P, U], F32R) for i in range(RING)]
        h_hi = new("h_hi", [P, KT, S], F32R)
        h_lo = new("h_lo", [P, KT, S], F32R)
        r_main = region(4 * 2 * KT * S)
        fm = at("conv_z_F", [P, 16, S], F32, r_main)
        m_hi = at("merged_hi", [P, KT, S], F32R, r_main)
        m_lo = at("merged_lo", [P, KT, S], F32R, r_main + 4 * KT * S)
        r_b = region(4 * (6 * S))
        qb = at("attn_q_F", [P, 4, S], F32, r_b)
        kb = at("attn_k_F", [P, S], F32, r_b + 4 * 4 * S)
        vb = at("attn_v_T", [P, TT, P], F32, r_b + 4 * 5 * S)
        r_tmp = region(4 * 3584)
        r_x = region(4 * TT * D)
        x = at("x_T", [P, TT, D], F32, r_x)
        oa_hi = at("oA_hi", [P, 4, S], F32R, r_x)
        oa_lo = at("oA_lo", [P, 4, S], F32R, r_x + 4 * 4 * S)
        r_o = region(4 * TT * D + 64)
        ob_hi = at("oB_hi", [P, 4, S], F32R, r_o)
        ob_lo = at("oB_lo", [P, 4, S], F32R, r_o + 4 * 4 * S)
        y = at("y_T", [P, TT, D], F32, r_x)
        xpad = [at(f"conv_in{i}", [P, S + 8], F32, r_o + i * 4 * (S + 8)) for i in range(2)]
        cacc = [at(f"conv_acc{i}", [P, S], F32, r_o + 4160 + i * 4 * S) for i in range(2)]
        v_f = cacc[0]
        sqb = [at(f"square{i}", [P, S], F32, r_o + 8256 + i * 4 * S) for i in range(2)]
        rsb = [at(f"norm_factor{i}", [P, S], F32, r_o + 12352 + i * 2048) for i in range(2)]
        junk = at("square_junk", [P, D], F32, r_tmp)
        junk_f = at("square_junk_final", [P, D], F32, r_main)
        rows = at("small_rows", [57, P], F32, r_tmp + 4096)
        ba_raw = at("ba_raw", [P, KT, 8], F32, r_tmp + 4608)
        ba_hi = at("ba_hi", [P, KT, 8], F32R, r_tmp + 4864)
        ba_lo = at("ba_lo", [P, KT, 8], F32R, r_tmp + 5120)
        ba_t = at("ba_T", [P, TT, 8], F32, r_tmp + 5376)
        ba_f = at("ba_F", [8, S], F32, r_tmp + 6144)
        ga1 = at("decay_in", [P, TT, HA], F32, r_tmp + 5504)
        ga2 = at("decay_abs", [P, TT, HA], F32, r_tmp + 5568)
        ga3 = at("decay_exp", [P, TT, HA], F32, r_tmp + 5632)
        dist_i = at("key_distance_i", [P, WIN], mybir.dt.int32, r_tmp + 8192)
        dist = at("key_distance", [P, WIN], F32, r_tmp + 8960)
        dist_m = at("key_distance_abs", [P, WIN], F32, r_tmp + 9728)
        wmask = at("window_mask", [P, WIN], F32, r_tmp + 10496)
        ob_t = at("attn_out_T", [P, HB, DB], F32, r_tmp + 11264)
        mxs = at("score_max", [P, GRP], F32, r_tmp + 13312)
        nmx = at("score_max_neg", [P, GRP], F32, r_tmp + 13344)
        esk = at("sink_term", [P, GRP], F32, r_tmp + 13376)
        sms = at("prob_sum", [P, GRP], F32, r_tmp + 13408)
        den = at("prob_norm", [P, GRP], F32, r_tmp + 13440)
        bias = at("alibi_bias", [P, HB, WIN], F32, r_x)
        pb = at("probs", [P, GRP, 2 * P], F32, r_x + 6144)
        pt = at("probs_F", [P, 2, GRP, P], F32, r_x + 10240)
        dn = [at(f"dn{i}", [P, HA, P], F32, r_b + 2048 * i) for i in range(12)]
        (d_dec, d_lt, d_qd, d_kq, d_k, d_v, d_kd, d_inv, d_invT, d_x, d_c, d_s) = dn
        sg = at("gates_F", [P, 4, S], F32, r_b)
        prod = at("gated_A", [P, 2, S], F32, r_b + 4 * 4 * S)
        mrg = at("merged", [P, 2, S], F32, r_tmp)
        ffn_raw = 16512
        tx = at("ffn_in_T", [P, TT, KT, P], F32, ffn_raw)
        th = at("ffn_in_T_hi", [P, TT, KT, P], F32R, ffn_raw + 65536)
        tl = at("ffn_in_T_lo", [P, TT, KT, P], F32R, ffn_raw + 81920)
        perm = at("to_slots", [P, TT, SLOTS, P], F32R, ffn_raw + 98304)
        hf = at("ffn_in_F", [P, KT, S], F32, ffn_raw + 114688)
        lgf = at("router_logits_F", [NG + NE, S], F32, r_o)
        dpos = at("pos_diagonal", [P, TT, P], F32, r_o + 2048)
        eraw = [at(f"ew_raw{i}", [P, U], F32, ffn_raw + 8192 * i) for i in range(EXPERT_RING)]
        gu_hi = [at(f"gate_up_hi{i}", [P, 2, KT, FF], F32R, ffn_raw + 32768 * (i + 1)) for i in range(2)]
        gu_lo = [at(f"gate_up_lo{i}", [P, 2, KT, FF], F32R, ffn_raw + 32768 * (i + 1) + 16384) for i in range(2)]
        dn_hi = at("down_hi", [P, 2, D], F32R, ffn_raw + 98304)
        dn_lo = at("down_lo", [P, 2, D], F32R, ffn_raw + 106496)
        xs = at("slot_tokens_F", [P, KT, SLOTS * P], F32, ffn_raw + 114688)
        xs_hi = at("slot_in_hi", [P, KT, P], F32R, ffn_raw + 143360)
        xs_lo = at("slot_in_lo", [P, KT, P], F32R, ffn_raw + 147456)
        eg = at("gate_silu", [P, FF], F32, ffn_raw + 151552)
        ea = [at(f"hidden_T{i}", [P, FF], F32, ffn_raw + 152576 + 1024 * i) for i in range(2)]
        ea_hi = at("hidden_hi", [P, 2, P], F32R, ffn_raw + 154624)
        ea_lo = at("hidden_lo", [P, 2, P], F32R, ffn_raw + 155648)
        nfin = at("norm_final_b", [P, D], F32, ffn_raw + 156672)
        assert ffn_raw + 160768 <= r_x
        os_hi = at("slot_out_hi", [P, 2, S], F32R, r_o)
        os_lo = at("slot_out_lo", [P, 2, S], F32R, r_o + 4096)
        posb = at("position_rows", [P, S], F32, r_o + 8192)
        back = at("from_slot", [P, S], F32R, r_o + 10240)
        out_t = at("out_T", [P, TT, D], F32, ffn_raw)
        rt_at = [r_o + 12288]

        def rt(name, shape):
            o = rt_at[0]
            rt_at[0] += (int(np.prod(shape[1:])) * 4 + 31) // 32 * 32
            return at(name, shape, F32, o)

        lg = rt("router_logits", [P, TT, NG + NE])
        gmx, gsm, gp = rt("group_max", [P, TT]), rt("group_sum", [P, TT]), rt("group_prob", [P, TT])
        gex, gkey, goh = rt("group_exp", [P, TT, NG]), rt("group_key", [P, TT, NG]), rt("group_onehot", [P, TT, NG])
        kmx = rt("key_max", [P, TT])
        eprod = rt("group_logits", [P, TT * NG, EG])
        ig, ekey = rt("in_group", [P, TT, EG]), rt("expert_key", [P, TT, EG])
        e1, e2 = rt("first_onehot", [P, TT, EG]), rt("second_onehot", [P, TT, EG])
        m1, m2, dif, w1, w2 = (rt(n_, [P, TT]) for n_ in ("first_logit", "second_logit", "logit_gap", "first_weight", "second_weight"))
        ce, ce2 = rt("in_group_weights", [P, TT, EG]), rt("in_group_weights2", [P, TT, EG])
        ident = new("ident", [P, P])
        ones = new("ones", [P, P])
        tri = new("tri", [P, P])
        negm = new("neg_mask", [P, P])
        blk = new("same_chunk", [P, P])
        lvl = new("level_masks", [P, 6, P])
        cols = new("small_cols", [P, 57])
        nffn = new("norm_ffn_cols", [P, KT])
        ssq = new("sum_squares", [P, TT])
        rst = new("rms_factor", [P, TT])
        rsq_i = new("rsqrt_seed", [P, TT], mybir.dt.int32)
        rsq_t = new("rsqrt_tmp", [P, TT])
        epsb = new("eps", [P, 1])
        bta = new("beta_T", [P, TT, HA])
        gdt = new("log_decay_T", [P, TT, HA])
        alog = new("a_log_b", [P, HA])
        dtb = new("dt_bias_b", [P, HA])
        ealog = new("exp_a_log", [P, HA])
        gsum = new("decay_sums_T", [P, 4, TT * HA])
        gexp = new("exp_G", [P, TT, HA])
        kds = new("exp_Gend_minus_G", [P, TT, HA])
        cdec = new("chunk_decay", [P, 2, TT, HA])
        bexp = new("beta_exp_G", [P, TT, HA])
        osq = new("out_square_sum", [P, HA])
        ors = new("out_rms_factor", [P, HA])
        sinkb = new("sinks_b", [P, HB])
        rw_raw = new("router_raw", [P, KT, NG + NE])
        prio = new("index_priority", [P, EG])
        before = new("earlier_tokens", [P, P])
        row_i = new("index_row_i", [P, P], mybir.dt.int32)
        row = new("index_row", [P, P])
        slot_qi = new("slot_position_i", [P, 1], mybir.dt.int32)
        slot_q = new("slot_position", [P, 1])
        slot_n = new("slot_numbers", [P, SLOTS + 1])
        tile_n = new("tile_thresholds", [P, NG])
        rank = new("rank_in_tile", [P, TT, NG])
        tot = new("tile_counts", [P, TT, NG])
        cnt = new("group_counts", [P, NG])
        over = new("count_over", [P, NG, NG])
        need = new("slots_of_group", [P, NG])
        ends = new("slot_ends", [P, NG])
        base = new("slot_bases", [P, NG])
        ppos = new("position_terms", [P, TT, NG])
        pos = new("position", [P, TT])
        pos_s = new("position_in_slot", [P, TT, SLOTS])
        past = new("slots_past", [P, SLOTS + 1, NG])
        gsl = new("group_of_slot", [P, SLOTS + 1])
        first_e = new("first_expert_of_slot", [P, SLOTS + 1], mybir.dt.int32)
        cws = new("slot_weights", [P, SLOTS, EG])
        cwe = new("this_slot_weights", [P, EG])
        brg = new("router_bias", [P, NG + NE])

        assert cursor[0] <= 229368, cursor[0]

        ps = [ctx.enter_context(nc.psum_tensor(f"bank{i}", [P, S], F32)) for i in range(8)]

        x_in = [sem(f"x_in{t}") for t in range(TT)]
        small_in = sem("small_in")
        raw_in = [sem(f"raw_in{i}") for i in range(RING)]
        dve_step, act_step, pool_step = sem("dve_step"), sem("act_step"), sem("pool_step")
        consts = sem("consts_ready")
        eps_set = sem("eps_set")
        hi_done, lo_done = sem("w_hi_done"), sem("w_lo_done")
        ssq_done, x_scaled = sem("ssq_done"), sem("x_scaled")
        rows_ps, cols_done = sem("rows_ps"), sem("cols_done")
        ht_ps, ht_hi, ht_lo = sem("ht_ps"), sem("ht_hi"), sem("ht_lo")
        pad_zero = sem("pad_zero")
        ba_hi_done, ba_lo_done, ba_ps, ba_copied = sem("ba_hi_done"), sem("ba_lo_done"), sem("ba_ps"), sem("ba_copied")
        ba_f_done, vt_ps, vb_done = sem("ba_F_done"), sem("attn_v_T_ps"), sem("attn_v_done")
        proj_ps, proj_evac = sem("proj_ps"), sem("proj_evac")
        conv_done, silu_done, sq_done = sem("conv_done"), sem("silu_done"), sem("sq_done")
        norm_ps, root_done, norm_done = sem("norm_ps"), sem("root_done"), sem("norm_done")
        gd_abs, gd_exp, gd_ln, gates_done = sem("gd_abs"), sem("gd_exp"), sem("gd_ln"), sem("gates_done")
        dist_set, bias_done, attn_zero = sem("dist_set"), sem("bias_done"), sem("probs_zeroed")
        sc_ps, max_done, exp_done = sem("scores_ps"), sem("max_done"), sem("probs_exp")
        pt_ps, pt_prev, pt_cur = sem("probsF_ps"), sem("probsF_prev"), sem("probsF_cur")
        pv_ps, ob_ready, obt_ps = sem("pv_ps"), sem("attn_out_T_ready"), sem("attn_out_F_ps")
        ob_hi_done, ob_lo_done = sem("oB_hi_done"), sem("oB_lo_done")
        gsum_ps, gsum_sub, gexp_done, dscal_done = sem("gsum_ps"), sem("gsum_sub"), sem("gexp_done"), sem("dscal_done")
        rb_ready, rb_ps, dec_in = sem("row_source"), sem("row_bcast_ps"), sem("decay_arg")
        egb_done, dec_done = sem("exp_G_rows"), sem("decay_done")
        kk_ps, kv_ps, qd_done, kbv_done = sem("kk_ps"), sem("kv_T_ps"), sem("q_decayed"), sem("kv_scaled")
        inv0, inv0_ps, inv0_copied = sem("inv_T_first"), sem("inv_first_ps"), sem("inv_first")
        ct_done, x_ps, xs_done, de_ps, de_done = (sem("level_block"), sem("block_inv_ps"), sem("block_inv"),
                                                  sem("inv_update_ps"), sem("inv_updated"))
        wu_ps, wu_done = sem("wu_ps"), sem("wu_done")
        s_zero, ws_ps, vn_done, o_ps, ds_ps, s_done = (sem("state_zero"), sem("w_state_ps"), sem("v_new"),
                                                       sem("o_ps"), sem("state_add_ps"), sem("state_done"))
        on_done, oat_ps, oaf_done = sem("o_normed"), sem("oA_F_ps"), sem("oA_F_gated")
        oa_hi_done, oa_lo_done = sem("oA_hi_done"), sem("oA_lo_done")
        mg_ps, sg_done, mul_done = sem("merge_ps"), sem("gate_sigmoid"), sem("gate_product")
        mg_hi, mg_lo = sem("merged_hi_done"), sem("merged_lo_done")
        x2_in, out_used, y_done = sem("x_again"), sem("out_proj_ps"), sem("residual_done")
        ssq2, t_scaled, tt_ps, hf_act, hf_dve = sem("ssq2"), sem("ffn_scaled"), sem("ffn_F_ps"), sem("ffn_F_even"), sem("ffn_F_odd")
        th_done, tl_done = sem("ffn_T_hi"), sem("ffn_T_lo")
        lgf_ps, lgf_done, lg_ps = sem("router_F_ps"), sem("router_F_done"), sem("router_ps")
        gd_in, gd_out, ed_in, ed_out = (sem("group_arg"), sem("group_exp_done"), sem("pair_arg"), sem("pair_exp_done"))
        idx_rows, goh_done, rank_ps, slots_done = sem("index_rows"), sem("group_onehot_done"), sem("rank_ps"), sem("slots_known")
        perm_done, dpos_done, posb_ps, posb_done = sem("to_slots_done"), sem("pos_diagonal_done"), sem("pos_rows_ps"), sem("pos_rows_done")
        cw_in, cw_ps, cw_done = sem("weights_known"), sem("slot_weights_ps"), sem("slot_weights_done")
        xs_ps, xs_act, xs_dve = sem("slot_tokens_ps"), sem("slot_tokens_even"), sem("slot_tokens_odd")
        eraw_in = [sem(f"ew_raw_in{i}") for i in range(EXPERT_RING)]
        ehi_done, elo_done = sem("ew_hi_done"), sem("ew_lo_done")
        xs_hi_done, xs_lo_done = sem("slot_in_hi_done"), sem("slot_in_lo_done")
        gu_ps, gsilu, hid_done, hidt_ps = sem("gate_up_ps"), sem("gate_silu_done"), sem("hidden_done"), sem("hidden_F_ps")
        hid_hi, hid_lo, dn_ps = sem("hidden_hi_done"), sem("hidden_lo_done"), sem("down_ps")
        os_hi_done, os_lo_done = sem("slot_out_hi_done"), sem("slot_out_lo_done")
        back_done, un_ps, tok_added = sem("from_slot_done"), sem("to_tokens_ps"), sem("y_added")
        cwe_done, slot_q_done = sem("this_slot_weights_done"), sem("slot_position_set")
        nfin_in, ssq3, fin_done, stored = sem("norm_final_in"), sem("ssq3"), sem("final_done"), sem("stored")

        w_in = a["w_in"][0].rearrange("(k p) n -> p k n", p=P)

        def unit_sources(u):
            r = raw[u % RING][:, :].rearrange("p (k n) -> p k n", k=KT)
            if u < 8:
                return [(r, w_in[:, :, 256 * u:256 * (u + 1)])]
            if u < 10:
                q = w_in[:, :, C_QB:C_QB + HB * DB].rearrange("p k (g j c) -> p k j g c", g=KVB, j=GRP)
                return [(r[:, :, 128 * i + 64 * g:128 * i + 64 * g + 64], q[:, :, 2 * (u - 8) + i, g, :])
                        for i in range(2) for g in range(KVB)]
            if u == 10:
                return [(r, w_in[:, :, C_KV:C_KV + 256])]
            if u < UNITS_PROJ + UNITS_MERGE:
                j, c = divmod(u - UNITS_PROJ, 3)
                cs = slice(256 * j, 256 * (j + 1))
                if c < 2:
                    o = (C_GA, C_GB)[c] + 256 * j
                    return [(r, w_in[:, :, o:o + 256])]
                return [(r[:, 0:4, :], a["w_out_a"][0].rearrange("(k p) n -> p k n", p=P)[:, :, cs]),
                        (r[:, 4:8, :], a["w_out_b"][0].rearrange("(k p) n -> p k n", p=P)[:, :, cs])]
            n_, kh = divmod(u - UNITS_PROJ - UNITS_MERGE, 2)
            return [(raw[u % RING][:, :].rearrange("p (k n) -> p k n", k=4),
                     a["w_out"][0].rearrange("(k p) n -> p k n", p=P)[:, 4 * kh:4 * kh + 4, 512 * n_:512 * (n_ + 1)])]

        def unit_dmas(u):
            return len(unit_sources(u))

        def raw_value(u):
            return 16 * sum(unit_dmas(v) for v in range(u % RING, u + 1, RING))

        def bc_mid(ap, n):
            return ap.unsqueeze(1).broadcast_to([ap.shape[0], n, ap.shape[1]])

        def bc_last(ap, n):
            return ap.unsqueeze(2).broadcast_to([ap.shape[0], ap.shape[1], n])

        def bank4(i):
            return ps[i][:, :].rearrange("p (h c) -> p h c", h=4)

        def tbank(j):
            return ps[7] if j % 2 else ps[2]

        block = ctx.enter_context(nc.Block())

        def wait_used(eng, v):
            if v < UNITS_PROJ:
                eng.wait_ge(proj_ps, 2 * (v + 1))
            elif v < UNITS_PROJ + UNITS_MERGE:
                j, c = divmod(v - UNITS_PROJ, 3)
                eng.wait_ge(mg_ps, 8 * j + (2, 4, 8)[c])
            else:
                eng.wait_ge(out_used, v - UNITS_PROJ - UNITS_MERGE + 1)

        def place(kind, s, j):
            c = {KIND_G: 3 * j - 1, KIND_U: 3 * j, KIND_D: 3 * j + 4}[kind]
            if isinstance(s, int) and s == 0 and j == 0 and kind != KIND_D:
                c += 1
            if isinstance(s, int) and s == SLOTS - 1 and j == EG - 1 and kind == KIND_D:
                c -= 2
            return c % EXPERT_RING, 3 * s + c // EXPERT_RING + 1, 12 * s + c + 1

        def is_first(s):
            return isinstance(s, int) and s == 0

        def is_last(s):
            return isinstance(s, int) and s == SLOTS - 1

        w_gate_v = a["w_gate"][0].rearrange("e (p k) f -> e p (k f)", p=P)
        w_up_v = a["w_up"][0].rearrange("e (p k) f -> e p (k f)", p=P)
        w_down_v = a["w_down"][0].rearrange("e (f p) d -> e p f d", p=P)
        kv_ = lambda r: r[:, :].rearrange("p (k n) -> p k n", k=KT)

        def norms_at(i):
            return range(2 * (i - 17), 2 * (i - 17) + 2) if 17 <= i < 17 + NORM_ITEMS // 2 else ()

        @block.sync
        def _(sp):
            for t in range(TT):
                sp.dma_start(x[:, t, :], a["x"][0, t * P:(t + 1) * P, :]).then_inc(x_in[t], 16)
            sp.dma_start(rows[0:8, :], a["norm_mix_w"][0].rearrange("(k p) -> k p", p=P)).then_inc(small_in, 16)
            sp.dma_start(rows[8:56, :], a["conv_w"][0].rearrange("j (i p) -> (j i) p", p=P)).then_inc(small_in, 16)
            sp.dma_start(rows[56:57, :], a["delta_norm_w"]).then_inc(small_in, 16)
            sp.dma_start(ba_raw[:, :, :], w_in[:, :, C_BA:C_BA + 8]).then_inc(small_in, 16)
            sp.dma_start(dtb[:, :], a["dt_bias"].to_broadcast([P, HA])).then_inc(small_in, 16)
            sp.dma_start(alog[:, :], a["a_log"].to_broadcast([P, HA])).then_inc(small_in, 16)
            sp.dma_start(sinkb[:, :], a["sinks"].to_broadcast([P, HB])).then_inc(small_in, 16)
            sp.dma_start(brg[:, 0:NG], a["b_router_group"].to_broadcast([P, NG])).then_inc(small_in, 16)
            sp.dma_start(brg[:, NG:], a["b_router_expert"].to_broadcast([P, NE])).then_inc(small_in, 16)
            sp.dma_start(nffn[:, :], a["norm_ffn_w"][0].rearrange("(p k) -> p k", k=KT)).then_inc(small_in, 16)
            sp.dma_start(rw_raw[:, :, 0:NG], a["w_router_group"][0].rearrange("(p k) n -> p k n", k=KT)).then_inc(small_in, 16)
            sp.dma_start(rw_raw[:, :, NG:], a["w_router_expert"][0].rearrange("(p k) n -> p k n", k=KT)).then_inc(small_in, 16)
            for u in range(UNITS_PRE):
                if u >= RING:
                    sp.wait_ge(hi_done, u - RING + 1)
                    sp.wait_ge(lo_done, u - RING + 1)
                for dst, src in unit_sources(u):
                    sp.dma_start(dst, src).then_inc(raw_in[u % RING], 16)
            sp.wait_ge(mg_ps, 8 * 4)
            sp.dma_start(y[:, :, :], a["x"][0].rearrange("(t p) d -> p t d", p=P)).then_inc(x2_in, 16)
            sp.dma_start(nfin[:, :], a["norm_final_w"].rearrange("(o d) -> o d", o=1).to_broadcast([P, D])).then_inc(nfin_in, 16)

            sp.wait_ge(slots_done, 1)

            def first_expert(s):
                return sp.value_load(first_e[0:1, bass.ds(s, 1)], min_val=0, max_val=NE - EG)

            def load(kind, s, j, e):
                slot, _, count = place(kind, s, j)
                if not (is_first(s) and count <= EXPERT_RING):
                    sp.wait_ge(ehi_done, count - EXPERT_RING)
                    sp.wait_ge(elo_done, count - EXPERT_RING)
                src = (w_gate_v, w_up_v, w_down_v)[kind][e]
                dst = eraw[slot][:, :]
                if kind == KIND_D:
                    dst = dst.rearrange("p (f d) -> p f d", f=2)
                sp.dma_start(dst, src).then_inc(eraw_in[slot], 16)

            def slot_loads(s):
                e0 = first_expert(s)
                if is_first(s):
                    load(KIND_G, 0, 0, e0)
                    load(KIND_U, 0, 0, e0)
                for j in range(EG - 1):
                    load(KIND_G, s, j + 1, e0 + (j + 1))
                    load(KIND_U, s, j + 1, e0 + (j + 1))
                    load(KIND_D, s, j, e0 + j)
                if not is_last(s):
                    e1 = first_expert(s + 1)
                    load(KIND_G, s, EG, e1)
                    load(KIND_U, s, EG, e1)
                load(KIND_D, s, EG - 1, e0 + (EG - 1))

            slot_loads(0)
            with sp.Fori(1, SLOTS - 1) as s:
                slot_loads(s)
            slot_loads(SLOTS - 1)
            for t in range(TT):
                sp.wait_ge(fin_done, t + 1)
                sp.dma_start(out[0, t * P:(t + 1) * P, :], out_t[:, t, :]).then_inc(stored, 16)
            sp.wait_ge(stored, 16 * TT)

        @block.gpsimd
        def _(pool):
            n = [0]

            def link(ins):
                n[0] += 1
                ins.then_inc(pool_step, 1)
                pool.wait_ge(pool_step, n[0])

            nc.gpsimd.memset(ones[:, :], 1.0)
            nc.gpsimd.memset(blk[:, :], 0.0)
            nc.gpsimd.memset(tri[:, :], 1.0)
            nc.gpsimd.memset(lvl[:, :, :], 1.0)
            link(nc.gpsimd.memset(ident[:, :], 0.0))
            link(nc.gpsimd.affine_select(out=ident[:, :], in_=ident[:, :], compare_op=ALU.not_equal, fill=1.0,
                                         base=0, pattern=[[-1, P]], channel_multiplier=1))
            link(nc.gpsimd.memset(blk[0:64, 0:64], 1.0))
            link(nc.gpsimd.memset(blk[64:128, 64:128], 1.0))
            link(nc.gpsimd.affine_select(out=tri[:, :], in_=tri[:, :], compare_op=ALU.is_ge, fill=0.0,
                                         base=0, pattern=[[1, P]], channel_multiplier=-1))
            link(nc.gpsimd.affine_select(out=tri[:, 64:128], in_=tri[:, 64:128], compare_op=ALU.is_ge, fill=0.0,
                                         base=-64, pattern=[[0, 64]], channel_multiplier=1))
            for l in range(6):
                b = 1 << l
                m = lvl[:, l, :].rearrange("p (n r) -> p n r", r=2 * b)
                nc.gpsimd.memset(m[:, :, 0:b], 0.0).then_inc(pool_step, 1)
                n[0] += 1
                pool.wait_ge(pool_step, n[0])
                link(nc.gpsimd.affine_select(out=m, in_=m, compare_op=ALU.is_ge, fill=0.0, base=0,
                                             pattern=[[-2 * b, P // (2 * b)], [0, 2 * b]], channel_multiplier=1))
                link(nc.gpsimd.affine_select(out=m, in_=m, compare_op=ALU.is_ge, fill=0.0, base=b - 1,
                                             pattern=[[2 * b, P // (2 * b)], [0, 2 * b]], channel_multiplier=-1))
            nc.gpsimd.tensor_scalar(negm[:, :], tri[:, :], -1.0, -NEG, ALU.add, ALU.mult).then_inc(consts, 1)
            link(nc.gpsimd.iota(dist_i[:, :], pattern=[[-1, WIN]], base=CHUNK, channel_multiplier=1))
            link(nc.gpsimd.memset(wmask[:, :], 0.0))
            nc.gpsimd.memset(wmask[0:64, 128:192], NEG)
            nc.gpsimd.memset(wmask[64:128, 0:64], NEG).then_inc(dist_set, 1)
            pool.wait_ge(dist_set, 1)
            link(nc.gpsimd.memset(before[:, :], 1.0))
            link(nc.gpsimd.affine_select(out=before[:, :], in_=before[:, :], compare_op=ALU.is_gt, fill=0.0,
                                         base=0, pattern=[[1, P]], channel_multiplier=-1))
            for i in range(SLOTS + 1):
                link(nc.gpsimd.memset(slot_n[:, i:i + 1], float(i)))
            for i in range(NG):
                link(nc.gpsimd.memset(tile_n[:, i:i + 1], float(P * i)))
            link(nc.gpsimd.iota(slot_qi[:, :], pattern=[[0, 1]], base=-P, channel_multiplier=1))
            nc.gpsimd.iota(row_i[:, :], pattern=[[1, P]], base=0, channel_multiplier=0).then_inc(idx_rows, 1)

        @block.scalar
        def _(act):
            n = [0]

            def link(ins):
                n[0] += 1
                ins.then_inc(act_step, 1)
                act.wait_ge(act_step, n[0])

            def split_hi(u):
                act.wait_ge(raw_in[u % RING], raw_value(u))
                if u >= RING:
                    wait_used(act, u - RING)
                act.activation(whi[u % RING][:, :], raw[u % RING][:, :], ACT.Copy).then_inc(hi_done, 1)

            act.wait_ge(eps_set, 1)
            for t in range(TT):
                act.wait_ge(x_in[t], 16)
                link(act.activation(junk[:, :], x[:, t, :], ACT.Square, accum_out=ssq[:, t:t + 1]))
                act.activation(rst[:, t:t + 1], ssq[:, t:t + 1], ACT.Sqrt, scale=1.0 / D, bias=epsb[:, :]).then_inc(ssq_done, 1)
            act.wait_ge(small_in, 192)
            act.activation(ba_hi[:, :, :], ba_raw[:, :, :], ACT.Copy).then_inc(ba_hi_done, 1)
            act.activation(ealog[:, :], alog[:, :], ACT.Exp).then_inc(gd_exp, 1)
            split_hi(0)
            split_hi(1)
            act.wait_ge(cols_done, 1)
            for k in range(KT):
                act.wait_ge(ht_ps, k + 1)
                act.activation(h_hi[:, k, :], ps[k % 2][:, :], ACT.Copy, scale=cols[:, k:k + 1]).then_inc(ht_hi, 1)

            def conv_silu(i):
                act.wait_ge(conv_done, i + 1)
                act.activation(fm[:, i, :], cacc[i % 2][:, :], ACT.Silu).then_inc(silu_done, 1)

            def square(i):
                act.wait_ge(silu_done, i + 1)
                if i >= 2:
                    act.wait_ge(norm_ps, i - 1)
                act.activation(sqb[i % 2][:, :], fm[:, i, :], ACT.Square).then_inc(sq_done, 1)

            def norm_root(i):
                act.wait_ge(norm_ps, i + 1)
                if i >= 2:
                    act.wait_ge(norm_done, i - 1)
                act.activation(rsb[i % 2][:, :], ps[2 + i % 2][:, :], ACT.Sqrt, bias=epsb[:, :]).then_inc(root_done, 1)

            for i in range(ITEMS):
                if i % 2 == 0 and i // 2 + 2 < UNITS_PROJ:
                    split_hi(i // 2 + 2)
                act.wait_ge(proj_ps, i + 1)
                if i < CONV_ITEMS:
                    act.wait_ge(pad_zero, 2)
                    if i >= 2:
                        act.wait_ge(conv_done, i - 1)
                    act.activation(xpad[i % 2][:, 3:3 + S], ps[i % 2][:, :], ACT.Copy).then_inc(proj_evac, 1)
                elif i < 16:
                    act.activation(fm[:, i, :], ps[i % 2][:, :], ACT.Silu).then_inc(proj_evac, 1)
                elif i < 20:
                    act.activation(qb[:, i - 16, :], ps[i % 2][:, :], ACT.Copy).then_inc(proj_evac, 1)
                elif i == 20:
                    act.activation(kb[:, :], ps[i % 2][:, :], ACT.Copy).then_inc(proj_evac, 1)
                else:
                    act.activation(v_f[:, :], ps[i % 2][:, :], ACT.Copy).then_inc(proj_evac, 1)
                if 1 <= i <= CONV_ITEMS:
                    conv_silu(i - 1)
                for j in norms_at(i):
                    norm_root(j)
                for j in norms_at(i + 1):
                    square(j)
            act.wait_ge(vt_ps, 1)
            act.activation(vb[:, :, :], bank4(4), ACT.Copy).then_inc(vb_done, 1)
            act.wait_ge(ba_copied, 1)
            act.activation(bta[:, :, :], ba_t[:, :, 0:HA], ACT.Sigmoid).then_inc(gates_done, 1)
            act.wait_ge(gd_abs, 1)
            link(act.activation(ga3[:, :, :], ga2[:, :, :], ACT.Exp, scale=-1.0))
            act.activation(ga2[:, :, :], ga3[:, :, :], ACT.Ln, bias=1.0).then_inc(gd_ln, 1)


            for a_ in range(2 * TT):
                m, g = a_ // 2, a_ % 2
                c0 = CHUNK if m else P
                act.wait_ge(max_done, a_ + 1)
                for h in range(GRP):
                    act.activation(pb[:, h, c0:], pb[:, h, c0:], ACT.Exp, bias=nmx[:, h:h + 1], accum_out=sms[:, h:h + 1])
                act.activation(esk[:, :], esk[:, :], ACT.Exp).then_inc(exp_done, 1)
                if m:
                    act.wait_ge(pt_ps, 2 * a_ + 1)
                    if a_ > 2:
                        act.wait_ge(pv_ps, a_)
                    act.activation(pt[:, 0, :, :], bank4(2), ACT.Copy).then_inc(pt_prev, 1)
                if g == 1:
                    act.wait_ge(obt_ps, m + 1)
                    act.activation(ob_hi[:, :, m * P:(m + 1) * P], bank4(5), ACT.Copy).then_inc(ob_hi_done, 1)

            act.wait_ge(gsum_sub, 1)
            act.activation(gexp[:, :, :], gsum[:, 0, :], ACT.Exp)
            act.activation(kds[:, :, :], gsum[:, 1, :], ACT.Exp)
            act.activation(cdec[:, :, :, :], gsum[:, 2:4, :], ACT.Exp).then_inc(gexp_done, 1)
            for m in range(TT):
                act.wait_ge(dec_in, m + 1)
                if m:
                    act.wait_ge(o_ps, m)
                act.activation(d_qd[:, :, :], bank4(2), ACT.Exp).then_inc(egb_done, 1)
                act.activation(d_dec[:, :, :], d_dec[:, :, :], ACT.Exp).then_inc(dec_done, 1)
                act.wait_ge(inv0_ps, m + 1)
                act.activation(d_inv[:, :, :], bank4(2), ACT.Copy).then_inc(inv0_copied, 1)
                for l in range(1, 6):
                    act.wait_ge(x_ps, 5 * m + l)
                    act.activation(d_x[:, :, :], bank4(2), ACT.Copy).then_inc(xs_done, 1)
                act.wait_ge(wu_ps, m + 1)
                act.activation(d_k[:, :, :], bank4(5), ACT.Copy)
                act.activation(d_v[:, :, :], bank4(6), ACT.Copy).then_inc(wu_done, 1)
                act.wait_ge(oaf_done, m + 1)
                act.activation(oa_hi[:, :, m * P:(m + 1) * P], d_lt[:, :, :], ACT.Copy).then_inc(oa_hi_done, 1)

            act.wait_ge(oa_lo_done, TT)
            for u in range(UNITS_PROJ, UNITS_PROJ + 2):
                split_hi(u)
            for j in range(4):
                for r in range(4):
                    if r % 2 == 0:
                        split_hi(UNITS_PROJ + 2 + 3 * j + r // 2)
                    act.wait_ge(mg_ps, 8 * j + r + 1)
                    if j:
                        act.wait_ge(mul_done, 4 * j)
                    act.activation(sg[:, r, :], ps[r][:, :], ACT.Sigmoid).then_inc(sg_done, 1)
                for r in range(2):
                    act.wait_ge(mul_done, 4 * j + 3 + r)
                    act.activation(m_hi[:, 2 * j + r, :], mrg[:, r, :], ACT.Copy).then_inc(mg_hi, 1)
                split_hi(UNITS_PROJ + 4 + 3 * j)
            for u in range(UNITS_PRE - 2, UNITS_PRE):
                split_hi(u)
            for t in range(TT):
                act.wait_ge(y_done, 4 + t + 1)
                if t:
                    act.wait_ge(ssq2, t)
                act.activation(junk[:, :], y[:, t, :], ACT.Square, accum_out=ssq[:, t:t + 1]).then_inc(ssq2, 1)

            for k in range(0, KT, 2):
                act.wait_ge(tt_ps, k + 1)
                act.activation(hf[:, k, :], ps[0][:, :], ACT.Copy, scale=nffn[:, k:k + 1]).then_inc(hf_act, 1)
            for t in range(TT):
                act.wait_ge(t_scaled, t + 1)
                act.activation(th[:, t, :, :], tx[:, t, :, :], ACT.Copy).then_inc(th_done, 1)
            act.wait_ge(gd_in, 1)
            act.activation(gex[:, :, :], gex[:, :, :], ACT.Exp).then_inc(gd_out, 1)
            act.wait_ge(ed_in, 1)
            act.activation(dif[:, :], dif[:, :], ACT.Exp).then_inc(ed_out, 1)
            act.wait_ge(posb_ps, 1)
            act.activation(posb[:, :], ps[3][:, :], ACT.Copy).then_inc(posb_done, 1)
            for i in range(0, 2 * KT, 2):
                act.wait_ge(xs_ps, i + 1)
                act.activation(xs[:, i // 2, 0:HALF], ps[4][:, 0:HALF], ACT.Copy, scale=nffn[:, i // 2:i // 2 + 1]).then_inc(xs_act, 1)

            def split_in_hi(s):
                act.activation(xs_hi[:, :, :], xs[:, :, bass.ds(P * s, P)], ACT.Copy).then_inc(xs_hi_done, 1)

            def split_expert(kind, s, j):
                slot, arrived, _ = place(kind, s, j)
                act.wait_ge(eraw_in[slot], 16 * arrived)
                if kind == KIND_D:
                    if not (is_first(s) and j == 0):
                        act.wait_ge(dn_ps, EG * s + j)
                    else:
                        act.wait_ge(cw_ps, 1)
                    dst, src = dn_hi[:, :, :], eraw[slot][:, :].rearrange("p (f d) -> p f d", f=2)
                else:
                    if not (is_first(s) and j < 2):
                        act.wait_ge(gu_ps, EG * s + j - 1)
                    dst, src = gu_hi[j % 2][:, kind, :, :], kv_(eraw[slot])
                act.activation(dst, src, ACT.Copy).then_inc(ehi_done, 1)

            split_expert(KIND_G, 0, 0)
            act.wait_ge(xs_act, KT)
            act.wait_ge(xs_dve, KT)
            split_in_hi(0)
            split_expert(KIND_U, 0, 0)
            split_expert(KIND_G, 0, 1)
            split_expert(KIND_U, 0, 1)

            def slot_out_hi(s):
                act.wait_ge(dn_ps, EG * s + EG)
                if not is_first(s):
                    act.wait_ge(un_ps, 8 * s)
                for n_ in range(2):
                    act.activation(os_hi[:, n_, :], ps[3 + n_][:, :], ACT.Copy).then_inc(os_hi_done, 1)

            def slot_act(s):
                for j in range(EG):
                    i = EG * s + j
                    act.wait_ge(gu_ps, i + 1)
                    if not (is_first(s) and j == 0):
                        act.wait_ge(hid_done, i)
                    act.activation(eg[:, :], ps[j % 2][:, 0:FF], ACT.Silu).then_inc(gsilu, 1)
                    if j == 0 and not is_first(s):
                        slot_out_hi(s - 1)
                    split_expert(KIND_D, s, j)
                    act.wait_ge(hidt_ps, i + 1)
                    if not (is_first(s) and j == 0):
                        act.wait_ge(dn_ps, i)
                    act.activation(ea_hi[:, :, :], tbank(j)[:, 0:FF].rearrange("p (f c) -> p f c", f=2),
                                   ACT.Copy).then_inc(hid_hi, 1)
                    if j < 2 or not is_last(s):
                        split_expert(KIND_G, s, j + 2)
                        if j == 2:
                            act.wait_ge(gu_ps, EG * s + EG)
                            split_in_hi(s + 1)
                        split_expert(KIND_U, s, j + 2)

            slot_act(0)
            with act.Fori(1, SLOTS - 1) as s:
                slot_act(s)
            slot_act(SLOTS - 1)
            slot_out_hi(SLOTS - 1)
            for t in range(TT):
                act.wait_ge(tok_added, 8 * (SLOTS - 1) + 2 * t + 4)
                if t:
                    act.wait_ge(ssq3, t)
                act.activation(junk_f[:, :], y[:, t, :], ACT.Square, accum_out=ssq[:, t:t + 1]).then_inc(ssq3, 1)

        @block.vector
        def _(dve):
            n = [0]

            def link(ins):
                n[0] += 1
                ins.then_inc(dve_step, 1)
                dve.wait_ge(dve_step, n[0])

            def split_lo(u):
                s = u % RING
                dve.wait_ge(hi_done, u + 1)
                dve.tensor_tensor(wlo[s][:, :], raw[s][:, :], whi[s][:, :].bitcast(F32), ALU.subtract).then_inc(lo_done, 1)

            dve.memset(epsb[:, :], EPS).then_inc(eps_set, 1)
            for t in range(TT):
                dve.wait_ge(ssq_done, t + 1)
                link(dve.reciprocal(rst[:, t:t + 1], rst[:, t:t + 1]))
                dve.tensor_scalar(x[:, t, :], x[:, t, :], rst[:, t:t + 1], None, ALU.mult).then_inc(x_scaled, 1)
            dve.wait_ge(rows_ps, 1)
            dve.tensor_copy(cols[:, :], ps[7][:, 0:57]).then_inc(cols_done, 1)
            for i in range(EG):
                dve.memset(prio[:, i:i + 1], float(EG - i))
            dve.wait_ge(ba_hi_done, 1)
            dve.tensor_tensor(ba_lo[:, :, :], ba_raw[:, :, :], ba_hi[:, :, :].bitcast(F32), ALU.subtract).then_inc(ba_lo_done, 1)
            split_lo(0)
            split_lo(1)
            dve.wait_ge(cols_done, 1)
            for k in range(KT):
                dve.wait_ge(ht_hi, k + 1)
                dve.scalar_tensor_tensor(h_lo[:, k, :], ps[k % 2][:, :], cols[:, k:k + 1],
                                         h_hi[:, k, :].bitcast(F32), ALU.mult, ALU.subtract).then_inc(ht_lo, 1)
            for i in range(2):
                dve.memset(xpad[i][:, 0:3], 0.0).then_inc(pad_zero, 1)
            dve.wait_ge(ba_ps, 1)
            dve.tensor_copy(ba_f[:, :], ps[4][0:8, :]).then_inc(ba_f_done, 1)
            dve.wait_ge(ba_ps, 2)
            dve.tensor_copy(ba_t[:, :, :], ps[5][:, 0:32].rearrange("p (t c) -> p t c", t=TT)).then_inc(ba_copied, 1)

            def tap(j, i):
                c = KT + j * CONV_ITEMS + i
                return cols[:, c:c + 1]

            def conv(i):
                b = i % 2
                dve.wait_ge(proj_evac, i + 1)
                if i >= 2:
                    dve.wait_ge(silu_done, i - 1)
                link(dve.tensor_scalar(cacc[b][:, :], xpad[b][:, 0:S], tap(0, i), None, ALU.mult))
                for j in range(1, TAPS):
                    ins = dve.scalar_tensor_tensor(cacc[b][:, :], xpad[b][:, j:j + S], tap(j, i), cacc[b][:, :],
                                                   ALU.mult, ALU.add)
                    if j < TAPS - 1:
                        link(ins)
                    else:
                        ins.then_inc(conv_done, 1)

            def l2_norm(i):
                dve.wait_ge(root_done, i + 1)
                r = rsb[i % 2][:, :]
                link(dve.reciprocal(r, r))
                dve.scalar_tensor_tensor(fm[:, i, :], fm[:, i, :], float(DA) ** -0.5 if i < HA else 1.0, r,
                                         ALU.mult, ALU.mult).then_inc(norm_done, 1)

            for i in range(ITEMS):
                if i % 2 == 0 and i // 2 + 2 < UNITS_PROJ:
                    split_lo(i // 2 + 2)
                if i < CONV_ITEMS:
                    conv(i)
                for j in norms_at(i):
                    l2_norm(j)
            dve.wait_ge(ba_copied, 1)
            for t in range(TT):
                ins = dve.tensor_tensor(ga1[:, t, :], ba_t[:, t, HA:], dtb[:, :], ALU.add)
            link(ins)
            dve.scalar_tensor_tensor(ga2[:, :, :], ga1[:, :, :], -1.0, ga1[:, :, :], ALU.mult, ALU.max).then_inc(gd_abs, 1)
            dve.wait_ge(gd_ln, 1)
            link(dve.scalar_tensor_tensor(ga3[:, :, :], ga1[:, :, :], 0.0, ga2[:, :, :], ALU.max, ALU.add))
            dve.wait_ge(gd_exp, 1)
            for t in range(TT):
                ins = dve.scalar_tensor_tensor(gdt[:, t, :], ga3[:, t, :], -1.0, ealog[:, :], ALU.mult, ALU.mult)
            ins.then_inc(gates_done, 1)


            dve.wait_ge(dist_set, 1)
            link(dve.tensor_copy(dist[:, :], dist_i[:, :]))
            link(dve.scalar_tensor_tensor(dist_m[:, :], dist[:, :], -1.0, dist[:, :], ALU.mult, ALU.max))
            for h in range(HB):
                slope = 2.0 ** (-8.0 * (h + 1) / HB)
                dve.scalar_tensor_tensor(bias[:, h, :], dist_m[:, :], -slope, wmask[:, :], ALU.mult, ALU.add)
            link(dve.memset(pb[:, :, 0:CHUNK], 0.0))
            for a_ in range(2 * TT):
                m, g = a_ // 2, a_ % 2
                c0 = CHUNK if m else P
                heads = slice(GRP * g, GRP * (g + 1))
                dve.wait_ge(sc_ps, a_ + 1)
                if a_:
                    dve.wait_ge(pt_ps, 2 * a_)
                for b in range(2):
                    bank = ps[b][:, :].rearrange("p (h c) -> p h c", h=2)
                    hs = GRP * g + 2 * b
                    ins = dve.scalar_tensor_tensor(pb[:, 2 * b:2 * b + 2, c0:], bank[:, :, c0:], DB ** -0.5,
                                                   bias[:, hs:hs + 2, c0 - CHUNK:], ALU.mult, ALU.add)
                link(ins)
                link(dve.tensor_reduce(mxs[:, :], pb[:, :, c0:], AX.X, ALU.max))
                link(dve.tensor_tensor(mxs[:, :], mxs[:, :], sinkb[:, heads], ALU.max))
                dve.tensor_scalar(nmx[:, :], mxs[:, :], -1.0, None, ALU.mult)
                dve.tensor_tensor(esk[:, :], sinkb[:, heads], mxs[:, :], ALU.subtract).then_inc(max_done, 1)
                dve.wait_ge(pt_ps, 2 * a_ + 2)
                if a_:
                    dve.wait_ge(pv_ps, a_)
                dve.tensor_copy(pt[:, 1, :, :], bank4(3)).then_inc(pt_cur, 1)
                dve.wait_ge(exp_done, a_ + 1)
                link(dve.tensor_tensor(den[:, :], sms[:, :], esk[:, :], ALU.add))
                link(dve.reciprocal(den[:, :], den[:, :]))
                dve.wait_ge(pv_ps, a_ + 1)
                if g == 0 and m:
                    dve.wait_ge(obt_ps, m)
                ins = dve.tensor_tensor(ob_t[:, heads, :], ps[4][:, 0:GRP * DB].rearrange("p (h c) -> p h c", h=GRP),
                                        bc_last(den[:, :], DB), ALU.mult)
                ins.then_inc(ob_ready, 1)
                if g == 1:
                    dve.wait_ge(ob_hi_done, m + 1)
                    ts = slice(m * P, (m + 1) * P)
                    dve.tensor_tensor(ob_lo[:, :, ts], bank4(5), ob_hi[:, :, ts].bitcast(F32), ALU.subtract).then_inc(ob_lo_done, 1)

            def rsqrt(v, y):
                w = y.shape[1]
                i, t = rsq_i[:, 0:w], rsq_t[:, 0:w]
                link(dve.tensor_scalar(i, v.bitcast(mybir.dt.int32), 1, None, ALU.arith_shift_right))
                link(dve.tensor_scalar(y.bitcast(mybir.dt.int32), i, -1.0, float(0x5F3759DF), ALU.mult, ALU.add))
                for _ in range(3):
                    link(dve.tensor_tensor(t, y, y, ALU.mult))
                    link(dve.scalar_tensor_tensor(t, t, -0.5, v, ALU.mult, ALU.mult))
                    link(dve.scalar_tensor_tensor(y, t, 1.5, y, ALU.add, ALU.mult))

            dve.wait_ge(gsum_ps, 1)
            dve.tensor_copy(gsum[:, 3, :], ps[6][:, 48:64])
            link(dve.tensor_copy(gsum[:, 0:3, :], ps[5][:, 0:48].rearrange("p (a c) -> p a c", a=3)))
            dve.tensor_tensor(gsum[:, 1, :], gsum[:, 1, :], gsum[:, 0, :], ALU.subtract).then_inc(gsum_sub, 1)
            dve.wait_ge(gexp_done, 1)
            link(dve.tensor_tensor(bexp[:, :, :], bta[:, :, :], gexp[:, :, :], ALU.mult))
            dve.memset(d_s[:, :, :], 0.0).then_inc(s_zero, 1)
            gT = gsum[:, 0, :].rearrange("p (t h) -> p t h", t=TT)
            for m in range(TT):
                ts = slice(m * P, (m + 1) * P)
                if m:
                    dve.wait_ge(oat_ps, m)
                dve.tensor_tensor(d_x[:, :, :], bc_mid(tri[:, :], HA), bc_last(gdt[:, m, :], P), ALU.mult).then_inc(rb_ready, 1)
                dve.tensor_tensor(d_c[:, :, :], bc_mid(ident[:, :], HA), bc_last(bta[:, m, :], P), ALU.mult).then_inc(rb_ready, 1)
                dve.wait_ge(rb_ps, 2 * m + 1)
                for h in range(HA):
                    ins = dve.scalar_tensor_tensor(d_dec[:, h, :], bank4(2)[:, h, :], gT[:, m, h:h + 1], negm[:, :],
                                                   ALU.subtract, ALU.add)
                ins.then_inc(dec_in, 1)
                dve.wait_ge(kk_ps, 2 * m + 1)
                dve.wait_ge(dec_done, m + 1)
                if m:
                    dve.wait_ge(oa_hi_done, m)
                    dve.wait_ge(oa_lo_done, m)
                link(dve.tensor_tensor(d_lt[:, :, :], bank4(4), d_dec[:, :, :], ALU.mult))
                dve.wait_ge(rb_ps, 2 * m + 2)
                link(dve.tensor_tensor(d_lt[:, :, :], d_lt[:, :, :], bank4(3), ALU.mult))
                link(dve.tensor_tensor(d_x[:, :, :], d_lt[:, :, :], bc_mid(lvl[:, 0, :], HA), ALU.mult))
                dve.tensor_tensor(d_invT[:, :, :], bc_mid(ident[:, :], HA), d_x[:, :, :], ALU.subtract).then_inc(inv0, 1)
                dve.wait_ge(kk_ps, 2 * m + 2)
                dve.tensor_tensor(d_kq[:, :, :], bank4(5), d_dec[:, :, :], ALU.mult)
                dve.wait_ge(egb_done, m + 1)
                dve.tensor_tensor(d_qd[:, :, :], fm[:, 0:HA, ts], d_qd[:, :, :], ALU.mult).then_inc(qd_done, 1)
                dve.wait_ge(kv_ps, 2 * m + 1)
                dve.tensor_tensor(d_k[:, :, :], bank4(6), bc_last(bexp[:, m, :], P), ALU.mult)
                dve.tensor_tensor(d_kd[:, :, :], bank4(6), bc_last(kds[:, m, :], P), ALU.mult)
                dve.wait_ge(kv_ps, 2 * m + 2)
                dve.tensor_tensor(d_v[:, :, :], bank4(7), bc_last(bta[:, m, :], P), ALU.mult).then_inc(kbv_done, 1)
                dve.wait_ge(inv0, m + 1)
                dve.wait_ge(inv0_copied, m + 1)
                for l in range(1, 6):
                    if l > 1:
                        dve.wait_ge(x_ps, 5 * m + l - 1)
                    dve.tensor_tensor(d_c[:, :, :], d_lt[:, :, :], bc_mid(lvl[:, l, :], HA), ALU.mult).then_inc(ct_done, 1)
                    dve.wait_ge(de_ps, 5 * m + l)
                    if l < 5:
                        dve.tensor_tensor(d_inv[:, :, :], d_inv[:, :, :], bank4(3), ALU.subtract)
                    dve.tensor_tensor(d_invT[:, :, :], d_invT[:, :, :], bank4(4), ALU.subtract).then_inc(de_done, 1)
                    dve.wait_ge(de_done, 5 * m + l)
                dve.wait_ge(wu_done, m + 1)
                for c in range(2):
                    r = slice(CHUNK * c, CHUNK * (c + 1))
                    j = 2 * m + c
                    dve.wait_ge(ws_ps, j + 1)
                    dve.tensor_tensor(d_x[r, :, :], d_v[r, :, :], bank4(2)[r, :, :], ALU.subtract).then_inc(vn_done, 1)
                    dve.wait_ge(ds_ps, j + 1)
                    for h in range(HA):
                        ins = dve.scalar_tensor_tensor(d_s[:, h, :], d_s[:, h, :], cdec[:, c, m, h:h + 1], bank4(3)[:, h, :],
                                                       ALU.mult, ALU.add)
                    ins.then_inc(s_done, 1)
                dve.wait_ge(o_ps, m + 1)
                link(dve.tensor_copy(d_c[:, :, :], bank4(7)))
                link(dve.tensor_tensor(d_dec[:, :, :], d_c[:, :, :], d_c[:, :, :], ALU.mult))
                link(dve.tensor_reduce(osq[:, :], d_dec[:, :, :], AX.X, ALU.add))
                link(dve.tensor_scalar(osq[:, :], osq[:, :], 1.0 / DA, EPS, ALU.mult, ALU.add))
                rsqrt(osq[:, :], ors[:, :])
                dve.tensor_tensor(d_c[:, :, :], d_c[:, :, :], bc_last(ors[:, :], P), ALU.mult).then_inc(on_done, 1)
                dve.wait_ge(oat_ps, m + 1)
                dve.scalar_tensor_tensor(d_lt[:, :, :], bank4(4), cols[:, 56:57], fm[:, 12:16, ts],
                                         ALU.mult, ALU.mult).then_inc(oaf_done, 1)
                dve.wait_ge(oa_hi_done, m + 1)
                dve.tensor_tensor(oa_lo[:, :, ts], d_lt[:, :, :], oa_hi[:, :, ts].bitcast(F32), ALU.subtract).then_inc(oa_lo_done, 1)

            for u in range(UNITS_PROJ, UNITS_PROJ + 2):
                split_lo(u)
            for j in range(4):
                split_lo(UNITS_PROJ + 2 + 3 * j)
                split_lo(UNITS_PROJ + 3 + 3 * j)
                for r in range(4):
                    h = r % 2
                    dve.wait_ge(mg_ps, 8 * j + 4 + r + 1)
                    dve.wait_ge(sg_done, 4 * j + r + 1)
                    if r < 2:
                        dve.tensor_tensor(prod[:, h, :], sg[:, r, :], ps[4 + r][:, :], ALU.mult).then_inc(mul_done, 1)
                    else:
                        if j:
                            dve.wait_ge(mg_hi, 2 * j)
                        link(dve.tensor_tensor(mrg[:, h, :], sg[:, r, :], ps[4 + r][:, :], ALU.mult))
                        dve.wait_ge(mul_done, 4 * j + h + 1)
                        dve.tensor_tensor(mrg[:, h, :], mrg[:, h, :], prod[:, h, :], ALU.add).then_inc(mul_done, 1)
                for r in range(2):
                    dve.wait_ge(mg_hi, 2 * j + r + 1)
                    dve.tensor_tensor(m_lo[:, 2 * j + r, :], mrg[:, r, :], m_hi[:, 2 * j + r, :].bitcast(F32),
                                      ALU.subtract).then_inc(mg_lo, 1)
                split_lo(UNITS_PROJ + 4 + 3 * j)
            for u in range(UNITS_PRE - 2, UNITS_PRE):
                split_lo(u)
            dve.wait_ge(x2_in, 16)
            for n_ in range(2):
                dve.wait_ge(out_used, 2 * n_ + 2)
                for t in range(TT):
                    o = y[:, t, 512 * n_:512 * (n_ + 1)]
                    dve.tensor_tensor(o, o, ps[4 * n_ + t][:, :], ALU.add).then_inc(y_done, 1)

            def token_rms(done):
                dve.wait_ge(done, TT)
                link(dve.tensor_scalar(ssq[:, :], ssq[:, :], 1.0 / D, EPS, ALU.mult, ALU.add))
                rsqrt(ssq[:, :], rst[:, :])

            token_rms(ssq2)
            for t in range(TT):
                dve.tensor_scalar(tx[:, t, :, :], y[:, t, :].rearrange("p (c k) -> p k c", k=KT), rst[:, t:t + 1], None,
                                  ALU.mult).then_inc(t_scaled, 1)
            for k in range(1, KT, 2):
                dve.wait_ge(tt_ps, k + 1)
                dve.tensor_scalar(hf[:, k, :], ps[1][:, :], nffn[:, k:k + 1], None, ALU.mult).then_inc(hf_dve, 1)
            for t in range(TT):
                dve.wait_ge(th_done, t + 1)
                dve.tensor_tensor(tl[:, t, :, :], tx[:, t, :, :], th[:, t, :, :].bitcast(F32), ALU.subtract).then_inc(tl_done, 1)

            def one_hot(oh, v, vmax, key, done=None):
                link(dve.tensor_tensor(key, v, bc_last(vmax, EG), ALU.is_equal))
                link(dve.tensor_tensor(key, key, bc_mid(prio[:, :], TT), ALU.mult))
                link(dve.tensor_reduce(kmx[:, :], key, AX.X, ALU.max))
                ins = dve.tensor_tensor(oh, key, bc_last(kmx[:, :], EG), ALU.is_equal)
                if done is None:
                    link(ins)
                else:
                    ins.then_inc(done, 1)
                    dve.wait_ge(done, 1)

            dve.wait_ge(idx_rows, 1)
            dve.tensor_copy(slot_q[:, :], slot_qi[:, :])
            dve.tensor_copy(row[:, :], row_i[:, :]).then_inc(tok_added, 2)
            dve.wait_ge(lgf_ps, 1)
            dve.tensor_copy(lgf[:, :], ps[2][0:NG + NE, :]).then_inc(lgf_done, 1)
            dve.wait_ge(lg_ps, 1)
            link(dve.tensor_tensor(lg[:, :, :], ps[3][:, 0:TT * (NG + NE)].rearrange("p (t c) -> p t c", t=TT),
                                   bc_mid(brg[:, :], TT), ALU.add))
            gl = lg[:, :, 0:NG]
            link(dve.tensor_reduce(gmx[:, :], gl, AX.X, ALU.max))
            dve.tensor_tensor(gex[:, :, :], gl, bc_last(gmx[:, :], NG), ALU.subtract).then_inc(gd_in, 1)
            one_hot(goh[:, :, :], gl, gmx[:, :], gkey[:, :, :], goh_done)
            dve.wait_ge(rank_ps, 1)
            dve.tensor_copy(rank[:, :, :], ps[5][:, 0:16].rearrange("p (t g) -> p t g", t=TT))
            link(dve.tensor_copy(tot[:, :, :], ps[5][:, 16:32].rearrange("p (t g) -> p t g", t=TT)))
            for t in range(1, TT):
                link(dve.tensor_tensor(tot[:, t, :], tot[:, t, :], tot[:, t - 1, :], ALU.add))
            dve.tensor_tensor(rank[:, 1:, :], rank[:, 1:, :], tot[:, 0:TT - 1, :], ALU.add)
            link(dve.tensor_tensor(over[:, :, :], bc_last(tot[:, TT - 1, :], NG), bc_mid(tile_n[:, :], NG), ALU.is_gt))
            link(dve.tensor_reduce(need[:, :], over[:, :, :], AX.X, ALU.add))
            link(dve.tensor_copy(ends[:, :], need[:, :]))
            for g in range(1, NG):
                link(dve.tensor_tensor(ends[:, g:g + 1], ends[:, g:g + 1], ends[:, g - 1:g], ALU.add))
            link(dve.tensor_tensor(past[:, :, :], bc_last(slot_n[:, :], NG), bc_mid(ends[:, :], SLOTS + 1), ALU.is_ge))
            link(dve.tensor_reduce(gsl[:, :], past[:, :, :], AX.X, ALU.add))
            dve.tensor_scalar(first_e[:, :], gsl[:, :], float(NG - 1), float(EG), ALU.min, ALU.mult).then_inc(slots_done, 1)
            link(dve.tensor_tensor(base[:, :], ends[:, :], need[:, :], ALU.subtract))
            link(dve.scalar_tensor_tensor(ppos[:, :, :], bc_mid(base[:, :], TT), float(P), rank[:, :, :], ALU.mult, ALU.add))
            link(dve.tensor_tensor(ppos[:, :, :], ppos[:, :, :], goh[:, :, :], ALU.mult))
            link(dve.tensor_reduce(pos[:, :], ppos[:, :, :], AX.X, ALU.add))
            link(dve.scalar_tensor_tensor(pos_s[:, :, :], bc_mid(slot_n[:, 0:SLOTS], TT), -float(P), bc_last(pos[:, :], SLOTS),
                                          ALU.mult, ALU.add))
            for t in range(TT):
                dve.tensor_tensor(perm[:, t, :, :], bc_mid(row[:, :], SLOTS), bc_last(pos_s[:, t, :], P),
                                  ALU.is_equal).then_inc(perm_done, 1)
            dve.tensor_tensor(dpos[:, :, :], bc_mid(ident[:, :], TT), bc_last(pos[:, :], P), ALU.mult).then_inc(dpos_done, 1)
            for t in range(TT):
                ins = dve.tensor_tensor(eprod[:, NG * t:NG * (t + 1), :], lg[:, t, NG:].rearrange("p (g e) -> p g e", g=NG),
                                        bc_last(goh[:, t, :], EG), ALU.mult)
            link(ins)
            link(dve.tensor_reduce(ig[:, :, :], eprod[:, :, :].rearrange("p (t g) e -> p t e g", t=TT), AX.X, ALU.add))
            link(dve.tensor_reduce(m1[:, :], ig[:, :, :], AX.X, ALU.max))
            one_hot(e1[:, :, :], ig[:, :, :], m1[:, :], ekey[:, :, :])
            link(dve.scalar_tensor_tensor(ig[:, :, :], e1[:, :, :], NEG, ig[:, :, :], ALU.mult, ALU.add))
            link(dve.tensor_reduce(m2[:, :], ig[:, :, :], AX.X, ALU.max))
            dve.tensor_tensor(dif[:, :], m2[:, :], m1[:, :], ALU.subtract).then_inc(ed_in, 1)
            one_hot(e2[:, :, :], ig[:, :, :], m2[:, :], ekey[:, :, :])
            dve.wait_ge(gd_out, 1)
            link(dve.tensor_reduce(gsm[:, :], gex[:, :, :], AX.X, ALU.add))
            link(dve.reciprocal(gp[:, :], gsm[:, :]))
            dve.wait_ge(ed_out, 1)
            link(dve.tensor_scalar(w1[:, :], dif[:, :], 1.0, None, ALU.add))
            link(dve.reciprocal(w1[:, :], w1[:, :]))
            link(dve.tensor_tensor(w1[:, :], w1[:, :], gp[:, :], ALU.mult))
            link(dve.tensor_tensor(w2[:, :], w1[:, :], dif[:, :], ALU.mult))
            link(dve.tensor_tensor(ce[:, :, :], e1[:, :, :], bc_last(w1[:, :], EG), ALU.mult))
            link(dve.tensor_tensor(ce2[:, :, :], e2[:, :, :], bc_last(w2[:, :], EG), ALU.mult))
            dve.tensor_tensor(ce[:, :, :], ce[:, :, :], ce2[:, :, :], ALU.add).then_inc(cw_in, 1)
            for i in range(1, 2 * KT, 2):
                dve.wait_ge(xs_ps, i + 1)
                dve.tensor_scalar(xs[:, i // 2, HALF:], ps[6][:, 0:HALF], nffn[:, i // 2:i // 2 + 1], None,
                                  ALU.mult).then_inc(xs_dve, 1)

            def split_in_lo(s):
                dve.wait_ge(xs_hi_done, s + 1)
                dve.tensor_tensor(xs_lo[:, :, :], xs[:, :, bass.ds(P * s, P)], xs_hi[:, :, :].bitcast(F32),
                                  ALU.subtract).then_inc(xs_lo_done, 1)

            def split_expert_lo(kind, s, j):
                slot, _, count = place(kind, s, j)
                dve.wait_ge(ehi_done, count)
                if kind == KIND_D:
                    dst, hi, src = dn_lo[:, :, :], dn_hi[:, :, :], eraw[slot][:, :].rearrange("p (f d) -> p f d", f=2)
                else:
                    dst, hi, src = gu_lo[j % 2][:, kind, :, :], gu_hi[j % 2][:, kind, :, :], kv_(eraw[slot])
                dve.tensor_tensor(dst, src, hi.bitcast(F32), ALU.subtract).then_inc(elo_done, 1)

            split_expert_lo(KIND_G, 0, 0)
            split_in_lo(0)
            split_expert_lo(KIND_U, 0, 0)
            dve.wait_ge(cw_ps, 1)
            dve.tensor_copy(cws[:, :, :], ps[1][:, 0:SLOTS * EG].rearrange("p (s e) -> p s e", e=EG)).then_inc(cw_done, 1)
            split_expert_lo(KIND_G, 0, 1)
            split_expert_lo(KIND_U, 0, 1)

            def slot_out_lo(s):
                for n_ in range(2):
                    dve.wait_ge(os_hi_done, 2 * s + n_ + 1)
                    dve.tensor_tensor(os_lo[:, n_, :], ps[3 + n_][:, :], os_hi[:, n_, :].bitcast(F32),
                                      ALU.subtract).then_inc(os_lo_done, 1)

            def from_slot(s):
                dve.wait_ge(posb_done, 1)
                dve.tensor_scalar(slot_q[:, :], slot_q[:, :], float(P), None, ALU.add).then_inc(slot_q_done, 1)
                dve.wait_ge(slot_q_done, s + 1)
                dve.tensor_scalar(back[:, :], posb[:, :], slot_q[:, 0:1], None, ALU.is_equal).then_inc(back_done, 1)

            def add_tokens(s, t):
                for n_ in range(2):
                    dve.wait_ge(un_ps, 8 * s + 2 * t + n_ + 1)
                    o = y[:, t, S * n_:S * (n_ + 1)]
                    dve.tensor_tensor(o, o, ps[5 + n_][:, :], ALU.add).then_inc(tok_added, 1)

            def slot_dve(s):
                dve.wait_ge(cw_done, 1)
                if not is_first(s):
                    dve.wait_ge(hid_done, EG * s)
                dve.tensor_copy(cwe[:, :], cws[:, bass.ds(s, 1), :].rearrange("p s e -> p (s e)")).then_inc(cwe_done, 1)
                dve.wait_ge(cwe_done, s + 1)
                for j in range(EG):
                    i = EG * s + j
                    dve.wait_ge(gsilu, i + 1)
                    if not (is_first(s) and j < 2):
                        dve.wait_ge(hidt_ps, i - 1)
                    dve.scalar_tensor_tensor(ea[j % 2][:, :], eg[:, :], cwe[:, j:j + 1], ps[j % 2][:, FF:],
                                             ALU.mult, ALU.mult).then_inc(hid_done, 1)
                    if j == 0 and not is_first(s):
                        slot_out_lo(s - 1)
                        from_slot(s - 1)
                    split_expert_lo(KIND_D, s, j)
                    dve.wait_ge(hid_hi, i + 1)
                    dve.tensor_tensor(ea_lo[:, :, :], tbank(j)[:, 0:FF].rearrange("p (f c) -> p f c", f=2),
                                      ea_hi[:, :, :].bitcast(F32), ALU.subtract).then_inc(hid_lo, 1)
                    if j < 2 or not is_last(s):
                        split_expert_lo(KIND_G, s, j + 2)
                        if j == 2:
                            split_in_lo(s + 1)
                        split_expert_lo(KIND_U, s, j + 2)
                    if not is_first(s):
                        add_tokens(s - 1, j)

            slot_dve(0)
            with dve.Fori(1, SLOTS - 1) as s:
                slot_dve(s)
            slot_dve(SLOTS - 1)
            slot_out_lo(SLOTS - 1)
            from_slot(SLOTS - 1)
            for t in range(TT):
                add_tokens(SLOTS - 1, t)
            token_rms(ssq3)
            dve.wait_ge(nfin_in, 16)
            for t in range(TT):
                dve.scalar_tensor_tensor(out_t[:, t, :], y[:, t, :], rst[:, t:t + 1], nfin[:, :],
                                         ALU.mult, ALU.mult).then_inc(fin_done, 1)

        @block.tensor
        def _(pe):
            def three(out_ap, lhs_hi, lhs_lo, rhs_hi, rhs_lo, first, last):
                pe.matmul(out_ap, lhs_hi, rhs_hi, start=first, stop=False)
                pe.matmul(out_ap, lhs_hi, rhs_lo, start=False, stop=False)
                return pe.matmul(out_ap, lhs_lo, rhs_hi, start=False, stop=last)

            pe.wait_ge(consts, 1)
            pe.wait_ge(small_in, 192)
            pe.transpose(ps[7][:, 0:57], rows[:, :], ident[0:57, 0:57]).then_inc(rows_ps, 1)
            for k in range(KT):
                if k >= 2:
                    pe.wait_ge(ht_lo, k - 1)
                for t in range(TT):
                    pe.wait_ge(x_scaled, t + 1)
                    ins = pe.transpose(ps[k % 2][:, t * P:(t + 1) * P], x[:, t, k * P:(k + 1) * P], ident[:, :])
                ins.then_inc(ht_ps, 1)
            pe.wait_ge(ht_lo, KT)
            pe.wait_ge(ba_lo_done, 1)
            for k in range(KT):
                ins = three(ps[4][0:8, :], ba_hi[:, k, :], ba_lo[:, k, :], h_hi[:, k, :], h_lo[:, k, :],
                            k == 0, k == KT - 1)
            ins.then_inc(ba_ps, 1)
            pe.wait_ge(ba_f_done, 1)
            for t in range(TT):
                ins = pe.transpose(ps[5][:, 8 * t:8 * t + 8], ba_f[:, t * P:(t + 1) * P], ident[0:8, 0:8])
            ins.then_inc(ba_ps, 1)

            def sum_squares(i):
                pe.wait_ge(sq_done, i + 1)
                if i >= 2:
                    pe.wait_ge(root_done, i - 1)
                pe.matmul(ps[2 + i % 2][:, :], ones[:, :], sqb[i % 2][:, :], start=True, stop=True).then_inc(norm_ps, 1)

            for i in range(ITEMS):
                u, half = i // 2, i % 2
                hi = whi[u % RING][:, :].rearrange("p (k n) -> p k n", k=KT)
                lo = wlo[u % RING][:, :].rearrange("p (k n) -> p k n", k=KT)
                pe.wait_ge(lo_done, u + 1)
                if i >= 2:
                    pe.wait_ge(proj_evac, i - 1)
                bank = ps[i % 2]
                for k in range(KT):
                    wh, wl = (w[:, k, 128 * half:128 * half + 128] for w in (hi, lo))
                    ins = three(bank[:, :], wh, wl, h_hi[:, k, :], h_lo[:, k, :], k == 0, k == KT - 1)
                ins.then_inc(proj_ps, 1)
                for j in norms_at(i):
                    sum_squares(j)


            pe.wait_ge(proj_evac, ITEMS)
            for t in range(TT):
                ins = pe.transpose(bank4(4)[:, t, :], v_f[:, t * P:(t + 1) * P], ident[:, :])
            ins.then_inc(vt_ps, 1)
            for a_ in range(2 * TT):
                m, g = a_ // 2, a_ % 2
                d = slice(DB * g, DB * (g + 1))
                c0 = CHUNK if m else P
                if a_:
                    pe.wait_ge(max_done, a_)
                for h in range(GRP):
                    o = ps[h // 2][:, 256 * (h % 2) + c0:256 * (h % 2) + 256]
                    ins = pe.matmul(o, qb[d, h, m * P:(m + 1) * P], kb[d, m * P - P + c0:(m + 1) * P],
                                    start=True, stop=True)
                ins.then_inc(sc_ps, 1)
                pe.wait_ge(exp_done, a_ + 1)
                for half in range(2):
                    if half == 1 or m:
                        if a_ > 2 and half == 0:
                            pe.wait_ge(pt_prev, a_ - 2)
                        if a_ and half == 1:
                            pe.wait_ge(pt_cur, a_)
                        for h in range(GRP):
                            ins = pe.transpose(bank4(2 + half)[:, h, :], pb[:, h, half * P:(half + 1) * P], ident[:, :])
                        ins.then_inc(pt_ps, 1 if m else 2)
                if m:
                    pe.wait_ge(pt_prev, a_ - 1)
                pe.wait_ge(pt_cur, a_ + 1)
                pe.wait_ge(vb_done, 1)
                if a_:
                    pe.wait_ge(ob_ready, a_)
                for h in range(GRP):
                    o = ps[4][:, DB * h:DB * (h + 1)]
                    if m:
                        pe.matmul(o, pt[:, 0, h, :], vb[:, m - 1, d], start=True, stop=False)
                    ins = pe.matmul(o, pt[:, 1, h, :], vb[:, m, d], start=not m, stop=True)
                ins.then_inc(pv_ps, 1)
                if g == 1:
                    pe.wait_ge(ob_ready, a_ + 1)
                    if m:
                        pe.wait_ge(ob_lo_done, m)
                    for k in range(4):
                        ins = pe.transpose(bank4(5)[:, k, :], ob_t[:, 2 * k:2 * k + 2, :], ident[:, :])
                    ins.then_inc(obt_ps, 1)

            pe.wait_ge(gates_done, 2)
            pe.wait_ge(norm_done, NORM_ITEMS)
            pe.wait_ge(ob_lo_done, TT)
            g_all = gdt[:, :, :].rearrange("p t h -> p (t h)")
            pe.matmul(ps[5][:, 0:16], tri[:, :], g_all, start=True, stop=True)
            pe.matmul(ps[5][:, 16:32], blk[:, :], g_all, start=True, stop=True)
            for c in range(2):
                r = slice(CHUNK * c, CHUNK * (c + 1))
                o = ps[5 + c][:, 32 + 16 * c:48 + 16 * c]
                ins = pe.matmul(o, ones[r, :],
                                gdt[r, :, :].rearrange("p t h -> p (t h)"), start=True, stop=True)
            ins.then_inc(gsum_ps, 1)
            pe.wait_ge(gsum_sub, 1)
            for m in range(TT):
                ts = slice(m * P, (m + 1) * P)
                pe.wait_ge(rb_ready, 2 * m + 1)
                pe.matmul(ps[2][:, :], ones[:, :], d_x[:, :, :], start=True, stop=True).then_inc(rb_ps, 1)
                pe.wait_ge(rb_ready, 2 * m + 2)
                if m:
                    pe.wait_ge(s_done, 2 * m)
                pe.matmul(ps[3][:, :], ones[:, :], d_c[:, :, :], start=True, stop=True).then_inc(rb_ps, 1)
                if m:
                    pe.wait_ge(oaf_done, m)
                for h in range(HA):
                    ins = pe.matmul(bank4(4)[:, h, :], fm[:, HA + h, ts], fm[:, HA + h, ts], start=True, stop=True)
                ins.then_inc(kk_ps, 1)
                for h in range(HA):
                    ins = pe.matmul(bank4(5)[:, h, :], fm[:, HA + h, ts], fm[:, h, ts], start=True, stop=True)
                ins.then_inc(kk_ps, 1)
                for w in range(2):
                    if w and m:
                        pe.wait_ge(on_done, m)
                    for h in range(HA):
                        ins = pe.transpose(bank4(6 + w)[:, h, :], fm[:, HA * (w + 1) + h, ts], ident[:, :])
                    ins.then_inc(kv_ps, 1)
                pe.wait_ge(inv0, m + 1)
                for h in range(HA):
                    ins = pe.transpose(bank4(2)[:, h, :], d_invT[:, h, :], ident[:, :])
                ins.then_inc(inv0_ps, 1)
                pe.wait_ge(inv0_copied, m + 1)
                for l in range(1, 6):
                    if l > 1:
                        pe.wait_ge(de_done, 5 * m + l - 1)
                    pe.wait_ge(ct_done, 5 * m + l)
                    for h in range(HA):
                        ins = pe.matmul(bank4(2)[:, h, :], d_c[:, h, :], d_inv[:, h, :], start=True, stop=True)
                    ins.then_inc(x_ps, 1)
                    pe.wait_ge(xs_done, 5 * m + l)
                    if l < 5:
                        for h in range(HA):
                            pe.matmul(bank4(3)[:, h, :], d_invT[:, h, :], d_x[:, h, :], start=True, stop=True)
                    for h in range(HA):
                        ins = pe.matmul(bank4(4)[:, h, :], d_x[:, h, :], d_invT[:, h, :], start=True, stop=True)
                    ins.then_inc(de_ps, 1)
                pe.wait_ge(de_done, 5 * m + 5)
                pe.wait_ge(kbv_done, m + 1)
                pe.wait_ge(qd_done, m + 1)
                for h in range(HA):
                    pe.matmul(bank4(5)[:, h, :], d_k[:, h, :], d_invT[:, h, :], start=True, stop=True)
                for h in range(HA):
                    ins = pe.matmul(bank4(6)[:, h, :], d_invT[:, h, :], d_v[:, h, :], start=True, stop=True)
                ins.then_inc(wu_ps, 1)
                pe.wait_ge(wu_done, m + 1)
                for c in range(2):
                    r = slice(CHUNK * c, CHUNK * (c + 1))
                    j = 2 * m + c
                    pe.wait_ge(s_zero, 1)
                    if j:
                        pe.wait_ge(s_done, j)
                    for h in range(HA):
                        ins = pe.matmul(bank4(2)[r, h, :], d_k[:, h, r], d_s[:, h, :], start=True, stop=True)
                    ins.then_inc(ws_ps, 1)
                    pe.wait_ge(vn_done, j + 1)
                    for h in range(HA):
                        pe.matmul(bank4(7)[r, h, :], d_qd[:, h, r], d_s[:, h, :], start=True, stop=False)
                        ins = pe.matmul(bank4(7)[r, h, :], d_kq[r, h, r], d_x[r, h, :], start=False, stop=True)
                    if c == 1:
                        ins.then_inc(o_ps, 1)
                    for h in range(HA):
                        ins = pe.matmul(bank4(3)[:, h, :], d_kd[r, h, :], d_x[r, h, :], start=True, stop=True)
                    ins.then_inc(ds_ps, 1)
                pe.wait_ge(on_done, m + 1)
                for h in range(HA):
                    ins = pe.transpose(bank4(4)[:, h, :], d_c[:, h, :], ident[:, :])
                ins.then_inc(oat_ps, 1)


            for j in range(4):
                for r in range(8):
                    c, half = min(r // 2, 2), r % 2
                    u = UNITS_PROJ + 3 * j + c
                    hi, lo = kv_(whi[u % RING]), kv_(wlo[u % RING])
                    cs = slice(128 * half, 128 * half + 128)
                    pe.wait_ge(lo_done, u + 1)
                    if j:
                        pe.wait_ge(sg_done if r < 4 else mul_done, 4 * (j - 1) + r % 4 + 1)
                    if r < 4:
                        for k in range(KT):
                            ins = three(ps[r][:, :], hi[:, k, cs], lo[:, k, cs], h_hi[:, k, :], h_lo[:, k, :],
                                        k == 0, k == KT - 1)
                    else:
                        xh, xl = (oa_hi, oa_lo) if r < 6 else (ob_hi, ob_lo)
                        if j == 0:
                            pe.wait_ge(oa_lo_done, TT)
                        for k in range(4):
                            kk = k + (0 if r < 6 else 4)
                            ins = three(ps[r][:, :], hi[:, kk, cs], lo[:, kk, cs], xh[:, k, :], xl[:, k, :], k == 0, k == 3)
                    ins.then_inc(mg_ps, 1)
            pe.wait_ge(mg_lo, KT)
            for n_ in range(2):
                for kh in range(2):
                    u = UNITS_PROJ + UNITS_MERGE + 2 * n_ + kh
                    hi, lo = (w[u % RING][:, :].rearrange("p (k n) -> p k n", k=4) for w in (whi, wlo))
                    pe.wait_ge(lo_done, u + 1)
                    if kh == 0:
                        pe.wait_ge(mul_done if n_ else sg_done, 16)
                    for t in range(TT):
                        ts = slice(t * P, (t + 1) * P)
                        for k in range(4):
                            kk = 4 * kh + k
                            ins = three(ps[4 * n_ + t][:, :], m_hi[:, kk, ts], m_lo[:, kk, ts], hi[:, k, :], lo[:, k, :],
                                        kk == 0, kk == KT - 1)
                    ins.then_inc(out_used, 1)
            pe.wait_ge(y_done, 8)
            for k in range(KT):
                if k >= 2:
                    pe.wait_ge((hf_act, hf_dve)[k % 2], k // 2)
                for t in range(TT):
                    pe.wait_ge(t_scaled, t + 1)
                    ins = pe.transpose(ps[k % 2][:, t * P:(t + 1) * P], tx[:, t, k, :], ident[:, :])
                ins.then_inc(tt_ps, 1)
            for k in range(KT):
                pe.wait_ge((hf_act, hf_dve)[k % 2], k // 2 + 1)
                ins = pe.matmul(ps[2][0:NG + NE, :], rw_raw[:, k, :], hf[:, k, :], start=k == 0, stop=k == KT - 1)
            ins.then_inc(lgf_ps, 1)
            pe.wait_ge(lgf_done, 1)
            for t in range(TT):
                ins = pe.transpose(ps[3][:, (NG + NE) * t:(NG + NE) * (t + 1)], lgf[:, t * P:(t + 1) * P],
                                   ident[0:NG + NE, 0:NG + NE])
            ins.then_inc(lg_ps, 1)
            pe.wait_ge(goh_done, 1)
            g_all = goh[:, :, :].rearrange("p t g -> p (t g)")
            pe.matmul(ps[5][:, 0:16], before[:, :], g_all, start=True, stop=True)
            pe.matmul(ps[5][:, 16:32], ones[:, :], g_all, start=True, stop=True).then_inc(rank_ps, 1)
            pe.wait_ge(tl_done, TT)
            for i in range(2 * KT):
                k, half = divmod(i, 2)
                if i >= 2:
                    pe.wait_ge((xs_act, xs_dve)[half], k)
                for t in range(TT):
                    pe.wait_ge(perm_done, t + 1)
                    to = perm[:, t, :, :].rearrange("p s q -> p (s q)")[:, HALF * half:HALF * (half + 1)]
                    o = ps[(4, 6)[half]][:, 0:HALF]
                    pe.matmul(o, th[:, t, k, :], to, start=t == 0, stop=False)
                    ins = pe.matmul(o, tl[:, t, k, :], to, start=False, stop=t == TT - 1)
                ins.then_inc(xs_ps, 1)
                if i == 1:
                    pe.wait_ge(dpos_done, 1)
                    pe.matmul(ps[3][:, :], ones[:, :], dpos[:, :, :].rearrange("p t c -> p (t c)"),
                              start=True, stop=True).then_inc(posb_ps, 1)
            pe.wait_ge(cw_in, 1)
            for s in range(SLOTS):
                for t in range(TT):
                    ins = pe.matmul(ps[1][:, EG * s:EG * (s + 1)], perm[:, t, s, :].bitcast(F32), ce[:, t, :],
                                    start=t == 0, stop=t == TT - 1)
            ins.then_inc(cw_ps, 1)

            def gate_up(s, j, ks):
                b = j % 2
                for k in ks:
                    ins = three(ps[b][:, :], xs_hi[:, k, :], xs_lo[:, k, :], gu_hi[b][:, :, k, :], gu_lo[b][:, :, k, :],
                                k == 0, k == KT - 1)
                if ks[-1] == KT - 1:
                    ins.then_inc(gu_ps, 1)

            def hidden_f(s, j):
                pe.wait_ge(hid_done, EG * s + j + 1)
                for f in range(2):
                    ins = pe.transpose(tbank(j)[:, P * f:P * (f + 1)], ea[j % 2][:, P * f:P * (f + 1)], ident[:, :])
                ins.then_inc(hidt_ps, 1)

            def to_tokens(s, t):
                pe.wait_ge(back_done, s + 1)
                pe.wait_ge(os_lo_done, 2 * s + 2)
                for n_ in range(2):
                    pe.wait_ge(tok_added, 8 * s + 2 * t + n_ + 1)
                    pe.matmul(ps[5 + n_][:, :], back[:, P * t:P * (t + 1)], os_hi[:, n_, :], start=True, stop=False)
                    pe.matmul(ps[5 + n_][:, :], back[:, P * t:P * (t + 1)], os_lo[:, n_, :],
                              start=False, stop=True).then_inc(un_ps, 1)

            def slot_pe(s):
                for j in range(EG):
                    i = EG * s + j
                    if j == EG - 1 and is_last(s):
                        hidden_f(s, j)
                    else:
                        pe.wait_ge(elo_done, place(KIND_U, s, j + 1)[2])
                        if not (is_first(s) and j == 0):
                            pe.wait_ge(hid_done, i)
                        if j == EG - 1:
                            pe.wait_ge(xs_lo_done, s + 2)
                        gate_up(s, j + 1, range(0, KT // 2))
                        hidden_f(s, j)
                        gate_up(s, j + 1, range(KT // 2, KT))
                    pe.wait_ge(elo_done, place(KIND_D, s, j)[2])
                    pe.wait_ge(hid_lo, i + 1)
                    if j == 0 and not is_first(s):
                        pe.wait_ge(os_lo_done, 2 * s)
                    for n_ in range(2):
                        ns = slice(S * n_, S * (n_ + 1))
                        for f in range(2):
                            ins = three(ps[3 + n_][:, :], ea_hi[:, f, :], ea_lo[:, f, :], dn_hi[:, f, ns], dn_lo[:, f, ns],
                                        j == 0 and f == 0, j == EG - 1 and f == 1)
                    ins.then_inc(dn_ps, 1)
                    if not is_first(s):
                        to_tokens(s - 1, j)

            pe.wait_ge(elo_done, 2)
            pe.wait_ge(xs_lo_done, 1)
            gate_up(0, 0, range(KT))
            pe.wait_ge(cw_done, 1)
            slot_pe(0)
            with pe.Fori(1, SLOTS - 1) as s:
                slot_pe(s)
            slot_pe(SLOTS - 1)
            for t in range(TT):
                to_tokens(SLOTS - 1, t)


_INS = ["x", "norm_mix_w", "w_in", "conv_w", "a_log", "dt_bias", "delta_norm_w", "sinks", "w_out_a", "w_out_b",
        "w_out", "norm_ffn_w", "w_router_group", "b_router_group", "w_router_expert", "b_router_expert",
        "w_gate", "w_up", "w_down", "norm_final_w"]


def kernel(**inputs):
    import concourse.bacc as bacc
    from concourse.bass_utils import run_bass_kernel_spmd

    nc = bacc.Bacc("TRN2", target_bir_lowering=False, num_devices=1)
    arrays, args = {}, {}
    for name in _INS:
        arr = np.ascontiguousarray(inputs[name])
        arrays[f"in_{name}"] = arr
        args[name] = nc.dram_tensor(f"in_{name}", arr.shape, mybir.dt.from_np(arr.dtype), kind="ExternalInput").ap()
    out = nc.dram_tensor("out_y", (1, S, D), F32, kind="ExternalOutput").ap()
    build(nc, args, out)
    r = run_bass_kernel_spmd(nc, [arrays], core_ids=[0])
    return r.results[0]["out_y"]
```

```python
from contextlib import ExitStack

import numpy as np

import concourse.bass as bass
from concourse import mybir

F32 = mybir.dt.float32
F32R = mybir.dt.float32r
ALU = mybir.AluOpType
ACT = mybir.ActivationFunctionType
AX = mybir.AxisListType

P = 128
D = 1024
S = 512
KT = D // P
TT = S // P
CHUNK = 64
HA, DA = 4, 128
KEYS_A = HA * DA
CONV = 3 * KEYS_A
TAPS = 4
HB, DB = 8, 64
KVB = 2
GRP = HB // KVB
WIN = 3 * CHUNK
NG, EG = 4, 4
NE = NG * EG
FF = 256
EPS = 1e-6
NEG = -1.0e30

C_Z = CONV
C_BA = C_Z + KEYS_A
C_QB = C_BA + 2 * HA
C_KV = C_QB + HB * DB
C_GA = C_KV + 2 * KVB * DB
C_GB = C_GA + D

U = 2048
RING = 2
U_SIDE = 9
U_BRANCH = U_SIDE + 2 + 8
U_OUT = U_BRANCH + 4
UNITS_PRE = U_OUT + 4
ITEMS = 2 * U_SIDE
Z_ITEMS = KEYS_A // P
SIDE_ITEMS = 2 * (U_BRANCH - U_SIDE)
CONV_ITEMS = CONV // P
NORM_ITEMS = 2 * HA
KIND_G, KIND_U, KIND_D = 0, 1, 2
SLOTS = (S + NG * (P - 1)) // P
EXPERT_RING = 8
UH = U // 2
HALF = SLOTS * P // 2


def build(nc, a, out):
    ctx = ExitStack()
    cursor = [16512]

    def at(name, shape, dt, offset):
        return nc.alloc_sbuf_tensor_at(name, shape, dt, offset=offset)

    def region(nbytes):
        o = cursor[0]
        cursor[0] += (nbytes + 31) // 32 * 32
        return o

    def new(name, shape, dt=F32):
        return at(name, shape, dt, region(int(np.prod(shape[1:])) * 4))

    with ctx:
        def sem(name):
            return ctx.enter_context(nc.semaphore(name))

        raw = [new(f"w_raw{i}", [P, U]) for i in range(RING)]
        whi = [new(f"w_hi{i}", [P, U], F32R) for i in range(RING)]
        wlo = [new(f"w_lo{i}", [P, U], F32R) for i in range(RING)]
        r_g = region(4 * 3 * 4 * S)
        r_h = region(4 * 2 * KT * S)
        h_hi = at("h_hi", [P, KT, S], F32R, r_h)
        h_lo = at("h_lo", [P, KT, S], F32R, r_h + 4 * KT * S)
        m_hi = at("merged_hi", [P, KT, S], F32R, r_h)
        m_lo = at("merged_lo", [P, KT, S], F32R, r_h + 4 * KT * S)
        r_main = region(4 * 2 * KT * S)
        fm = at("conv_z_F", [P, 16, S], F32, r_main)
        oa_hi = at("oA_hi", [P, 4, S], F32R, r_main + 4 * 4 * S)
        oa_lo = at("oA_lo", [P, 4, S], F32R, r_main)
        r_b = region(4 * (6 * S))
        qb = at("attn_q_F", [P, 4, S], F32, r_b)
        kb = at("attn_k_F", [P, S], F32, r_b + 4 * 4 * S)
        vb = at("attn_v_T", [P, TT, P], F32, r_b + 4 * 5 * S)
        r_tmp = region(4 * 3584)
        r_x = region(4 * TT * D)
        x = at("x_T", [P, TT, D], F32, r_x)
        gt = [at(f"gates_F{j}", [P, 4, S], F32, r_g + 4 * 4 * S * j if j < 3 else r_x) for j in range(4)]
        r_o = region(4 * TT * D + 64)
        ob_hi = at("oB_hi", [P, 4, S], F32R, r_o)
        ob_lo = at("oB_lo", [P, 4, S], F32R, r_o + 4 * 4 * S)
        y = at("y_T", [P, TT, D], F32, r_x)
        xpad = [at(f"conv_in{i}", [P, S + 8], F32, r_o + i * 4 * (S + 8)) for i in range(2)]
        cacc = [at(f"conv_acc{i}", [P, S], F32, r_o + 4160 + i * 4 * S) for i in range(2)]
        v_f = cacc[0]
        sqb = [at(f"square{i}", [P, S], F32, r_o + 8256 + i * 4 * S) for i in range(2)]
        rsb = [at(f"norm_factor{i}", [P, S], F32, r_o + 12352 + i * 2048) for i in range(2)]
        junk = at("square_junk", [P, D], F32, r_tmp)
        junk_f = at("square_junk_final", [P, D], F32, r_main)
        rows = at("small_rows", [57, P], F32, r_tmp + 4096)
        ba_raw = at("ba_raw", [P, KT, 8], F32, r_tmp + 4608)
        ba_hi = at("ba_hi", [P, KT, 8], F32R, r_tmp + 4864)
        ba_lo = at("ba_lo", [P, KT, 8], F32R, r_tmp + 5120)
        ba_t = at("ba_T", [P, TT, 8], F32, r_tmp + 5376)
        ba_f = at("ba_F", [8, S], F32, r_tmp + 6144)
        ga1 = at("decay_in", [P, TT, HA], F32, r_tmp + 5504)
        ga2 = at("decay_abs", [P, TT, HA], F32, r_tmp + 5568)
        ga3 = at("decay_exp", [P, TT, HA], F32, r_tmp + 5632)
        dist_i = at("key_distance_i", [P, WIN], mybir.dt.int32, r_tmp + 8192)
        dist = at("key_distance", [P, WIN], F32, r_tmp + 8960)
        dist_m = at("key_distance_abs", [P, WIN], F32, r_tmp + 9728)
        wmask = at("window_mask", [P, WIN], F32, r_tmp + 10496)
        ob_t = at("attn_out_T", [P, HB, DB], F32, r_tmp + 11264)
        mxs, nmx, esk, sms, den = ([at(f"{n_}{i}", [P, GRP], F32, r_tmp + 13312 + 64 * q + 32 * i) for i in range(2)]
                                   for q, n_ in enumerate(("score_max", "score_max_neg", "sink_term", "prob_sum", "prob_norm")))
        bias = at("alibi_bias", [P, HB, WIN], F32, r_x)
        pb = [at(f"probs{i}", [P, GRP, 2 * P], F32, o) for i, o in enumerate((r_x + 6144, r_tmp))]
        pt = at("probs_F", [P, 2, GRP, P], F32, r_x + 10240)
        dn = [at(f"dn{i}", [P, HA, P], F32, r_b + 2048 * i) for i in range(12)]
        (d_dec, d_lt, d_qd, d_kq, d_k, d_v, d_kd, d_inv, d_invT, d_x, d_c, d_s) = dn
        prod = at("gated_A", [P, 2, S], F32, r_b + 4 * 4 * S)
        mrg = at("merged", [P, 2, S], F32, r_tmp)
        ffn_raw = 16512
        tx = at("ffn_in_T", [P, TT, KT, P], F32, ffn_raw)
        th = at("ffn_in_T_hi", [P, TT, KT, P], F32R, ffn_raw + 65536)
        tl = at("ffn_in_T_lo", [P, TT, KT, P], F32R, ffn_raw + 81920)
        perm = at("to_slots", [P, TT, SLOTS, P], F32R, ffn_raw + 98304)
        hf = at("ffn_in_F", [P, KT, S], F32, ffn_raw + 114688)
        lgf = at("router_logits_F", [NG + NE, S], F32, r_o)
        dpos = at("pos_diagonal", [P, TT, P], F32, r_o + 2048)
        eraw = [at(f"ew_raw{i}", [P, UH], F32, ffn_raw + 4096 * i) for i in range(EXPERT_RING)]
        gu_hi = [at(f"gate_up_hi{i}", [P, 2, KT, FF], F32R, ffn_raw + 32768 * (i + 1)) for i in range(2)]
        gu_lo = [at(f"gate_up_lo{i}", [P, 2, KT, FF], F32R, ffn_raw + 32768 * (i + 1) + 16384) for i in range(2)]
        dn_hi = at("down_hi", [P, 2, D], F32R, ffn_raw + 98304)
        dn_lo = at("down_lo", [P, 2, D], F32R, ffn_raw + 106496)
        xs = at("slot_tokens_F", [P, KT, SLOTS * P], F32, ffn_raw + 114688)
        xs_hi = at("slot_in_hi", [P, KT, P], F32R, ffn_raw + 143360)
        xs_lo = at("slot_in_lo", [P, KT, P], F32R, ffn_raw + 147456)
        eg = at("gate_silu", [P, FF], F32, ffn_raw + 151552)
        ea = [at(f"hidden_T{i}", [P, FF], F32, ffn_raw + 152576 + 1024 * i) for i in range(2)]
        ea_hi = at("hidden_hi", [P, 2, P], F32R, ffn_raw + 154624)
        ea_lo = at("hidden_lo", [P, 2, P], F32R, ffn_raw + 155648)
        nfin = at("norm_final_b", [P, D], F32, ffn_raw + 156672)
        assert ffn_raw + 160768 <= r_x
        os_hi = at("slot_out_hi", [P, 2, S], F32R, r_o)
        os_lo = at("slot_out_lo", [P, 2, S], F32R, r_o + 4096)
        posb = at("position_rows", [P, S], F32, r_o + 8192)
        back = at("from_slot", [P, S], F32R, r_o + 10240)
        out_t = at("out_T", [P, TT, D], F32, ffn_raw)
        rt_at = [r_o + 12288]

        def rt(name, shape):
            o = rt_at[0]
            rt_at[0] += (int(np.prod(shape[1:])) * 4 + 31) // 32 * 32
            return at(name, shape, F32, o)

        lg = rt("router_logits", [P, TT, NG + NE])
        gmx, gsm, gp = rt("group_max", [P, TT]), rt("group_sum", [P, TT]), rt("group_prob", [P, TT])
        gex, gkey, goh = rt("group_exp", [P, TT, NG]), rt("group_key", [P, TT, NG]), rt("group_onehot", [P, TT, NG])
        kmx = rt("key_max", [P, TT])
        eprod = rt("group_logits", [P, TT * NG, EG])
        ig, ekey = rt("in_group", [P, TT, EG]), rt("expert_key", [P, TT, EG])
        e1, e2 = rt("first_onehot", [P, TT, EG]), rt("second_onehot", [P, TT, EG])
        m1, m2, dif, w1, w2 = (rt(n_, [P, TT]) for n_ in ("first_logit", "second_logit", "logit_gap", "first_weight", "second_weight"))
        ce, ce2 = rt("in_group_weights", [P, TT, EG]), rt("in_group_weights2", [P, TT, EG])
        ident = new("ident", [P, P])
        ones = new("ones", [P, P])
        tri = new("tri", [P, P])
        negm = new("neg_mask", [P, P])
        blk = new("same_chunk", [P, P])
        lvl = new("level_masks", [P, 6, P])
        cols = new("small_cols", [P, 57])
        nffn = new("norm_ffn_cols", [P, KT])
        ssq = new("sum_squares", [P, TT])
        rst = new("rms_factor", [P, TT])
        rsq_i = new("rsqrt_seed", [P, TT], mybir.dt.int32)
        rsq_t = new("rsqrt_tmp", [P, TT])
        epsb = new("eps", [P, 1])
        bta = new("beta_T", [P, TT, HA])
        gdt = new("log_decay_T", [P, TT, HA])
        alog = new("a_log_b", [P, HA])
        dtb = new("dt_bias_b", [P, HA])
        ealog = new("exp_a_log", [P, HA])
        gsum = new("decay_sums_T", [P, 4, TT * HA])
        gexp = new("exp_G", [P, TT, HA])
        kds = new("exp_Gend_minus_G", [P, TT, HA])
        cdec = new("chunk_decay", [P, 2, TT, HA])
        bexp = new("beta_exp_G", [P, TT, HA])
        osq = new("out_square_sum", [P, HA])
        ors = new("out_rms_factor", [P, HA])
        sinkb = new("sinks_b", [P, HB])
        rw_raw = new("router_raw", [P, KT, NG + NE])
        prio = new("index_priority", [P, EG])
        before = new("earlier_tokens", [P, P])
        row_i = new("index_row_i", [P, P], mybir.dt.int32)
        row = new("index_row", [P, P])
        slot_qi = new("slot_position_i", [P, 1], mybir.dt.int32)
        slot_q = new("slot_position", [P, 1])
        slot_n = new("slot_numbers", [P, SLOTS + 1])
        tile_n = new("tile_thresholds", [P, NG])
        rank = new("rank_in_tile", [P, TT, NG])
        tot = new("tile_counts", [P, TT, NG])
        over = new("count_over", [P, NG, NG])
        need = new("slots_of_group", [P, NG])
        ends = new("slot_ends", [P, NG])
        base = new("slot_bases", [P, NG])
        ppos = new("position_terms", [P, TT, NG])
        pos = new("position", [P, TT])
        pos_s = new("position_in_slot", [P, TT, SLOTS])
        past = new("slots_past", [P, SLOTS + 1, NG])
        gsl = new("group_of_slot", [P, SLOTS + 1])
        first_e = new("first_expert_of_slot", [P, SLOTS + 1], mybir.dt.int32)
        cws = new("slot_weights", [P, SLOTS, EG])
        cwe = new("this_slot_weights", [P, EG])
        brg = new("router_bias", [P, NG + NE])

        assert cursor[0] <= 229368, cursor[0]

        ps = [ctx.enter_context(nc.psum_tensor(f"bank{i}", [P, S], F32)) for i in range(8)]

        x_in = [sem(f"x_in{t}") for t in range(TT)]
        small_in = sem("small_in")
        raw_in = [sem(f"raw_in{i}") for i in range(RING)]
        dve_step, act_step, pool_step = sem("dve_step"), sem("act_step"), sem("pool_step")
        consts = sem("consts_ready")
        eps_set = sem("eps_set")
        hi_done, lo_done = sem("w_hi_done"), sem("w_lo_done")
        ssq_done, x_scaled = sem("ssq_done"), sem("x_scaled")
        rows_ps, cols_done = sem("rows_ps"), sem("cols_done")
        ht_ps, ht_hi, ht_lo = sem("ht_ps"), sem("ht_hi"), sem("ht_lo")
        pad_zero = sem("pad_zero")
        ba_hi_done, ba_lo_done, ba_ps, ba_copied = sem("ba_hi_done"), sem("ba_lo_done"), sem("ba_ps"), sem("ba_copied")
        ba_f_done, vt_ps, vb_done = sem("ba_F_done"), sem("attn_v_T_ps"), sem("attn_v_done")
        proj_ps, proj_evac = sem("proj_ps"), sem("proj_evac")
        side_ps, side_evac, z_done = sem("side_ps"), sem("side_evac"), sem("z_silu_done")
        conv_done, silu_done, sq_done = sem("conv_done"), sem("silu_done"), sem("sq_done")
        norm_ps, root_done, norm_done = sem("norm_ps"), sem("root_done"), sem("norm_done")
        gd_abs, gd_exp, gd_ln, gates_done = sem("gd_abs"), sem("gd_exp"), sem("gd_ln"), sem("gates_done")
        dist_set = sem("dist_set")
        sc_ps, max_done, exp_done = sem("scores_ps"), sem("max_done"), sem("probs_exp")
        pt_ps, pt_prev, pt_cur = sem("probsF_ps"), sem("probsF_prev"), sem("probsF_cur")
        pv_ps, ob_ready, obt_ps = sem("pv_ps"), sem("attn_out_T_ready"), sem("attn_out_F_ps")
        ob_hi_done, ob_lo_done = sem("oB_hi_done"), sem("oB_lo_done")
        gsum_ps, gsum_sub, gexp_done, dscal_done = sem("gsum_ps"), sem("gsum_sub"), sem("gexp_done"), sem("dscal_done")
        rb_ready, rb_ps, dec_in = sem("row_source"), sem("row_bcast_ps"), sem("decay_arg")
        egb_done, dec_done = sem("exp_G_rows"), sem("decay_done")
        kk_ps, kv_ps, qd_done, kbv_done = sem("kk_ps"), sem("kv_T_ps"), sem("q_decayed"), sem("kv_scaled")
        inv0, inv0_ps, inv0_copied = sem("inv_T_first"), sem("inv_first_ps"), sem("inv_first")
        ct_done, x_ps, xs_done, de_ps, de_done = (sem("level_block"), sem("block_inv_ps"), sem("block_inv"),
                                                  sem("inv_update_ps"), sem("inv_updated"))
        wu_ps, wu_done, u_done = sem("wu_ps"), sem("w_done"), sem("u_done")
        s_zero, ws_ps, vn_done, o_ps, ds_ps, s_done = (sem("state_zero"), sem("w_state_ps"), sem("v_new"),
                                                       sem("o_ps"), sem("state_add_ps"), sem("state_done"))
        osq_done, on_done, oat_ps, oaf_done = sem("o_square_sums"), sem("o_normed"), sem("oA_F_ps"), sem("oA_F_gated")
        oa_hi_done, oa_lo_done = sem("oA_hi_done"), sem("oA_lo_done")
        mg_ps, sg_done, mul_done = sem("merge_ps"), sem("gate_sigmoid"), sem("gate_product")
        mg_hi, mg_lo = sem("merged_hi_done"), sem("merged_lo_done")
        x2_in, out_used, y_done = sem("x_again"), sem("out_proj_ps"), sem("residual_done")
        ssq2, t_scaled, tt_ps, hf_act, hf_dve = sem("ssq2"), sem("ffn_scaled"), sem("ffn_F_ps"), sem("ffn_F_even"), sem("ffn_F_odd")
        th_done, tl_done = sem("ffn_T_hi"), sem("ffn_T_lo")
        lgf_ps, lgf_done, lg_ps = sem("router_F_ps"), sem("router_F_done"), sem("router_ps")
        gd_in, gd_out, ed_in, ed_out = (sem("group_arg"), sem("group_exp_done"), sem("pair_arg"), sem("pair_exp_done"))
        idx_rows, goh_done, rank_ps, slots_done = sem("index_rows"), sem("group_onehot_done"), sem("rank_ps"), sem("slots_known")
        perm_done, dpos_done, posb_ps, posb_done = sem("to_slots_done"), sem("pos_diagonal_done"), sem("pos_rows_ps"), sem("pos_rows_done")
        cw_in, cw_ps, cw_done = sem("weights_known"), sem("slot_weights_ps"), sem("slot_weights_done")
        xs_ps, xs_act, xs_dve = sem("slot_tokens_ps"), sem("slot_tokens_even"), sem("slot_tokens_odd")
        eraw_in = [sem(f"ew_raw_in{i}") for i in range(EXPERT_RING)]
        ehi_done, elo_done = sem("ew_hi_done"), sem("ew_lo_done")
        xs_hi_done, xs_lo_done = sem("slot_in_hi_done"), sem("slot_in_lo_done")
        gu_ps, gsilu, hid_done, hidt_ps = sem("gate_up_ps"), sem("gate_silu_done"), sem("hidden_done"), sem("hidden_F_ps")
        hid_hi, hid_lo, dn_ps = sem("hidden_hi_done"), sem("hidden_lo_done"), sem("down_ps")
        os_hi_done, os_lo_done = sem("slot_out_hi_done"), sem("slot_out_lo_done")
        back_done, un_ps, tok_added = sem("from_slot_done"), sem("to_tokens_ps"), sem("y_added")
        cwe_done, slot_q_done = sem("this_slot_weights_done"), sem("slot_position_set")
        fin_done, stored = sem("final_done"), sem("stored")

        w_in = a["w_in"][0].rearrange("(k p) n -> p k n", p=P)

        def unit_sources(u):
            r = raw[u % RING][:, :].rearrange("p (k n) -> p k n", k=KT)
            if u < 6:
                return [(r, w_in[:, :, 256 * u:256 * (u + 1)])]
            if u < 8:
                q = w_in[:, :, C_QB:C_QB + HB * DB].rearrange("p k (g j c) -> p k j g c", g=KVB, j=GRP)
                return [(r[:, :, 128 * i + 64 * g:128 * i + 64 * g + 64], q[:, :, 2 * (u - 6) + i, g, :])
                        for i in range(2) for g in range(KVB)]
            if u < U_BRANCH:
                v = u - U_SIDE
                if v < 0:
                    o = C_KV
                elif v < 2:
                    o = C_Z + 256 * v
                else:
                    o = (C_GA, C_GB)[v % 2] + 256 * ((v - 2) // 2)
                return [(r, w_in[:, :, o:o + 256])]
            if u < U_OUT:
                cs = slice(256 * (u - U_BRANCH), 256 * (u - U_BRANCH + 1))
                return [(r[:, 0:4, :], a["w_out_a"][0].rearrange("(k p) n -> p k n", p=P)[:, :, cs]),
                        (r[:, 4:8, :], a["w_out_b"][0].rearrange("(k p) n -> p k n", p=P)[:, :, cs])]
            n_, kh = divmod(u - U_OUT, 2)
            return [(raw[u % RING][:, :].rearrange("p (k n) -> p k n", k=4),
                     a["w_out"][0].rearrange("(k p) n -> p k n", p=P)[:, 4 * kh:4 * kh + 4, 512 * n_:512 * (n_ + 1)])]

        def unit_dmas(u):
            return len(unit_sources(u))

        def raw_value(u):
            return 16 * sum(unit_dmas(v) for v in range(u % RING, u + 1, RING))

        def bc_mid(ap, n):
            return ap.unsqueeze(1).broadcast_to([ap.shape[0], n, ap.shape[1]])

        def bc_last(ap, n):
            return ap.unsqueeze(2).broadcast_to([ap.shape[0], ap.shape[1], n])

        def bank4(i):
            return ps[i][:, :].rearrange("p (h c) -> p h c", h=4)

        def side_bank(f):
            return ps[f % 2 + (6 if f < Z_ITEMS else 0)]

        def branch_bank(j, r):
            return ps[4 * ((j + 1) % 2) + r]

        def tbank(j):
            return ps[7] if j % 2 else ps[2]

        block = ctx.enter_context(nc.Block())

        def out_count(n_, kh, t=TT - 1):
            return (TT + 1) * n_ + (t + 2 if kh else 1)

        def wait_used(eng, v):
            if v < U_SIDE:
                eng.wait_ge(proj_ps, 2 * (v + 1))
            elif v < U_BRANCH:
                eng.wait_ge(side_ps, 2 * (v - U_SIDE + 1))
            elif v < U_OUT:
                eng.wait_ge(mg_ps, 4 * (v - U_BRANCH + 1))
            else:
                eng.wait_ge(out_used, out_count(*divmod(v - U_OUT, 2)))

        def place(kind, s, j, half=1):
            c = {KIND_G: 3 * j - 1, KIND_U: 3 * j, KIND_D: 3 * j + 4}[kind]
            if isinstance(s, int) and s == 0 and j == 0 and kind != KIND_D:
                c += 1
            if isinstance(s, int) and s == SLOTS - 1 and j == EG - 1 and kind == KIND_D:
                c -= 2
            c = 2 * c + half
            return c % EXPERT_RING, 3 * s + (c // EXPERT_RING + 1), 24 * s + (c + 1)

        def halves(gu, kind):
            return [gu[:, kind, KT // 2 * h:KT // 2 * (h + 1), :].rearrange("p k f -> p (k f)") for h in range(2)]

        def is_first(s):
            return isinstance(s, int) and s == 0

        def is_last(s):
            return isinstance(s, int) and s == SLOTS - 1

        w_gate_v = a["w_gate"][0].rearrange("e (p k) f -> e p (k f)", p=P)
        w_up_v = a["w_up"][0].rearrange("e (p k) f -> e p (k f)", p=P)
        w_down_v = a["w_down"][0].rearrange("e (f p) d -> e p f d", p=P)
        kv_ = lambda r: r[:, :].rearrange("p (k n) -> p k n", k=KT)

        def norms_at(i):
            behind = (6, 8, 10, 12, 13, 14, 15, 16)
            return [behind.index(i)] if i in behind else []

        @block.sync
        def _(sp):
            for t in range(TT):
                sp.dma_start(x[:, t, :], a["x"][0, t * P:(t + 1) * P, :]).then_inc(x_in[t], 16)
            sp.dma_start(rows[0:8, :], a["norm_mix_w"][0].rearrange("(k p) -> k p", p=P)).then_inc(small_in, 16)
            sp.dma_start(rows[8:56, :], a["conv_w"][0].rearrange("j (i p) -> (j i) p", p=P)).then_inc(small_in, 16)
            sp.dma_start(rows[56:57, :], a["delta_norm_w"]).then_inc(small_in, 16)
            sp.dma_start(ba_raw[:, :, :], w_in[:, :, C_BA:C_BA + 8]).then_inc(small_in, 16)
            sp.dma_start(dtb[:, :], a["dt_bias"].to_broadcast([P, HA])).then_inc(small_in, 16)
            sp.dma_start(alog[:, :], a["a_log"].to_broadcast([P, HA])).then_inc(small_in, 16)
            sp.dma_start(sinkb[:, :], a["sinks"].to_broadcast([P, HB])).then_inc(small_in, 16)
            sp.dma_start(brg[:, 0:NG], a["b_router_group"].to_broadcast([P, NG])).then_inc(small_in, 16)
            sp.dma_start(brg[:, NG:], a["b_router_expert"].to_broadcast([P, NE])).then_inc(small_in, 16)
            sp.dma_start(nffn[:, :], a["norm_ffn_w"][0].rearrange("(p k) -> p k", k=KT)).then_inc(small_in, 16)
            sp.dma_start(rw_raw[:, :, 0:NG], a["w_router_group"][0].rearrange("(p k) n -> p k n", k=KT)).then_inc(small_in, 16)
            sp.dma_start(rw_raw[:, :, NG:], a["w_router_expert"][0].rearrange("(p k) n -> p k n", k=KT)).then_inc(small_in, 16)
            for u in range(UNITS_PRE):
                if u >= RING:
                    sp.wait_ge(hi_done, u - RING + 1)
                    sp.wait_ge(lo_done, u - RING + 1)
                for dst, src in unit_sources(u):
                    sp.dma_start(dst, src).then_inc(raw_in[u % RING], 16)
            sp.wait_ge(mul_done, 16)
            sp.dma_start(y[:, :, :], a["x"][0].rearrange("(t p) d -> p t d", p=P)).then_inc(x2_in, 16)
            sp.dma_start(nfin[:, :], a["norm_final_w"].rearrange("(o d) -> o d", o=1).to_broadcast([P, D])).then_inc(x2_in, 16)

            sp.wait_ge(slots_done, 1)

            def first_expert(s):
                return sp.value_load(first_e[0:1, bass.ds(s, 1)], min_val=0, max_val=NE - EG)

            def load(kind, s, j, e):
                for half in range(2):
                    slot, _, count = place(kind, s, j, half)
                    if not (is_first(s) and count <= EXPERT_RING):
                        sp.wait_ge(elo_done, count - EXPERT_RING)
                    src = (w_gate_v, w_up_v, w_down_v)[kind][e]
                    src = src[:, half, :] if kind == KIND_D else src[:, UH * half:UH * (half + 1)]
                    sp.dma_start(eraw[slot][:, :], src).then_inc(eraw_in[slot], 16)

            def slot_loads(s):
                e0 = first_expert(s)
                if is_first(s):
                    load(KIND_G, 0, 0, e0)
                    load(KIND_U, 0, 0, e0)
                for j in range(EG - 1):
                    load(KIND_G, s, j + 1, e0 + (j + 1))
                    load(KIND_U, s, j + 1, e0 + (j + 1))
                    load(KIND_D, s, j, e0 + j)
                if not is_last(s):
                    e1 = first_expert(s + 1)
                    load(KIND_G, s, EG, e1)
                    load(KIND_U, s, EG, e1)
                load(KIND_D, s, EG - 1, e0 + (EG - 1))

            slot_loads(0)
            with sp.Fori(1, SLOTS - 1) as s:
                slot_loads(s)
            slot_loads(SLOTS - 1)
            for t in range(TT):
                sp.wait_ge(fin_done, t + 1)
                sp.dma_start(out[0, t * P:(t + 1) * P, :], out_t[:, t, :]).then_inc(stored, 16)
            sp.wait_ge(stored, 16 * TT)

        @block.gpsimd
        def _(pool):
            n = [0]

            def link(ins):
                n[0] += 1
                ins.then_inc(pool_step, 1)
                pool.wait_ge(pool_step, n[0])

            nc.gpsimd.memset(ones[:, :], 1.0)
            nc.gpsimd.memset(blk[:, :], 0.0)
            nc.gpsimd.memset(tri[:, :], 1.0)
            nc.gpsimd.memset(lvl[:, :, :], 1.0)
            link(nc.gpsimd.memset(ident[:, :], 0.0))
            link(nc.gpsimd.affine_select(out=ident[:, :], in_=ident[:, :], compare_op=ALU.not_equal, fill=1.0,
                                         base=0, pattern=[[-1, P]], channel_multiplier=1))
            link(nc.gpsimd.memset(blk[0:64, 0:64], 1.0))
            link(nc.gpsimd.memset(blk[64:128, 64:128], 1.0))
            link(nc.gpsimd.affine_select(out=tri[:, :], in_=tri[:, :], compare_op=ALU.is_ge, fill=0.0,
                                         base=0, pattern=[[1, P]], channel_multiplier=-1))
            link(nc.gpsimd.affine_select(out=tri[:, 64:128], in_=tri[:, 64:128], compare_op=ALU.is_ge, fill=0.0,
                                         base=-64, pattern=[[0, 64]], channel_multiplier=1))
            for l in range(6):
                b = 1 << l
                m = lvl[:, l, :].rearrange("p (n r) -> p n r", r=2 * b)
                nc.gpsimd.memset(m[:, :, 0:b], 0.0).then_inc(pool_step, 1)
                n[0] += 1
                pool.wait_ge(pool_step, n[0])
                link(nc.gpsimd.affine_select(out=m, in_=m, compare_op=ALU.is_ge, fill=0.0, base=0,
                                             pattern=[[-2 * b, P // (2 * b)], [0, 2 * b]], channel_multiplier=1))
                link(nc.gpsimd.affine_select(out=m, in_=m, compare_op=ALU.is_ge, fill=0.0, base=b - 1,
                                             pattern=[[2 * b, P // (2 * b)], [0, 2 * b]], channel_multiplier=-1))
            nc.gpsimd.tensor_scalar(negm[:, :], tri[:, :], -1.0, -NEG, ALU.add, ALU.mult).then_inc(consts, 1)
            link(nc.gpsimd.iota(dist_i[:, :], pattern=[[-1, WIN]], base=CHUNK, channel_multiplier=1))
            link(nc.gpsimd.memset(wmask[:, :], 0.0))
            nc.gpsimd.memset(wmask[0:64, 128:192], NEG)
            nc.gpsimd.memset(wmask[64:128, 0:64], NEG).then_inc(dist_set, 1)
            pool.wait_ge(dist_set, 1)
            link(nc.gpsimd.memset(before[:, :], 1.0))
            link(nc.gpsimd.affine_select(out=before[:, :], in_=before[:, :], compare_op=ALU.is_gt, fill=0.0,
                                         base=0, pattern=[[1, P]], channel_multiplier=-1))
            for i in range(SLOTS + 1):
                link(nc.gpsimd.memset(slot_n[:, i:i + 1], float(i)))
            for i in range(NG):
                link(nc.gpsimd.memset(tile_n[:, i:i + 1], float(P * i)))
            link(nc.gpsimd.iota(slot_qi[:, :], pattern=[[0, 1]], base=-P, channel_multiplier=1))
            nc.gpsimd.iota(row_i[:, :], pattern=[[1, P]], base=0, channel_multiplier=0).then_inc(idx_rows, 1)

        @block.scalar
        def _(act):
            n = [0]

            def link(ins):
                n[0] += 1
                ins.then_inc(act_step, 1)
                act.wait_ge(act_step, n[0])

            def split_hi(u):
                act.wait_ge(raw_in[u % RING], raw_value(u))
                if u >= RING:
                    wait_used(act, u - RING)
                act.activation(whi[u % RING][:, :], raw[u % RING][:, :], ACT.Copy).then_inc(hi_done, 1)

            act.wait_ge(eps_set, 1)
            for t in range(TT):
                act.wait_ge(x_in[t], 16)
                link(act.activation(junk[:, :], x[:, t, :], ACT.Square, accum_out=ssq[:, t:t + 1]))
                act.activation(rst[:, t:t + 1], ssq[:, t:t + 1], ACT.Sqrt, scale=1.0 / D, bias=epsb[:, :]).then_inc(ssq_done, 1)
            act.wait_ge(small_in, 192)
            act.activation(ba_hi[:, :, :], ba_raw[:, :, :], ACT.Copy).then_inc(ba_hi_done, 1)
            act.wait_ge(cols_done, 1)
            for k in range(KT):
                act.wait_ge(ht_ps, k + 1)
                act.activation(h_hi[:, k, :], ps[k % 2][:, :], ACT.Copy, scale=cols[:, k:k + 1]).then_inc(ht_hi, 1)
            split_hi(0)
            split_hi(1)

            def conv_silu(i):
                act.wait_ge(conv_done, i + 1)
                act.activation(fm[:, i, :], cacc[i % 2][:, :], ACT.Silu).then_inc(silu_done, 1)

            def square(i):
                act.wait_ge(silu_done, i + 1)
                if i >= 2:
                    act.wait_ge(norm_ps, i - 1)
                act.activation(sqb[i % 2][:, :], fm[:, i, :], ACT.Square).then_inc(sq_done, 1)

            def norm_root(i):
                act.wait_ge(norm_ps, i + 1)
                if i >= 2:
                    act.wait_ge(norm_done, i - 1)
                act.activation(rsb[i % 2][:, :], ps[2 + i % 2][:, :], ACT.Sqrt, bias=epsb[:, :]).then_inc(root_done, 1)

            for i in range(ITEMS):
                act.wait_ge(proj_ps, i + 1)
                if i < CONV_ITEMS:
                    act.wait_ge(pad_zero, 2)
                    if i >= 2:
                        act.wait_ge(conv_done, i - 1)
                    act.activation(xpad[i % 2][:, 3:3 + S], ps[i % 2][:, :], ACT.Copy).then_inc(proj_evac, 1)
                elif i < 16:
                    act.activation(qb[:, i - 12, :], ps[i % 2][:, :], ACT.Copy).then_inc(proj_evac, 1)
                elif i == 16:
                    act.activation(kb[:, :], ps[i % 2][:, :], ACT.Copy).then_inc(proj_evac, 1)
                else:
                    act.activation(v_f[:, :], ps[i % 2][:, :], ACT.Copy).then_inc(proj_evac, 1)
                if i % 2 == 1:
                    split_hi((i - 1) // 2 + 2)
                if 1 <= i <= CONV_ITEMS:
                    conv_silu(i - 1)
                if i == CONV_ITEMS:
                    act.wait_ge(ba_copied, 1)
                    act.activation(bta[:, :, :], ba_t[:, :, 0:HA], ACT.Sigmoid).then_inc(gates_done, 1)
                    act.activation(ealog[:, :], alog[:, :], ACT.Exp).then_inc(gd_exp, 1)
                    act.wait_ge(gd_abs, 1)
                    link(act.activation(ga3[:, :, :], ga2[:, :, :], ACT.Exp, scale=-1.0))
                    act.activation(ga2[:, :, :], ga3[:, :, :], ACT.Ln, bias=1.0).then_inc(gd_ln, 1)
                for j in norms_at(i):
                    norm_root(j)
                for j in norms_at(i + 1):
                    square(j)
            act.wait_ge(vt_ps, 1)
            act.activation(vb[:, :, :], bank4(4), ACT.Copy).then_inc(vb_done, 1)


            def side_copy(f):
                act.wait_ge(side_ps, f + 1)
                if f < Z_ITEMS:
                    dst = fm[:, CONV_ITEMS + f, :]
                else:
                    dst = gt[(f - Z_ITEMS) // 4][:, (f - Z_ITEMS) % 4, :]
                act.activation(dst, side_bank(f)[:, :], ACT.Copy).then_inc(side_evac, 1)

            def probs_exp(a_):
                c0, b = CHUNK if a_ >= 2 else P, a_ % 2
                act.wait_ge(max_done, a_ + 1)
                for h in range(GRP):
                    act.activation(pb[b][:, h, c0:], pb[b][:, h, c0:], ACT.Exp, bias=nmx[b][:, h:h + 1],
                                   accum_out=sms[b][:, h:h + 1])
                act.activation(esk[b][:, :], esk[b][:, :], ACT.Exp).then_inc(exp_done, 1)

            probs_exp(0)
            for a_ in range(2 * TT):
                m, g = a_ // 2, a_ % 2
                if m:
                    act.wait_ge(pt_ps, 2 * a_ + 1)
                    if a_ > 2:
                        act.wait_ge(pv_ps, a_)
                    act.activation(pt[:, 0, :, :], bank4(2), ACT.Copy).then_inc(pt_prev, 1)
                if a_ + 1 < 2 * TT:
                    probs_exp(a_ + 1)
                if a_ >= 2 and a_ % 2 == 0:
                    side_copy(a_ // 2 - 1)
                if a_ == 5:
                    split_hi(U_SIDE + 2)
                if g == 1:
                    act.wait_ge(obt_ps, m + 1)
                    act.activation(ob_hi[:, :, m * P:(m + 1) * P], bank4(5), ACT.Copy).then_inc(ob_hi_done, 1)
            side_copy(Z_ITEMS - 1)
            act.wait_ge(side_evac, Z_ITEMS)
            act.activation(fm[:, CONV_ITEMS:, :], fm[:, CONV_ITEMS:, :], ACT.Silu).then_inc(z_done, 1)

            act.wait_ge(gsum_sub, 1)
            act.activation(gexp[:, :, :], gsum[:, 0, :], ACT.Exp)
            act.activation(kds[:, :, :], gsum[:, 1, :], ACT.Exp)
            act.activation(cdec[:, :, :, :], gsum[:, 2:4, :], ACT.Exp).then_inc(gexp_done, 1)
            def decay_exps(m):
                act.wait_ge(dec_in, m + 1)
                if m:
                    act.wait_ge(o_ps, m)
                act.activation(d_qd[:, :, :], bank4(2), ACT.Exp).then_inc(egb_done, 1)
                act.activation(d_dec[:, :, :], d_dec[:, :, :], ACT.Exp).then_inc(dec_done, 1)

            decay_exps(0)
            for m in range(TT):
                act.wait_ge(inv0_ps, m + 1)
                act.activation(d_inv[:, :, :], bank4(2), ACT.Copy).then_inc(inv0_copied, 1)
                for l in range(1, 6):
                    act.wait_ge(x_ps, 5 * m + l)
                    act.activation(d_x[:, :, :], bank4(2), ACT.Copy).then_inc(xs_done, 1)
                    if l == 1:
                        split_hi(U_SIDE + 3 + 2 * m)
                    if l == 2:
                        side_copy(Z_ITEMS + 4 * m)
                    if l == 4:
                        side_copy(Z_ITEMS + 4 * m + 1)
                        split_hi(U_SIDE + 4 + 2 * m)
                act.wait_ge(wu_ps, 2 * m + 1)
                act.activation(d_k[:, :, :], bank4(5), ACT.Copy).then_inc(wu_done, 1)
                act.wait_ge(wu_ps, 2 * m + 2)
                act.activation(d_v[:, :, :], bank4(6), ACT.Copy).then_inc(u_done, 1)
                side_copy(Z_ITEMS + 4 * m + 2)
                act.wait_ge(o_ps, m + 1)
                for h in range(HA):
                    ins = act.activation(d_dec[:, h, :], bank4(7)[:, h, :], ACT.Square, accum_out=osq[:, h:h + 1])
                ins.then_inc(osq_done, 1)
                side_copy(Z_ITEMS + 4 * m + 3)
                if m + 1 < TT:
                    decay_exps(m + 1)
                act.wait_ge(oaf_done, m + 1)
                act.activation(oa_hi[:, :, m * P:(m + 1) * P], d_inv[:, :, :], ACT.Copy).then_inc(oa_hi_done, 1)

            split_hi(U_BRANCH + 1)
            act.wait_ge(side_evac, SIDE_ITEMS)
            for j in range(4):
                act.activation(gt[j][:, :, :], gt[j][:, :, :], ACT.Sigmoid).then_inc(sg_done, 1)
                for r in range(2):
                    act.wait_ge(mul_done, 4 * j + 3 + r)
                    act.activation(m_hi[:, 2 * j + r, :], mrg[:, r, :], ACT.Copy).then_inc(mg_hi, 1)
                split_hi(U_BRANCH + 2 + j)
            for u in range(UNITS_PRE - 2, UNITS_PRE):
                split_hi(u)
            for t in range(TT):
                act.wait_ge(y_done, 4 + t + 1)
                if t:
                    act.wait_ge(ssq2, t)
                act.activation(junk[:, :], y[:, t, :], ACT.Square, accum_out=ssq[:, t:t + 1]).then_inc(ssq2, 1)

            for k in range(0, KT, 2):
                act.wait_ge(tt_ps, k + 1)
                act.activation(hf[:, k, :], ps[0][:, :], ACT.Copy, scale=nffn[:, k:k + 1]).then_inc(hf_act, 1)
            for t in range(TT):
                act.wait_ge(t_scaled, t + 1)
                act.activation(th[:, t, :, :], tx[:, t, :, :], ACT.Copy).then_inc(th_done, 1)
            act.wait_ge(gd_in, 1)
            act.activation(gex[:, :, :], gex[:, :, :], ACT.Exp).then_inc(gd_out, 1)
            act.wait_ge(ed_in, 1)
            act.activation(dif[:, :], dif[:, :], ACT.Exp).then_inc(ed_out, 1)
            def split_in_hi(s):
                act.activation(xs_hi[:, :, :], xs[:, :, bass.ds(P * s, P)], ACT.Copy).then_inc(xs_hi_done, 1)

            def split_expert(kind, s, j):
                if kind == KIND_D:
                    if not (is_first(s) and j == 0):
                        act.wait_ge(dn_ps, EG * s + j)
                    else:
                        act.wait_ge(cw_ps, 1)
                    dst = [dn_hi[:, h, :] for h in range(2)]
                else:
                    if not (is_first(s) and j < 2):
                        act.wait_ge(gu_ps, EG * s + j - 1)
                    dst = halves(gu_hi[j % 2], kind)
                for half in range(2):
                    slot, arrived, _ = place(kind, s, j, half)
                    act.wait_ge(eraw_in[slot], 16 * arrived)
                    act.activation(dst[half], eraw[slot][:, :], ACT.Copy).then_inc(ehi_done, 1)

            act.wait_ge(posb_ps, 1)
            act.activation(posb[:, :], ps[3][:, :], ACT.Copy).then_inc(posb_done, 1)
            for i in range(0, 2 * KT, 2):
                act.wait_ge(xs_ps, i + 1)
                act.activation(xs[:, i // 2, 0:HALF], ps[4][:, 0:HALF], ACT.Copy, scale=nffn[:, i // 2:i // 2 + 1]).then_inc(xs_act, 1)
                if i == 4:
                    split_expert(KIND_G, 0, 0)
                if i == 8:
                    split_expert(KIND_U, 0, 0)

            act.wait_ge(xs_act, KT)
            act.wait_ge(xs_dve, KT)
            split_in_hi(0)
            split_expert(KIND_G, 0, 1)
            split_expert(KIND_U, 0, 1)

            def slot_out_hi(s):
                act.wait_ge(dn_ps, EG * s + EG)
                if not is_first(s):
                    act.wait_ge(un_ps, 8 * s)
                for n_ in range(2):
                    act.activation(os_hi[:, n_, :], ps[3 + n_][:, :], ACT.Copy).then_inc(os_hi_done, 1)

            def slot_act(s):
                for j in range(EG):
                    i = EG * s + j
                    act.wait_ge(gu_ps, i + 1)
                    if not (is_first(s) and j == 0):
                        act.wait_ge(hid_done, i)
                    act.activation(eg[:, :], ps[j % 2][:, 0:FF], ACT.Silu).then_inc(gsilu, 1)
                    if j == 0 and not is_first(s):
                        slot_out_hi(s - 1)
                    split_expert(KIND_D, s, j)
                    act.wait_ge(hidt_ps, i + 1)
                    if not (is_first(s) and j == 0):
                        act.wait_ge(dn_ps, i)
                    act.activation(ea_hi[:, :, :], tbank(j)[:, 0:FF].rearrange("p (f c) -> p f c", f=2),
                                   ACT.Copy).then_inc(hid_hi, 1)
                    if j < 2 or not is_last(s):
                        split_expert(KIND_G, s, j + 2)
                        if j == 2:
                            act.wait_ge(gu_ps, EG * s + EG)
                            split_in_hi(s + 1)
                        split_expert(KIND_U, s, j + 2)

            slot_act(0)
            with act.Fori(1, SLOTS - 1) as s:
                slot_act(s)
            slot_act(SLOTS - 1)
            slot_out_hi(SLOTS - 1)
            for t in range(TT):
                act.wait_ge(tok_added, 8 * (SLOTS - 1) + 2 * t + 4)
                if t:
                    act.wait_ge(ssq2, TT + t)
                act.activation(junk_f[:, :], y[:, t, :], ACT.Square, accum_out=ssq[:, t:t + 1]).then_inc(ssq2, 1)

        @block.vector
        def _(dve):
            n = [0]

            def link(ins):
                n[0] += 1
                ins.then_inc(dve_step, 1)
                dve.wait_ge(dve_step, n[0])

            def split_lo(u):
                s = u % RING
                dve.wait_ge(hi_done, u + 1)
                dve.tensor_tensor(wlo[s][:, :], raw[s][:, :], whi[s][:, :].bitcast(F32), ALU.subtract).then_inc(lo_done, 1)

            dve.memset(epsb[:, :], EPS).then_inc(eps_set, 1)
            for t in range(TT):
                dve.wait_ge(ssq_done, t + 1)
                link(dve.reciprocal(rst[:, t:t + 1], rst[:, t:t + 1]))
                dve.tensor_scalar(x[:, t, :], x[:, t, :], rst[:, t:t + 1], None, ALU.mult).then_inc(x_scaled, 1)
            dve.wait_ge(rows_ps, 1)
            dve.tensor_copy(cols[:, :], ps[7][:, 0:57]).then_inc(cols_done, 1)
            for i in range(EG):
                dve.memset(prio[:, i:i + 1], float(EG - i))
            dve.wait_ge(ba_hi_done, 1)
            dve.tensor_tensor(ba_lo[:, :, :], ba_raw[:, :, :], ba_hi[:, :, :].bitcast(F32), ALU.subtract).then_inc(ba_lo_done, 1)
            dve.wait_ge(cols_done, 1)
            for k in range(KT):
                dve.wait_ge(ht_hi, k + 1)
                dve.scalar_tensor_tensor(h_lo[:, k, :], ps[k % 2][:, :], cols[:, k:k + 1],
                                         h_hi[:, k, :].bitcast(F32), ALU.mult, ALU.subtract).then_inc(ht_lo, 1)
            split_lo(0)
            for i in range(2):
                dve.memset(xpad[i][:, 0:3], 0.0).then_inc(pad_zero, 1)
            dve.wait_ge(ba_ps, 1)
            dve.tensor_copy(ba_f[:, :], ps[4][0:8, :]).then_inc(ba_f_done, 1)
            dve.wait_ge(ba_ps, 2)
            dve.tensor_copy(ba_t[:, :, :], ps[5][:, 0:32].rearrange("p (t c) -> p t c", t=TT)).then_inc(ba_copied, 1)
            split_lo(1)

            def tap(j, i):
                c = KT + j * CONV_ITEMS + i
                return cols[:, c:c + 1]

            def conv(i):
                b = i % 2
                dve.wait_ge(proj_evac, i + 1)
                if i >= 2:
                    dve.wait_ge(silu_done, i - 1)
                link(dve.tensor_scalar(cacc[b][:, :], xpad[b][:, 0:S], tap(0, i), None, ALU.mult))
                for j in range(1, TAPS):
                    ins = dve.scalar_tensor_tensor(cacc[b][:, :], xpad[b][:, j:j + S], tap(j, i), cacc[b][:, :],
                                                   ALU.mult, ALU.add)
                    if j < TAPS - 1:
                        link(ins)
                    else:
                        ins.then_inc(conv_done, 1)

            def l2_norm(i):
                dve.wait_ge(root_done, i + 1)
                r = rsb[i % 2][:, :]
                link(dve.reciprocal(r, r))
                dve.scalar_tensor_tensor(fm[:, i, :], fm[:, i, :], float(DA) ** -0.5 if i < HA else 1.0, r,
                                         ALU.mult, ALU.mult).then_inc(norm_done, 1)

            for i in range(ITEMS):
                if i < CONV_ITEMS:
                    conv(i)
                if i % 2 == 1:
                    split_lo((i - 1) // 2 + 2)
                for j in norms_at(i):
                    l2_norm(j)
                if i == 2:
                    dve.wait_ge(dist_set, 1)
                    link(dve.tensor_copy(dist[:, :], dist_i[:, :]))
                    link(dve.scalar_tensor_tensor(dist_m[:, :], dist[:, :], -1.0, dist[:, :], ALU.mult, ALU.max))
                    for h in range(HB):
                        slope = 2.0 ** (-8.0 * (h + 1) / HB)
                        dve.scalar_tensor_tensor(bias[:, h, :], dist_m[:, :], -slope, wmask[:, :], ALU.mult, ALU.add)
                if i == 4:
                    dve.wait_ge(ba_copied, 1)
                    for t in range(TT):
                        ins = dve.tensor_tensor(ga1[:, t, :], ba_t[:, t, HA:], dtb[:, :], ALU.add)
                    link(ins)
                    dve.scalar_tensor_tensor(ga2[:, :, :], ga1[:, :, :], -1.0, ga1[:, :, :], ALU.mult, ALU.max).then_inc(gd_abs, 1)
                if i == CONV_ITEMS + 1:
                    dve.wait_ge(gd_ln, 1)
                    link(dve.scalar_tensor_tensor(ga3[:, :, :], ga1[:, :, :], 0.0, ga2[:, :, :], ALU.max, ALU.add))
                    dve.wait_ge(gd_exp, 1)
                    for t in range(TT):
                        ins = dve.scalar_tensor_tensor(gdt[:, t, :], ga3[:, t, :], -1.0, ealog[:, :], ALU.mult, ALU.mult)
                    ins.then_inc(gates_done, 1)
            dve.memset(pb[0][:, :, 0:CHUNK], 0.0)
            link(dve.memset(pb[1][:, :, 0:CHUNK], 0.0))

            def score_max(a_):
                g, c0, v = a_ % 2, CHUNK if a_ >= 2 else P, a_ % 2
                heads = slice(GRP * g, GRP * (g + 1))
                dve.wait_ge(sc_ps, a_ + 1)
                if a_ >= 2:
                    dve.wait_ge(pt_ps, 2 * a_ - 2)
                for b in range(2):
                    bank = ps[b][:, :].rearrange("p (h c) -> p h c", h=2)
                    hs = GRP * g + 2 * b
                    ins = dve.scalar_tensor_tensor(pb[v][:, 2 * b:2 * b + 2, c0:], bank[:, :, c0:], DB ** -0.5,
                                                   bias[:, hs:hs + 2, c0 - CHUNK:], ALU.mult, ALU.add)
                link(ins)
                link(dve.tensor_reduce(mxs[v][:, :], pb[v][:, :, c0:], AX.X, ALU.max))
                link(dve.tensor_tensor(mxs[v][:, :], mxs[v][:, :], sinkb[:, heads], ALU.max))
                dve.tensor_scalar(nmx[v][:, :], mxs[v][:, :], -1.0, None, ALU.mult)
                dve.tensor_tensor(esk[v][:, :], sinkb[:, heads], mxs[v][:, :], ALU.subtract).then_inc(max_done, 1)

            def out_lo(m):
                dve.wait_ge(ob_hi_done, m + 1)
                ts = slice(m * P, (m + 1) * P)
                dve.tensor_tensor(ob_lo[:, :, ts], bank4(5), ob_hi[:, :, ts].bitcast(F32), ALU.subtract).then_inc(ob_lo_done, 1)

            score_max(0)
            for a_ in range(2 * TT):
                m, g, v = a_ // 2, a_ % 2, a_ % 2
                heads = slice(GRP * g, GRP * (g + 1))
                if a_ + 1 < 2 * TT:
                    score_max(a_ + 1)
                if g == 0 and m:
                    out_lo(m - 1)
                if a_ == 6:
                    split_lo(U_SIDE + 2)
                dve.wait_ge(pt_ps, 2 * a_ + 2)
                if a_:
                    dve.wait_ge(pv_ps, a_)
                dve.tensor_copy(pt[:, 1, :, :], bank4(3)).then_inc(pt_cur, 1)
                dve.wait_ge(exp_done, a_ + 1)
                link(dve.tensor_tensor(den[v][:, :], sms[v][:, :], esk[v][:, :], ALU.add))
                link(dve.reciprocal(den[v][:, :], den[v][:, :]))
                dve.wait_ge(pv_ps, a_ + 1)
                if g == 0 and m:
                    dve.wait_ge(obt_ps, m)
                dve.tensor_tensor(ob_t[:, heads, :], ps[4][:, 0:GRP * DB].rearrange("p (h c) -> p h c", h=GRP),
                                  bc_last(den[v][:, :], DB), ALU.mult).then_inc(ob_ready, 1)
            out_lo(TT - 1)

            def rsqrt(v, y):
                w = y.shape[1]
                i, t = rsq_i[:, 0:w], rsq_t[:, 0:w]
                link(dve.tensor_scalar(i, v.bitcast(mybir.dt.int32), 1, None, ALU.arith_shift_right))
                link(dve.tensor_scalar(y.bitcast(mybir.dt.int32), i, -1.0, float(0x5F3759DF), ALU.mult, ALU.add))
                for _ in range(3):
                    link(dve.tensor_tensor(t, y, y, ALU.mult))
                    link(dve.scalar_tensor_tensor(t, t, -0.5, v, ALU.mult, ALU.mult))
                    link(dve.scalar_tensor_tensor(y, t, 1.5, y, ALU.add, ALU.mult))

            dve.wait_ge(gsum_ps, 1)
            dve.tensor_copy(gsum[:, 3, :], ps[6][:, 48:64])
            link(dve.tensor_copy(gsum[:, 0:3, :], ps[5][:, 0:48].rearrange("p (a c) -> p a c", a=3)))
            dve.tensor_tensor(gsum[:, 1, :], gsum[:, 1, :], gsum[:, 0, :], ALU.subtract).then_inc(gsum_sub, 1)
            dve.wait_ge(gexp_done, 1)
            link(dve.tensor_tensor(bexp[:, :, :], bta[:, :, :], gexp[:, :, :], ALU.mult))
            dve.memset(d_s[:, :, :], 0.0).then_inc(s_zero, 1)
            gT = gsum[:, 0, :].rearrange("p (t h) -> p t h", t=TT)

            def row_source(m):
                dve.tensor_tensor(d_x[:, :, :], bc_mid(tri[:, :], HA), bc_last(gdt[:, m, :], P), ALU.mult).then_inc(rb_ready, 1)

            def beta_source(m):
                if m:
                    dve.wait_ge(oat_ps, m)
                dve.tensor_tensor(d_c[:, :, :], bc_mid(ident[:, :], HA), bc_last(bta[:, m, :], P), ALU.mult).then_inc(rb_ready, 1)

            def decay_arg(m):
                dve.wait_ge(rb_ps, 2 * m + 1)
                for h in range(HA):
                    ins = dve.scalar_tensor_tensor(d_dec[:, h, :], bank4(2)[:, h, :], gT[:, m, h:h + 1], negm[:, :],
                                                   ALU.subtract, ALU.add)
                ins.then_inc(dec_in, 1)

            row_source(0)
            decay_arg(0)
            beta_source(0)
            for m in range(TT):
                ts = slice(m * P, (m + 1) * P)
                dve.wait_ge(kk_ps, 2 * m + 1)
                dve.wait_ge(dec_done, m + 1)
                link(dve.tensor_tensor(d_lt[:, :, :], bank4(4), d_dec[:, :, :], ALU.mult))
                dve.wait_ge(rb_ps, 2 * m + 2)
                link(dve.tensor_tensor(d_lt[:, :, :], d_lt[:, :, :], bank4(3), ALU.mult))
                link(dve.tensor_tensor(d_x[:, :, :], d_lt[:, :, :], bc_mid(lvl[:, 0, :], HA), ALU.mult))
                dve.tensor_tensor(d_invT[:, :, :], bc_mid(ident[:, :], HA), d_x[:, :, :], ALU.subtract).then_inc(inv0, 1)
                for l in range(1, 6):
                    if l > 1:
                        dve.wait_ge(x_ps, 5 * m + l - 1)
                    dve.tensor_tensor(d_c[:, :, :], d_lt[:, :, :], bc_mid(lvl[:, l, :], HA), ALU.mult).then_inc(ct_done, 1)
                    if l == 1:
                        dve.wait_ge(kk_ps, 2 * m + 2)
                        dve.tensor_tensor(d_kq[:, :, :], bank4(5), d_dec[:, :, :], ALU.mult)
                        dve.wait_ge(egb_done, m + 1)
                        dve.tensor_tensor(d_qd[:, :, :], fm[:, 0:HA, ts], d_qd[:, :, :], ALU.mult).then_inc(qd_done, 1)
                    if l == 2:
                        split_lo(U_SIDE + 3 + 2 * m)
                    if l == 3:
                        dve.wait_ge(kv_ps, 2 * m + 1)
                        dve.tensor_tensor(d_k[:, :, :], bank4(6), bc_last(bexp[:, m, :], P), ALU.mult)
                        dve.tensor_tensor(d_kd[:, :, :], bank4(6), bc_last(kds[:, m, :], P), ALU.mult)
                    if l == 4:
                        dve.wait_ge(kv_ps, 2 * m + 2)
                        dve.tensor_tensor(d_v[:, :, :], bank4(7), bc_last(bta[:, m, :], P), ALU.mult).then_inc(kbv_done, 1)
                    if l == 5:
                        split_lo(U_SIDE + 4 + 2 * m)
                    dve.wait_ge(inv0_copied, m + 1)
                    dve.wait_ge(de_ps, 5 * m + l)
                    if l < 5:
                        dve.tensor_tensor(d_inv[:, :, :], d_inv[:, :, :], bank4(3), ALU.subtract)
                    dve.tensor_tensor(d_invT[:, :, :], d_invT[:, :, :], bank4(4), ALU.subtract).then_inc(de_done, 1)
                    dve.wait_ge(de_done, 5 * m + l)
                for c in range(2):
                    r = slice(CHUNK * c, CHUNK * (c + 1))
                    j = 2 * m + c
                    dve.wait_ge(ws_ps, j + 1)
                    dve.wait_ge(u_done, m + 1)
                    dve.tensor_tensor(d_x[r, :, :], d_v[r, :, :], bank4(2)[r, :, :], ALU.subtract).then_inc(vn_done, 1)
                    dve.wait_ge(ds_ps, j + 1)
                    for h in range(HA):
                        ins = dve.scalar_tensor_tensor(d_s[:, h, :], d_s[:, h, :], cdec[:, c, m, h:h + 1], bank4(3)[:, h, :],
                                                       ALU.mult, ALU.add)
                    ins.then_inc(s_done, 1)
                if m + 1 < TT:
                    row_source(m + 1)
                dve.wait_ge(osq_done, m + 1)
                link(dve.tensor_scalar(osq[:, :], osq[:, :], 1.0 / DA, EPS, ALU.mult, ALU.add))
                rsqrt(osq[:, :], ors[:, :])
                dve.tensor_tensor(d_c[:, :, :], bank4(7), bc_last(ors[:, :], P), ALU.mult).then_inc(on_done, 1)
                if m + 1 < TT:
                    decay_arg(m + 1)
                dve.wait_ge(oat_ps, m + 1)
                dve.wait_ge(z_done, 1)
                dve.scalar_tensor_tensor(d_inv[:, :, :], bank4(6), cols[:, 56:57], fm[:, 12:16, ts],
                                         ALU.mult, ALU.mult).then_inc(oaf_done, 1)
                if m + 1 < TT:
                    beta_source(m + 1)
                dve.wait_ge(oa_hi_done, m + 1)
                dve.tensor_tensor(oa_lo[:, :, ts], d_inv[:, :, :], oa_hi[:, :, ts].bitcast(F32), ALU.subtract).then_inc(oa_lo_done, 1)

            split_lo(U_BRANCH + 1)
            for j in range(4):
                for r in range(4):
                    h = r % 2
                    dve.wait_ge(mg_ps, 4 * j + r + 1)
                    dve.wait_ge(sg_done, j + 1)
                    if r < 2:
                        dve.tensor_tensor(prod[:, h, :], gt[j][:, r, :], branch_bank(j, r)[:, :], ALU.mult).then_inc(mul_done, 1)
                    else:
                        if j:
                            dve.wait_ge(mg_lo, 2 * j)
                        link(dve.tensor_tensor(mrg[:, h, :], gt[j][:, r, :], branch_bank(j, r)[:, :], ALU.mult))
                        dve.wait_ge(mul_done, 4 * j + h + 1)
                        dve.tensor_tensor(mrg[:, h, :], mrg[:, h, :], prod[:, h, :], ALU.add).then_inc(mul_done, 1)
                for r in range(2):
                    dve.wait_ge(mg_hi, 2 * j + r + 1)
                    dve.tensor_tensor(m_lo[:, 2 * j + r, :], mrg[:, r, :], m_hi[:, 2 * j + r, :].bitcast(F32),
                                      ALU.subtract).then_inc(mg_lo, 1)
                split_lo(U_BRANCH + 2 + j)
            for u in range(UNITS_PRE - 2, UNITS_PRE):
                split_lo(u)
            dve.wait_ge(x2_in, 32)
            for n_ in range(2):
                for t in range(TT):
                    dve.wait_ge(out_used, out_count(n_, 1, t))
                    o = y[:, t, 512 * n_:512 * (n_ + 1)]
                    dve.tensor_tensor(o, o, ps[4 * (1 - n_) + t][:, :], ALU.add).then_inc(y_done, 1)

            def token_rms(count):
                dve.wait_ge(ssq2, count)
                link(dve.tensor_scalar(ssq[:, :], ssq[:, :], 1.0 / D, EPS, ALU.mult, ALU.add))
                rsqrt(ssq[:, :], rst[:, :])

            token_rms(TT)
            for t in range(TT):
                dve.tensor_scalar(tx[:, t, :, :], y[:, t, :].rearrange("p (c k) -> p k c", k=KT), rst[:, t:t + 1], None,
                                  ALU.mult).then_inc(t_scaled, 1)
            for k in range(1, KT, 2):
                dve.wait_ge(tt_ps, k + 1)
                dve.tensor_scalar(hf[:, k, :], ps[1][:, :], nffn[:, k:k + 1], None, ALU.mult).then_inc(hf_dve, 1)
            for t in range(TT):
                dve.wait_ge(th_done, t + 1)
                dve.tensor_tensor(tl[:, t, :, :], tx[:, t, :, :], th[:, t, :, :].bitcast(F32), ALU.subtract).then_inc(tl_done, 1)

            def one_hot(oh, v, vmax, key, done=None):
                link(dve.tensor_tensor(key, v, bc_last(vmax, EG), ALU.is_equal))
                link(dve.tensor_tensor(key, key, bc_mid(prio[:, :], TT), ALU.mult))
                link(dve.tensor_reduce(kmx[:, :], key, AX.X, ALU.max))
                ins = dve.tensor_tensor(oh, key, bc_last(kmx[:, :], EG), ALU.is_equal)
                if done is None:
                    link(ins)
                else:
                    ins.then_inc(done, 1)
                    dve.wait_ge(done, 1)

            dve.wait_ge(idx_rows, 1)
            dve.tensor_copy(slot_q[:, :], slot_qi[:, :])
            dve.tensor_copy(row[:, :], row_i[:, :]).then_inc(tok_added, 2)
            dve.wait_ge(lgf_ps, 1)
            dve.tensor_copy(lgf[:, :], ps[2][0:NG + NE, :]).then_inc(lgf_done, 1)
            dve.wait_ge(lg_ps, 1)
            link(dve.tensor_tensor(lg[:, :, :], ps[3][:, 0:TT * (NG + NE)].rearrange("p (t c) -> p t c", t=TT),
                                   bc_mid(brg[:, :], TT), ALU.add))
            gl = lg[:, :, 0:NG]
            link(dve.tensor_reduce(gmx[:, :], gl, AX.X, ALU.max))
            dve.tensor_tensor(gex[:, :, :], gl, bc_last(gmx[:, :], NG), ALU.subtract).then_inc(gd_in, 1)
            one_hot(goh[:, :, :], gl, gmx[:, :], gkey[:, :, :], goh_done)
            dve.wait_ge(rank_ps, 1)
            dve.tensor_copy(rank[:, :, :], ps[5][:, 0:16].rearrange("p (t g) -> p t g", t=TT))
            link(dve.tensor_copy(tot[:, :, :], ps[5][:, 16:32].rearrange("p (t g) -> p t g", t=TT)))
            for t in range(1, TT):
                link(dve.tensor_tensor(tot[:, t, :], tot[:, t, :], tot[:, t - 1, :], ALU.add))
            dve.tensor_tensor(rank[:, 1:, :], rank[:, 1:, :], tot[:, 0:TT - 1, :], ALU.add)
            link(dve.tensor_tensor(over[:, :, :], bc_last(tot[:, TT - 1, :], NG), bc_mid(tile_n[:, :], NG), ALU.is_gt))
            link(dve.tensor_reduce(need[:, :], over[:, :, :], AX.X, ALU.add))
            link(dve.tensor_copy(ends[:, :], need[:, :]))
            for g in range(1, NG):
                link(dve.tensor_tensor(ends[:, g:g + 1], ends[:, g:g + 1], ends[:, g - 1:g], ALU.add))
            link(dve.tensor_tensor(past[:, :, :], bc_last(slot_n[:, :], NG), bc_mid(ends[:, :], SLOTS + 1), ALU.is_ge))
            link(dve.tensor_reduce(gsl[:, :], past[:, :, :], AX.X, ALU.add))
            dve.tensor_scalar(first_e[:, :], gsl[:, :], float(NG - 1), float(EG), ALU.min, ALU.mult).then_inc(slots_done, 1)
            link(dve.tensor_tensor(base[:, :], ends[:, :], need[:, :], ALU.subtract))
            link(dve.scalar_tensor_tensor(ppos[:, :, :], bc_mid(base[:, :], TT), float(P), rank[:, :, :], ALU.mult, ALU.add))
            link(dve.tensor_tensor(ppos[:, :, :], ppos[:, :, :], goh[:, :, :], ALU.mult))
            link(dve.tensor_reduce(pos[:, :], ppos[:, :, :], AX.X, ALU.add))
            link(dve.scalar_tensor_tensor(pos_s[:, :, :], bc_mid(slot_n[:, 0:SLOTS], TT), -float(P), bc_last(pos[:, :], SLOTS),
                                          ALU.mult, ALU.add))
            for t in range(TT):
                dve.tensor_tensor(perm[:, t, :, :], bc_mid(row[:, :], SLOTS), bc_last(pos_s[:, t, :], P),
                                  ALU.is_equal).then_inc(perm_done, 1)
            dve.tensor_tensor(dpos[:, :, :], bc_mid(ident[:, :], TT), bc_last(pos[:, :], P), ALU.mult).then_inc(dpos_done, 1)
            for t in range(TT):
                ins = dve.tensor_tensor(eprod[:, NG * t:NG * (t + 1), :], lg[:, t, NG:].rearrange("p (g e) -> p g e", g=NG),
                                        bc_last(goh[:, t, :], EG), ALU.mult)
            link(ins)
            link(dve.tensor_reduce(ig[:, :, :], eprod[:, :, :].rearrange("p (t g) e -> p t e g", t=TT), AX.X, ALU.add))
            link(dve.tensor_reduce(m1[:, :], ig[:, :, :], AX.X, ALU.max))
            one_hot(e1[:, :, :], ig[:, :, :], m1[:, :], ekey[:, :, :])
            link(dve.scalar_tensor_tensor(ig[:, :, :], e1[:, :, :], NEG, ig[:, :, :], ALU.mult, ALU.add))
            link(dve.tensor_reduce(m2[:, :], ig[:, :, :], AX.X, ALU.max))
            dve.tensor_tensor(dif[:, :], m2[:, :], m1[:, :], ALU.subtract).then_inc(ed_in, 1)
            one_hot(e2[:, :, :], ig[:, :, :], m2[:, :], ekey[:, :, :])
            dve.wait_ge(gd_out, 1)
            link(dve.tensor_reduce(gsm[:, :], gex[:, :, :], AX.X, ALU.add))
            link(dve.reciprocal(gp[:, :], gsm[:, :]))
            dve.wait_ge(ed_out, 1)
            link(dve.tensor_scalar(w1[:, :], dif[:, :], 1.0, None, ALU.add))
            link(dve.reciprocal(w1[:, :], w1[:, :]))
            link(dve.tensor_tensor(w1[:, :], w1[:, :], gp[:, :], ALU.mult))
            link(dve.tensor_tensor(w2[:, :], w1[:, :], dif[:, :], ALU.mult))
            link(dve.tensor_tensor(ce[:, :, :], e1[:, :, :], bc_last(w1[:, :], EG), ALU.mult))
            link(dve.tensor_tensor(ce2[:, :, :], e2[:, :, :], bc_last(w2[:, :], EG), ALU.mult))
            dve.tensor_tensor(ce[:, :, :], ce[:, :, :], ce2[:, :, :], ALU.add).then_inc(cw_in, 1)
            def split_in_lo(s):
                dve.wait_ge(xs_hi_done, s + 1)
                dve.tensor_tensor(xs_lo[:, :, :], xs[:, :, bass.ds(P * s, P)], xs_hi[:, :, :].bitcast(F32),
                                  ALU.subtract).then_inc(xs_lo_done, 1)

            def split_expert_lo(kind, s, j):
                for half in range(2):
                    slot, _, count = place(kind, s, j, half)
                    dve.wait_ge(ehi_done, count)
                    if kind == KIND_D:
                        dst, hi = dn_lo[:, half, :], dn_hi[:, half, :]
                    else:
                        dst, hi = halves(gu_lo[j % 2], kind)[half], halves(gu_hi[j % 2], kind)[half]
                    dve.tensor_tensor(dst, eraw[slot][:, :], hi.bitcast(F32), ALU.subtract).then_inc(elo_done, 1)

            for i in range(1, 2 * KT, 2):
                dve.wait_ge(xs_ps, i + 1)
                dve.tensor_scalar(xs[:, i // 2, HALF:], ps[6][:, 0:HALF], nffn[:, i // 2:i // 2 + 1], None,
                                  ALU.mult).then_inc(xs_dve, 1)
                if i == 5:
                    split_expert_lo(KIND_G, 0, 0)
                if i == 9:
                    split_expert_lo(KIND_U, 0, 0)

            split_in_lo(0)
            split_expert_lo(KIND_G, 0, 1)
            split_expert_lo(KIND_U, 0, 1)
            dve.wait_ge(cw_ps, 1)
            dve.tensor_copy(cws[:, :, :], ps[1][:, 0:SLOTS * EG].rearrange("p (s e) -> p s e", e=EG)).then_inc(cw_done, 1)

            def slot_out_lo(s):
                for n_ in range(2):
                    dve.wait_ge(os_hi_done, 2 * s + n_ + 1)
                    dve.tensor_tensor(os_lo[:, n_, :], ps[3 + n_][:, :], os_hi[:, n_, :].bitcast(F32),
                                      ALU.subtract).then_inc(os_lo_done, 1)

            def from_slot(s):
                dve.wait_ge(posb_done, 1)
                dve.tensor_scalar(slot_q[:, :], slot_q[:, :], float(P), None, ALU.add).then_inc(slot_q_done, 1)
                dve.wait_ge(slot_q_done, s + 1)
                dve.tensor_scalar(back[:, :], posb[:, :], slot_q[:, 0:1], None, ALU.is_equal).then_inc(back_done, 1)

            def add_tokens(s, t):
                for n_ in range(2):
                    dve.wait_ge(un_ps, 8 * s + 2 * t + n_ + 1)
                    o = y[:, t, S * n_:S * (n_ + 1)]
                    dve.tensor_tensor(o, o, ps[5 + n_][:, :], ALU.add).then_inc(tok_added, 1)

            def slot_dve(s):
                dve.wait_ge(cw_done, 1)
                if not is_first(s):
                    dve.wait_ge(hid_done, EG * s)
                dve.tensor_copy(cwe[:, :], cws[:, bass.ds(s, 1), :].rearrange("p s e -> p (s e)")).then_inc(cwe_done, 1)
                dve.wait_ge(cwe_done, s + 1)
                for j in range(EG):
                    i = EG * s + j
                    dve.wait_ge(gsilu, i + 1)
                    if not (is_first(s) and j < 2):
                        dve.wait_ge(hidt_ps, i - 1)
                    dve.scalar_tensor_tensor(ea[j % 2][:, :], eg[:, :], cwe[:, j:j + 1], ps[j % 2][:, FF:],
                                             ALU.mult, ALU.mult).then_inc(hid_done, 1)
                    if j == 0 and not is_first(s):
                        slot_out_lo(s - 1)
                        from_slot(s - 1)
                    split_expert_lo(KIND_D, s, j)
                    dve.wait_ge(hid_hi, i + 1)
                    dve.tensor_tensor(ea_lo[:, :, :], tbank(j)[:, 0:FF].rearrange("p (f c) -> p f c", f=2),
                                      ea_hi[:, :, :].bitcast(F32), ALU.subtract).then_inc(hid_lo, 1)
                    if j < 2 or not is_last(s):
                        split_expert_lo(KIND_G, s, j + 2)
                        if j == 2:
                            split_in_lo(s + 1)
                        split_expert_lo(KIND_U, s, j + 2)
                    if not is_first(s):
                        add_tokens(s - 1, j)

            slot_dve(0)
            with dve.Fori(1, SLOTS - 1) as s:
                slot_dve(s)
            slot_dve(SLOTS - 1)
            slot_out_lo(SLOTS - 1)
            from_slot(SLOTS - 1)
            for t in range(TT):
                add_tokens(SLOTS - 1, t)
            token_rms(2 * TT)
            for t in range(TT):
                dve.scalar_tensor_tensor(out_t[:, t, :], y[:, t, :], rst[:, t:t + 1], nfin[:, :],
                                         ALU.mult, ALU.mult).then_inc(fin_done, 1)

        @block.tensor
        def _(pe):
            def three(out_ap, lhs_hi, lhs_lo, rhs_hi, rhs_lo, first, last):
                pe.matmul(out_ap, lhs_hi, rhs_hi, start=first, stop=False)
                pe.matmul(out_ap, lhs_hi, rhs_lo, start=False, stop=False)
                return pe.matmul(out_ap, lhs_lo, rhs_hi, start=False, stop=last)

            pe.wait_ge(consts, 1)
            pe.wait_ge(small_in, 192)
            pe.transpose(ps[7][:, 0:57], rows[:, :], ident[0:57, 0:57]).then_inc(rows_ps, 1)
            for k in range(KT):
                if k >= 2:
                    pe.wait_ge(ht_lo, k - 1)
                for t in range(TT):
                    pe.wait_ge(x_scaled, t + 1)
                    ins = pe.transpose(ps[k % 2][:, t * P:(t + 1) * P], x[:, t, k * P:(k + 1) * P], ident[:, :])
                ins.then_inc(ht_ps, 1)
            pe.wait_ge(ht_lo, KT)
            pe.wait_ge(ba_lo_done, 1)
            for k in range(KT):
                ins = three(ps[4][0:8, :], ba_hi[:, k, :], ba_lo[:, k, :], h_hi[:, k, :], h_lo[:, k, :],
                            k == 0, k == KT - 1)
            ins.then_inc(ba_ps, 1)
            pe.wait_ge(ba_f_done, 1)
            for t in range(TT):
                ins = pe.transpose(ps[5][:, 8 * t:8 * t + 8], ba_f[:, t * P:(t + 1) * P], ident[0:8, 0:8])
            ins.then_inc(ba_ps, 1)

            def sum_squares(i):
                pe.wait_ge(sq_done, i + 1)
                if i >= 2:
                    pe.wait_ge(root_done, i - 1)
                pe.matmul(ps[2 + i % 2][:, :], ones[:, :], sqb[i % 2][:, :], start=True, stop=True).then_inc(norm_ps, 1)

            for i in range(ITEMS):
                u, half = i // 2, i % 2
                hi = whi[u % RING][:, :].rearrange("p (k n) -> p k n", k=KT)
                lo = wlo[u % RING][:, :].rearrange("p (k n) -> p k n", k=KT)
                pe.wait_ge(lo_done, u + 1)
                if i >= 2:
                    pe.wait_ge(proj_evac, i - 1)
                bank = ps[i % 2]
                for k in range(KT):
                    wh, wl = (w[:, k, 128 * half:128 * half + 128] for w in (hi, lo))
                    ins = three(bank[:, :], wh, wl, h_hi[:, k, :], h_lo[:, k, :], k == 0, k == KT - 1)
                ins.then_inc(proj_ps, 1)
                for j in norms_at(i):
                    sum_squares(j)

            at_step = [0]

            def side(steps):
                for _ in range(steps):
                    f, k = divmod(at_step[0], KT)
                    at_step[0] += 1
                    u = U_SIDE + f // 2
                    hi, lo = kv_(whi[u % RING]), kv_(wlo[u % RING])
                    cs = slice(P * (f % 2), P * (f % 2 + 1))
                    if k == 0:
                        pe.wait_ge(lo_done, u + 1)
                        if f >= 2:
                            pe.wait_ge(side_evac, f - 1)
                    ins = three(side_bank(f)[:, :], hi[:, k, cs], lo[:, k, cs], h_hi[:, k, :], h_lo[:, k, :],
                                k == 0, k == KT - 1)
                    if k == KT - 1:
                        ins.then_inc(side_ps, 1)

            pe.wait_ge(proj_evac, ITEMS)
            for t in range(TT):
                ins = pe.transpose(bank4(4)[:, t, :], v_f[:, t * P:(t + 1) * P], ident[:, :])
            ins.then_inc(vt_ps, 1)
            def scores(a_):
                m, g = a_ // 2, a_ % 2
                d = slice(DB * g, DB * (g + 1))
                c0 = CHUNK if m else P
                if a_:
                    pe.wait_ge(max_done, a_)
                for h in range(GRP):
                    o = ps[h // 2][:, 256 * (h % 2) + c0:256 * (h % 2) + 256]
                    ins = pe.matmul(o, qb[d, h, m * P:(m + 1) * P], kb[d, m * P - P + c0:(m + 1) * P],
                                    start=True, stop=True)
                ins.then_inc(sc_ps, 1)

            scores(0)
            for a_ in range(2 * TT):
                m, g = a_ // 2, a_ % 2
                d = slice(DB * g, DB * (g + 1))
                if a_ + 1 < 2 * TT:
                    scores(a_ + 1)
                pe.wait_ge(exp_done, a_ + 1)
                for half in range(2):
                    if half == 1 or m:
                        if a_ > 2 and half == 0:
                            pe.wait_ge(pt_prev, a_ - 2)
                        if a_ and half == 1:
                            pe.wait_ge(pt_cur, a_)
                        for h in range(GRP):
                            ins = pe.transpose(bank4(2 + half)[:, h, :], pb[a_ % 2][:, h, half * P:(half + 1) * P], ident[:, :])
                        ins.then_inc(pt_ps, 1 if m else 2)
                side(3)
                if m:
                    pe.wait_ge(pt_prev, a_ - 1)
                pe.wait_ge(pt_cur, a_ + 1)
                pe.wait_ge(vb_done, 1)
                if a_:
                    pe.wait_ge(ob_ready, a_)
                for h in range(GRP):
                    o = ps[4][:, DB * h:DB * (h + 1)]
                    if m:
                        pe.matmul(o, pt[:, 0, h, :], vb[:, m - 1, d], start=True, stop=False)
                    ins = pe.matmul(o, pt[:, 1, h, :], vb[:, m, d], start=not m, stop=True)
                ins.then_inc(pv_ps, 1)
                side(1)
                if g == 1:
                    pe.wait_ge(ob_ready, a_ + 1)
                    if m:
                        pe.wait_ge(ob_lo_done, m)
                    for k in range(4):
                        ins = pe.transpose(bank4(5)[:, k, :], ob_t[:, 2 * k:2 * k + 2, :], ident[:, :])
                    ins.then_inc(obt_ps, 1)

            pe.wait_ge(gates_done, 2)
            pe.wait_ge(norm_done, NORM_ITEMS)
            pe.wait_ge(ob_lo_done, TT)
            pe.wait_ge(side_evac, Z_ITEMS)
            g_all = gdt[:, :, :].rearrange("p t h -> p (t h)")
            pe.matmul(ps[5][:, 0:16], tri[:, :], g_all, start=True, stop=True)
            pe.matmul(ps[5][:, 16:32], blk[:, :], g_all, start=True, stop=True)
            for c in range(2):
                r = slice(CHUNK * c, CHUNK * (c + 1))
                o = ps[5 + c][:, 32 + 16 * c:48 + 16 * c]
                ins = pe.matmul(o, ones[r, :],
                                gdt[r, :, :].rearrange("p t h -> p (t h)"), start=True, stop=True)
            ins.then_inc(gsum_ps, 1)
            pe.wait_ge(gsum_sub, 1)

            def tile_front(m):
                ts = slice(m * P, (m + 1) * P)
                pe.wait_ge(rb_ready, 2 * m + 1)
                pe.matmul(ps[2][:, :], ones[:, :], d_x[:, :, :], start=True, stop=True).then_inc(rb_ps, 1)
                for h in range(HA):
                    ins = pe.matmul(bank4(4)[:, h, :], fm[:, HA + h, ts], fm[:, HA + h, ts], start=True, stop=True)
                ins.then_inc(kk_ps, 1)
                for h in range(HA):
                    ins = pe.matmul(bank4(5)[:, h, :], fm[:, HA + h, ts], fm[:, h, ts], start=True, stop=True)
                ins.then_inc(kk_ps, 1)

            tile_front(0)
            for m in range(TT):
                ts = slice(m * P, (m + 1) * P)
                side(2)
                pe.wait_ge(rb_ready, 2 * m + 2)
                if m:
                    pe.wait_ge(s_done, 2 * m)
                pe.matmul(ps[3][:, :], ones[:, :], d_c[:, :, :], start=True, stop=True).then_inc(rb_ps, 1)
                if m:
                    pe.wait_ge(oaf_done, m)
                for w in range(2):
                    if w and m:
                        pe.wait_ge(on_done, m)
                    for h in range(HA):
                        ins = pe.transpose(bank4(6 + w)[:, h, :], fm[:, HA * (w + 1) + h, ts], ident[:, :])
                    ins.then_inc(kv_ps, 1)
                side(4)
                pe.wait_ge(inv0, m + 1)
                for h in range(HA):
                    ins = pe.transpose(bank4(2)[:, h, :], d_invT[:, h, :], ident[:, :])
                ins.then_inc(inv0_ps, 1)
                pe.wait_ge(inv0_copied, m + 1)
                for l in range(1, 6):
                    if l > 1:
                        pe.wait_ge(de_done, 5 * m + l - 1)
                    pe.wait_ge(ct_done, 5 * m + l)
                    for h in range(HA):
                        ins = pe.matmul(bank4(2)[:, h, :], d_c[:, h, :], d_inv[:, h, :], start=True, stop=True)
                    ins.then_inc(x_ps, 1)
                    side(1)
                    pe.wait_ge(xs_done, 5 * m + l)
                    if l < 5:
                        for h in range(HA):
                            pe.matmul(bank4(3)[:, h, :], d_invT[:, h, :], d_x[:, h, :], start=True, stop=True)
                    for h in range(HA):
                        ins = pe.matmul(bank4(4)[:, h, :], d_x[:, h, :], d_invT[:, h, :], start=True, stop=True)
                    ins.then_inc(de_ps, 1)
                    side(3)
                pe.wait_ge(de_done, 5 * m + 5)
                pe.wait_ge(kbv_done, m + 1)
                pe.wait_ge(qd_done, m + 1)
                for h in range(HA):
                    ins = pe.matmul(bank4(5)[:, h, :], d_k[:, h, :], d_invT[:, h, :], start=True, stop=True)
                ins.then_inc(wu_ps, 1)
                for h in range(HA):
                    ins = pe.matmul(bank4(6)[:, h, :], d_invT[:, h, :], d_v[:, h, :], start=True, stop=True)
                ins.then_inc(wu_ps, 1)
                pe.wait_ge(wu_done, m + 1)
                for c in range(2):
                    r = slice(CHUNK * c, CHUNK * (c + 1))
                    j = 2 * m + c
                    pe.wait_ge(s_zero, 1)
                    if j:
                        pe.wait_ge(s_done, j)
                    for h in range(HA):
                        ins = pe.matmul(bank4(2)[r, h, :], d_k[:, h, r], d_s[:, h, :], start=True, stop=True)
                    ins.then_inc(ws_ps, 1)
                    side(1)
                    pe.wait_ge(vn_done, j + 1)
                    for h in range(HA):
                        pe.matmul(bank4(7)[r, h, :], d_qd[:, h, r], d_s[:, h, :], start=True, stop=False)
                        ins = pe.matmul(bank4(7)[r, h, :], d_kq[r, h, r], d_x[r, h, :], start=False, stop=True)
                    if c == 1:
                        ins.then_inc(o_ps, 1)
                    for h in range(HA):
                        ins = pe.matmul(bank4(3)[:, h, :], d_kd[r, h, :], d_x[r, h, :], start=True, stop=True)
                    ins.then_inc(ds_ps, 1)
                if m + 1 < TT:
                    tile_front(m + 1)
                side(4)
                pe.wait_ge(on_done, m + 1)
                for h in range(HA):
                    ins = pe.transpose(bank4(6)[:, h, :], d_c[:, h, :], ident[:, :])
                ins.then_inc(oat_ps, 1)


            assert at_step[0] == SIDE_ITEMS * KT
            pe.wait_ge(side_evac, SIDE_ITEMS)
            pe.wait_ge(oa_lo_done, TT)
            for j in range(4):
                u = U_BRANCH + j
                hi, lo = kv_(whi[u % RING]), kv_(wlo[u % RING])
                pe.wait_ge(lo_done, u + 1)
                for r in range(4):
                    cs = slice(P * (r % 2), P * (r % 2 + 1))
                    xh, xl = (oa_hi, oa_lo) if r < 2 else (ob_hi, ob_lo)
                    if j >= 2:
                        pe.wait_ge(mul_done, 4 * (j - 2) + r + 1)
                    for k in range(4):
                        kk = k + (0 if r < 2 else 4)
                        ins = three(branch_bank(j, r)[:, :], hi[:, kk, cs], lo[:, kk, cs], xh[:, k, :], xl[:, k, :],
                                    k == 0, k == 3)
                    ins.then_inc(mg_ps, 1)
            pe.wait_ge(mg_lo, KT)
            for n_ in range(2):
                for kh in range(2):
                    u = U_OUT + 2 * n_ + kh
                    hi, lo = (w[u % RING][:, :].rearrange("p (k n) -> p k n", k=4) for w in (whi, wlo))
                    pe.wait_ge(lo_done, u + 1)
                    if kh == 0:
                        pe.wait_ge(mul_done, 12 + 4 * n_)
                    for t in range(TT):
                        ts = slice(t * P, (t + 1) * P)
                        for k in range(4):
                            kk = 4 * kh + k
                            ins = three(ps[4 * (1 - n_) + t][:, :], m_hi[:, kk, ts], m_lo[:, kk, ts], hi[:, k, :], lo[:, k, :],
                                        kk == 0, kk == KT - 1)
                        if kh or t == TT - 1:
                            ins.then_inc(out_used, 1)
            pe.wait_ge(y_done, 8)
            for k in range(KT):
                if k >= 2:
                    pe.wait_ge((hf_act, hf_dve)[k % 2], k // 2)
                for t in range(TT):
                    pe.wait_ge(t_scaled, t + 1)
                    ins = pe.transpose(ps[k % 2][:, t * P:(t + 1) * P], tx[:, t, k, :], ident[:, :])
                ins.then_inc(tt_ps, 1)
            for k in range(KT):
                pe.wait_ge((hf_act, hf_dve)[k % 2], k // 2 + 1)
                ins = pe.matmul(ps[2][0:NG + NE, :], rw_raw[:, k, :], hf[:, k, :], start=k == 0, stop=k == KT - 1)
            ins.then_inc(lgf_ps, 1)
            pe.wait_ge(lgf_done, 1)
            for t in range(TT):
                ins = pe.transpose(ps[3][:, (NG + NE) * t:(NG + NE) * (t + 1)], lgf[:, t * P:(t + 1) * P],
                                   ident[0:NG + NE, 0:NG + NE])
            ins.then_inc(lg_ps, 1)
            pe.wait_ge(goh_done, 1)
            g_all = goh[:, :, :].rearrange("p t g -> p (t g)")
            pe.matmul(ps[5][:, 0:16], before[:, :], g_all, start=True, stop=True)
            pe.matmul(ps[5][:, 16:32], ones[:, :], g_all, start=True, stop=True).then_inc(rank_ps, 1)
            pe.wait_ge(tl_done, TT)
            for i in range(2 * KT):
                k, half = divmod(i, 2)
                if i >= 2:
                    pe.wait_ge((xs_act, xs_dve)[half], k)
                for t in range(TT):
                    pe.wait_ge(perm_done, t + 1)
                    to = perm[:, t, :, :].rearrange("p s q -> p (s q)")[:, HALF * half:HALF * (half + 1)]
                    o = ps[(4, 6)[half]][:, 0:HALF]
                    pe.matmul(o, th[:, t, k, :], to, start=t == 0, stop=False)
                    ins = pe.matmul(o, tl[:, t, k, :], to, start=False, stop=t == TT - 1)
                ins.then_inc(xs_ps, 1)
                if i == 1:
                    pe.wait_ge(dpos_done, 1)
                    pe.matmul(ps[3][:, :], ones[:, :], dpos[:, :, :].rearrange("p t c -> p (t c)"),
                              start=True, stop=True).then_inc(posb_ps, 1)
            pe.wait_ge(cw_in, 1)
            for s in range(SLOTS):
                for t in range(TT):
                    ins = pe.matmul(ps[1][:, EG * s:EG * (s + 1)], perm[:, t, s, :].bitcast(F32), ce[:, t, :],
                                    start=t == 0, stop=t == TT - 1)
            ins.then_inc(cw_ps, 1)

            def gate_up(s, j, ks):
                b = j % 2
                for k in ks:
                    ins = three(ps[b][:, :], xs_hi[:, k, :], xs_lo[:, k, :], gu_hi[b][:, :, k, :], gu_lo[b][:, :, k, :],
                                k == 0, k == KT - 1)
                if ks[-1] == KT - 1:
                    ins.then_inc(gu_ps, 1)

            def hidden_f(s, j):
                pe.wait_ge(hid_done, EG * s + j + 1)
                for f in range(2):
                    ins = pe.transpose(tbank(j)[:, P * f:P * (f + 1)], ea[j % 2][:, P * f:P * (f + 1)], ident[:, :])
                ins.then_inc(hidt_ps, 1)

            def to_tokens(s, t):
                pe.wait_ge(back_done, s + 1)
                pe.wait_ge(os_lo_done, 2 * s + 2)
                for n_ in range(2):
                    pe.wait_ge(tok_added, 8 * s + 2 * t + n_ + 1)
                    pe.matmul(ps[5 + n_][:, :], back[:, P * t:P * (t + 1)], os_hi[:, n_, :], start=True, stop=False)
                    pe.matmul(ps[5 + n_][:, :], back[:, P * t:P * (t + 1)], os_lo[:, n_, :],
                              start=False, stop=True).then_inc(un_ps, 1)

            def slot_pe(s):
                for j in range(EG):
                    i = EG * s + j
                    if j == EG - 1 and is_last(s):
                        hidden_f(s, j)
                    else:
                        pe.wait_ge(elo_done, place(KIND_U, s, j + 1)[2])
                        if not (is_first(s) and j == 0):
                            pe.wait_ge(hid_done, i)
                        if j == EG - 1:
                            pe.wait_ge(xs_lo_done, s + 2)
                        gate_up(s, j + 1, range(0, KT // 2))
                        hidden_f(s, j)
                        gate_up(s, j + 1, range(KT // 2, KT))
                    pe.wait_ge(elo_done, place(KIND_D, s, j)[2])
                    pe.wait_ge(hid_lo, i + 1)
                    if j == 0 and not is_first(s):
                        pe.wait_ge(os_lo_done, 2 * s)
                    for n_ in range(2):
                        ns = slice(S * n_, S * (n_ + 1))
                        for f in range(2):
                            ins = three(ps[3 + n_][:, :], ea_hi[:, f, :], ea_lo[:, f, :], dn_hi[:, f, ns], dn_lo[:, f, ns],
                                        j == 0 and f == 0, j == EG - 1 and f == 1)
                    ins.then_inc(dn_ps, 1)
                    if not is_first(s):
                        to_tokens(s - 1, j)

            pe.wait_ge(elo_done, place(KIND_U, 0, 0)[2])
            pe.wait_ge(xs_lo_done, 1)
            gate_up(0, 0, range(KT))
            pe.wait_ge(cw_done, 1)
            slot_pe(0)
            with pe.Fori(1, SLOTS - 1) as s:
                slot_pe(s)
            slot_pe(SLOTS - 1)
            for t in range(TT):
                to_tokens(SLOTS - 1, t)


_INS = ["x", "norm_mix_w", "w_in", "conv_w", "a_log", "dt_bias", "delta_norm_w", "sinks", "w_out_a", "w_out_b",
        "w_out", "norm_ffn_w", "w_router_group", "b_router_group", "w_router_expert", "b_router_expert",
        "w_gate", "w_up", "w_down", "norm_final_w"]


def kernel(**inputs):
    import concourse.bacc as bacc
    from concourse.bass_utils import run_bass_kernel_spmd

    nc = bacc.Bacc("TRN2", target_bir_lowering=False, num_devices=1)
    arrays, args = {}, {}
    for name in _INS:
        arr = np.ascontiguousarray(inputs[name])
        arrays[f"in_{name}"] = arr
        args[name] = nc.dram_tensor(f"in_{name}", arr.shape, mybir.dt.from_np(arr.dtype), kind="ExternalInput").ap()
    out = nc.dram_tensor("out_y", (1, S, D), F32, kind="ExternalOutput").ap()
    build(nc, args, out)
    r = run_bass_kernel_spmd(nc, [arrays], core_ids=[0])
    return r.results[0]["out_y"]
```
